# Optimizing a Trainium2 kernel written in Bass

```python
import math
import jax
import jax.numpy as jnp
from jax import lax
import numpy as np

D_MODEL = 1024
BATCH = 1
SEQ = 256
DEPTH = 2
DEC_BATCH = 8
DEC_SEQ = 8
PAST_LEN = 256
PAGE_SIZE = 128

H_A = 4
D_QK = 64
D_VA = 2 * D_QK
QK_W = H_A * 2 * D_QK
ATT_W = H_A * D_VA
ROT_DIM = D_QK // 4
ROPE_THETA = 500000.0
Q_BLOCK = 128
CONV_CH = D_MODEL // 2
CONV_W = 31
H_C = 4
DK_C = D_MODEL // H_C
DV_C = 2 * DK_C
RET_THETA = 10000.0
RET_CHUNK = 128
N_EXPERTS = 16
N_GROUPS = 4
EXPERTS_PER_GROUP = N_EXPERTS // N_GROUPS
TOP_K = 2
D_FF = D_MODEL // 2
DN_ALPHA = (2 * DEPTH) ** 0.25
DN_BETA = (8 * DEPTH) ** -0.25
LN_EPS = 1e-5

N_A_LAYERS = (DEPTH + 1) // 2
N_C_LAYERS = DEPTH // 2
IN_A = 2 * QK_W + ATT_W + 2 * CONV_CH
IN_C = 2 * H_C * DK_C + 2 * H_C * DV_C

kernel_name = 'diffattn_conformer_retention_sharedrouter_moe_step'

F32 = jnp.float32

def _layer_norm(x, g, b):
    xf = x.astype(F32)
    mu = jnp.mean(xf, -1, keepdims=True)
    var = jnp.mean(jnp.square(xf - mu), -1, keepdims=True)
    return ((xf - mu) * lax.rsqrt(var + LN_EPS) * g.astype(F32) + b.astype(F32)).astype(x.dtype)

def _rms_norm(x, g):
    xf = x.astype(F32)
    return (xf * lax.rsqrt(jnp.mean(jnp.square(xf), -1, keepdims=True) + LN_EPS) * g.astype(F32)).astype(x.dtype)

def _head_norm(x):
    mu = jnp.mean(x, -1, keepdims=True)
    var = jnp.mean(jnp.square(x - mu), -1, keepdims=True)
    return (x - mu) * lax.rsqrt(var + LN_EPS)

def _rotate(t, pos, inv_freq):
    half = inv_freq.shape[0]
    ang = pos.astype(F32)[:, None] * inv_freq[None, :]
    shape = (1, ang.shape[0]) + (1,) * (t.ndim - 3) + (half,)
    cos = jnp.cos(ang).reshape(shape)
    sin = jnp.sin(ang).reshape(shape)
    t1 = t[..., :half].astype(F32)
    t2 = t[..., half:2 * half].astype(F32)
    rot = jnp.concatenate([t1 * cos - t2 * sin, t2 * cos + t1 * sin], -1).astype(t.dtype)
    return jnp.concatenate([rot, t[..., 2 * half:]], -1)

def _diff_attention(q, k, v, q_pos, k_pos, lam):
    scale = D_QK ** -0.5

    def block(args):
        qb, pb = args
        s = jnp.einsum('bqhmd,bkhmd->bhmqk', qb, k).astype(F32) * scale
        mask = k_pos[None, :] <= pb[:, None]
        p = jax.nn.softmax(jnp.where(mask, s, -jnp.inf), axis=-1)
        w = p[:, :, 0] - lam * p[:, :, 1]
        return jnp.einsum('bhqk,bkhe->bqhe', w.astype(v.dtype), v)

    b, lq = q.shape[0], q.shape[1]
    if lq > Q_BLOCK and lq % Q_BLOCK == 0:
        nb = lq // Q_BLOCK
        qb = jnp.moveaxis(q.reshape(b, nb, Q_BLOCK, H_A, 2, D_QK), 1, 0)
        pb = q_pos.reshape(nb, Q_BLOCK)
        out = lax.map(block, (qb, pb))
        return jnp.moveaxis(out, 0, 1).reshape(b, lq, H_A, D_VA)
    return block((q, q_pos))

def _diff_conv_mixer(x, pos, past, conv_buf, layer_idx, w_in, lam_p, subln_g, cw, cb, cg, cbeta, w_out):
    b, L, _ = x.shape
    q, k, v, a, g = jnp.split(x @ w_in, [QK_W, 2 * QK_W, 2 * QK_W + ATT_W, 2 * QK_W + ATT_W + CONV_CH], axis=-1)
    inv = ROPE_THETA ** (-jnp.arange(0, ROT_DIM, 2, dtype=F32) / ROT_DIM)
    q = _rotate(q.reshape(b, L, H_A, 2, D_QK), pos, inv)
    k = _rotate(k.reshape(b, L, H_A, 2, D_QK), pos, inv)
    v = v.reshape(b, L, H_A, D_VA)
    if past is None:
        k_all, v_all, k_pos = k, v, pos
    else:
        k_past, v_past = past
        k_all = jnp.concatenate([k_past.astype(k.dtype), k], 1)
        v_all = jnp.concatenate([v_past.astype(v.dtype), v], 1)
        k_pos = jnp.concatenate([jnp.arange(k_past.shape[1], dtype=pos.dtype), pos])
    lam_init = 0.8 - 0.6 * math.exp(-0.3 * layer_idx)
    lf = lam_p.astype(F32)
    lam = jnp.exp(jnp.sum(lf[0] * lf[1])) - jnp.exp(jnp.sum(lf[2] * lf[3])) + lam_init
    att = _rms_norm(_diff_attention(q, k_all, v_all, pos, k_pos, lam), subln_g) * (1.0 - lam_init)
    u = a * jax.nn.sigmoid(g)
    u_ext = jnp.concatenate([conv_buf.astype(u.dtype), u], 1)
    c = lax.conv_general_dilated(u_ext, cw[:, None, :].astype(u.dtype), window_strides=(1,), padding='VALID',
                                 dimension_numbers=('NWC', 'WIO', 'NWC'), feature_group_count=CONV_CH) + cb
    c = jax.nn.silu(_layer_norm(c, cg, cbeta))
    mix = jnp.concatenate([att.reshape(b, L, ATT_W), c], -1) @ w_out
    return mix, k.reshape(b, L, 2 * H_A, D_QK), v, u_ext[:, -(CONV_W - 1):]

def _retention(q, k, v, s0):
    b, L, h, _ = q.shape
    dv = v.shape[-1]
    c = RET_CHUNK if L % RET_CHUNK == 0 else L
    n = L // c
    log_g = jnp.log1p(-jnp.exp2(-5.0 - jnp.arange(h, dtype=F32)))
    idx = jnp.arange(c, dtype=F32)
    diff = idx[:, None] - idx[None, :]
    causal = diff >= 0
    d_intra = jnp.where(causal[None], jnp.exp(jnp.where(causal, diff, 0.0)[None] * log_g[:, None, None]), 0.0)
    q_dec = jnp.exp((idx[:, None] + 1.0) * log_g[None])
    k_dec = jnp.exp((c - 1.0 - idx[:, None]) * log_g[None])
    c_dec = jnp.exp(c * log_g)

    def to_chunks(t):
        return jnp.moveaxis(t.astype(F32).reshape(b, n, c, h, t.shape[-1]), 1, 0)

    def step(s, inp):
        qc, kc, vc = inp
        sc = jnp.einsum('bihd,bjhd->bhij', qc, kc) * d_intra
        o = jnp.einsum('bhij,bjhe->bihe', sc, vc) + jnp.einsum('bihd,bhde->bihe', qc * q_dec[:, :, None], s)
        s = s * c_dec[:, None, None] + jnp.einsum('bjhd,bjhe->bhde', kc * k_dec[:, :, None], vc)
        return s, o

    s, o = lax.scan(step, s0.astype(F32), (to_chunks(q), to_chunks(k), to_chunks(v)))
    return jnp.moveaxis(o, 0, 1).reshape(b, L, h, dv), s

def _retention_mixer(x, pos, s0, w_in, w_out):
    b, L, _ = x.shape
    q, k, v, g = jnp.split(x @ w_in, [H_C * DK_C, 2 * H_C * DK_C, 2 * H_C * DK_C + H_C * DV_C], axis=-1)
    inv = RET_THETA ** (-jnp.linspace(0.0, 1.0, DK_C // 2, dtype=F32))
    q = _rotate(q.reshape(b, L, H_C, DK_C), pos, inv)
    k = _rotate(k.reshape(b, L, H_C, DK_C), pos, inv) * (DK_C ** -0.5)
    o, s_new = _retention(q, k, v.reshape(b, L, H_C, DV_C), s0)
    o = _head_norm(o).astype(x.dtype).reshape(b, L, H_C * DV_C)
    return (jax.nn.silu(g) * o) @ w_out, s_new.astype(x.dtype)

def _moe(x, w_router, b_router, wg, wu, wd):
    xt = x.reshape(-1, D_MODEL)
    probs = jax.nn.softmax((xt @ w_router).astype(F32), axis=-1)
    sel = (probs + b_router.astype(F32)).reshape(-1, N_GROUPS, EXPERTS_PER_GROUP)
    group_score = lax.top_k(sel, TOP_K)[0].sum(-1)
    g_idx = jnp.argmax(group_score, axis=-1)
    in_group = jnp.take_along_axis(sel, g_idx[:, None, None], axis=1)[:, 0]
    _, local = lax.top_k(in_group, TOP_K)
    e_idx = g_idx[:, None] * EXPERTS_PER_GROUP + local
    w = jnp.take_along_axis(probs, e_idx, axis=-1)
    w = w / jnp.sum(w, -1, keepdims=True)
    gates = jnp.sum(jax.nn.one_hot(e_idx, N_EXPERTS, dtype=F32) * w[..., None], axis=1).astype(x.dtype)
    y = jnp.zeros_like(xt)
    for e in range(N_EXPERTS):
        hid = jax.nn.silu(xt @ wg[e]) * (xt @ wu[e])
        y = y + gates[:, e:e + 1] * (hid @ wd[e])
    return y.reshape(x.shape)

def _trunk(x, pos, paged, conv_state, ret_state, w_in_a, lambda_a, subln_a, conv_w, conv_b, conv_ln_g, conv_ln_b,
           w_out_a, w_in_c, w_out_c, ln_g, ln_b, w_router, b_router, w_e_gate, w_e_up, w_e_down):
    k_rows, v_rows, conv_rows, ret_rows = [], [], [], []
    for l in range(DEPTH):
        if l % 2 == 0:
            ia = l // 2
            past = None
            if paged is not None:
                cache_k, cache_v, page_table = paged
                nb, n_pages = page_table.shape
                past = (cache_k[ia][page_table].reshape(nb, n_pages * PAGE_SIZE, H_A, 2, D_QK),
                        cache_v[ia][page_table].reshape(nb, n_pages * PAGE_SIZE, H_A, D_VA))
            mix, k_new, v_new, buf = _diff_conv_mixer(x, pos, past, conv_state[ia], l, w_in_a[ia], lambda_a[ia],
                                                      subln_a[ia], conv_w[ia], conv_b[ia], conv_ln_g[ia],
                                                      conv_ln_b[ia], w_out_a[ia])
            k_rows.append(k_new)
            v_rows.append(v_new)
            conv_rows.append(buf)
        else:
            ic = l // 2
            mix, s_new = _retention_mixer(x, pos, ret_state[ic], w_in_c[ic], w_out_c[ic])
            ret_rows.append(s_new)
        x = _layer_norm(DN_ALPHA * x + mix, ln_g[l, 0], ln_b[l, 0])
        x = _layer_norm(DN_ALPHA * x + _moe(x, w_router, b_router, w_e_gate[l], w_e_up[l], w_e_down[l]),
                        ln_g[l, 1], ln_b[l, 1])
    return x, jnp.stack(k_rows), jnp.stack(v_rows), jnp.stack(conv_rows), jnp.stack(ret_rows)

def setup_inputs(seed: int = 0) -> dict:
    key = jax.random.key(seed)
    ks = jax.random.split(key, 24)
    n_pages = PAST_LEN // PAGE_SIZE
    n_phys = (DEC_BATCH * n_pages * 5) // 4

    def nrm(k, shape, s):
        return jax.random.normal(k, shape, F32) * s

    return {
        'x_prompt': nrm(ks[0], (BATCH, SEQ, D_MODEL), 1.0),
        'x_sample': nrm(ks[1], (DEC_BATCH, DEC_SEQ, D_MODEL), 1.0),
        'cache_k': nrm(ks[2], (N_A_LAYERS, n_phys, PAGE_SIZE, 2 * H_A, D_QK), 1.0),
        'cache_v': nrm(ks[3], (N_A_LAYERS, n_phys, PAGE_SIZE, H_A, D_VA), 1.0),
        'page_table': jax.random.permutation(ks[4], n_phys)[:DEC_BATCH * n_pages].reshape(DEC_BATCH, n_pages).astype(jnp.int32),
        'state_conv': nrm(ks[5], (N_A_LAYERS, DEC_BATCH, CONV_W - 1, CONV_CH), 0.5),
        'state_ret': nrm(ks[6], (N_C_LAYERS, DEC_BATCH, H_C, DK_C, DV_C), 0.5),
        'w_in_a': nrm(ks[7], (N_A_LAYERS, D_MODEL, IN_A), D_MODEL ** -0.5),
        'lambda_a': nrm(ks[8], (N_A_LAYERS, 4, D_QK), 0.1),
        'subln_a': 1.0 + nrm(ks[9], (N_A_LAYERS, D_VA), 0.01),
        'conv_w': nrm(ks[10], (N_A_LAYERS, CONV_W, CONV_CH), CONV_W ** -0.5),
        'conv_b': nrm(ks[11], (N_A_LAYERS, CONV_CH), 0.01),
        'conv_ln_g': 1.0 + nrm(ks[12], (N_A_LAYERS, CONV_CH), 0.01),
        'conv_ln_b': nrm(ks[13], (N_A_LAYERS, CONV_CH), 0.01),
        'w_out_a': nrm(ks[14], (N_A_LAYERS, ATT_W + CONV_CH, D_MODEL), DN_BETA * (ATT_W + CONV_CH) ** -0.5),
        'w_in_c': nrm(ks[15], (N_C_LAYERS, D_MODEL, IN_C), D_MODEL ** -0.5),
        'w_out_c': nrm(ks[16], (N_C_LAYERS, H_C * DV_C, D_MODEL), DN_BETA * (H_C * DV_C) ** -0.5),
        'ln_g': 1.0 + nrm(ks[17], (DEPTH, 2, D_MODEL), 0.01),
        'ln_b': nrm(ks[18], (DEPTH, 2, D_MODEL), 0.01),
        'w_router': nrm(ks[19], (D_MODEL, N_EXPERTS), D_MODEL ** -0.5),
        'b_router': nrm(ks[20], (N_EXPERTS,), 0.01),
        'w_e_gate': nrm(ks[21], (DEPTH, N_EXPERTS, D_MODEL, D_FF), D_MODEL ** -0.5),
        'w_e_up': nrm(ks[22], (DEPTH, N_EXPERTS, D_MODEL, D_FF), D_MODEL ** -0.5),
        'w_e_down': nrm(ks[23], (DEPTH, N_EXPERTS, D_FF, D_MODEL), DN_BETA * D_FF ** -0.5),
    }

def reference(x_prompt, x_sample, cache_k, cache_v, page_table, state_conv, state_ret,
              w_in_a, lambda_a, subln_a, conv_w, conv_b, conv_ln_g, conv_ln_b, w_out_a,
              w_in_c, w_out_c, ln_g, ln_b, w_router, b_router, w_e_gate, w_e_up, w_e_down):
    bp, seq_p = x_prompt.shape[0], x_prompt.shape[1]
    pos_p = jnp.arange(seq_p, dtype=jnp.int32)
    past_len = page_table.shape[1] * PAGE_SIZE
    pos_s = past_len + jnp.arange(x_sample.shape[1], dtype=jnp.int32)
    zeros_conv = jnp.zeros((N_A_LAYERS, bp, CONV_W - 1, CONV_CH), x_prompt.dtype)
    zeros_ret = jnp.zeros((N_C_LAYERS, bp, H_C, DK_C, DV_C), F32)
    y_prompt, k_p, v_p, conv_p, ret_p = _trunk(
        x_prompt, pos_p, None, zeros_conv, zeros_ret, w_in_a, lambda_a, subln_a, conv_w, conv_b, conv_ln_g,
        conv_ln_b, w_out_a, w_in_c, w_out_c, ln_g, ln_b, w_router, b_router, w_e_gate, w_e_up, w_e_down)
    y_sample, k_s, v_s, conv_s, ret_s = _trunk(
        x_sample, pos_s, (cache_k, cache_v, page_table), state_conv, state_ret, w_in_a, lambda_a, subln_a,
        conv_w, conv_b, conv_ln_g, conv_ln_b, w_out_a, w_in_c, w_out_c, ln_g, ln_b, w_router, b_router,
        w_e_gate, w_e_up, w_e_down)
    return (y_prompt, y_sample, k_p, v_p, conv_p, ret_p, k_s, v_s, conv_s, ret_s)


_drawn_inputs = setup_inputs


def setup_inputs(seed=0):
    import zlib

    import numpy as np

    out = dict(_drawn_inputs(seed))
    spreads = {}
    factors = {'conv_b': 2.926, 'conv_ln_g': 13.922, 'conv_ln_b': 32.941, 'subln_a': 17.234}
    for name, (base, spread) in spreads.items():
        noise = np.random.default_rng([zlib.crc32(name.encode()), seed]).standard_normal(out[name].shape)
        drawn = base * np.exp(spread * noise) if base else spread * noise
        out[name] = jnp.asarray(drawn.astype(out[name].dtype))
    for name, factor in factors.items():
        out[name] = (out[name] * factor).astype(out[name].dtype)
    return out
```

```python
import math
from contextlib import ExitStack

import numpy as np

import concourse.bass as bass
from concourse import mybir

F32 = mybir.dt.float32
I32 = mybir.dt.int32
ALU = mybir.AluOpType
ACT = mybir.ActivationFunctionType
X = mybir.AxisListType.X

P = 128
D = 1024
N_PROMPT = 256
DEC_B, DEC_T = 8, 8
N_SAMPLE = DEC_B * DEC_T
TOK = N_PROMPT + N_SAMPLE
SZ = [P, P, N_SAMPLE]
OFF = [0, P, 2 * P]
KD = D // P
PAST, PAGE = 256, 128
PAGES = PAST // PAGE
H = 4
DQK, DV_A = 64, 128
ATT_W = H * DV_A
CONV_CH, CONV_W = 512, 31
CC = CONV_CH // P
HIST = CONV_W - 1
DK_C, DV_C = 256, 512
N_EXP, N_GRP, PER_GRP = 16, 4, 4
D_FF = 512
KF = D_FF // P
ALPHA = float((2 * 2) ** 0.25)
EPS = 1e-5
SLOTS = P
MAX_PASSES = (TOK + SLOTS - 1) // SLOTS
NSLOT = MAX_PASSES * SLOTS
RING = 6
LAM_INIT = 0.8 - 0.6 * math.exp(-0.3 * 0)
NEG = -1e30

LOG_G = np.log1p(-np.exp2(-5.0 - np.arange(H, dtype=np.float64)))


def layout(*fields):
    at, out = 0, {}
    for name, width in fields:
        out[name] = (at, width)
        at += width
    return out, at


GEN, GEN_W = layout(("ident", P), ("before", P), ("ones", P), ("eidx", 3 * N_EXP), ("gidx", 3 * N_GRP),
                    ("ecol", N_EXP), ("thr", MAX_PASSES))
TBA, TBA_W = layout(("cos", 3 * 8), ("sin", 3 * 8), ("mask", P), ("smask", 4 * N_SAMPLE), ("pair", N_SAMPLE),
                    ("sgn", 2))
TBC, TBC_W = layout(("cos", TOK), ("sin", TOK), ("dec", H * P), ("sdec", H * N_SAMPLE), ("qdec", H * (TOK - P)),
                    ("kdec", 3 * H), ("own", DEC_B))


def host_tables():
    f = np.float32
    p = np.arange(P)
    gen = np.zeros((P, GEN_W), f)

    def put(t, lay, name, a):
        at, w = lay[name]
        t[:, at:at + w] = np.asarray(a, f).reshape(P, w)

    put(gen, GEN, "ident", np.eye(P))
    put(gen, GEN, "before", p[:, None] < p[None, :])
    put(gen, GEN, "ones", np.ones((P, P)))
    put(gen, GEN, "eidx", np.tile(np.arange(N_EXP) - 32.0, (P, 3)))
    put(gen, GEN, "gidx", np.tile(np.arange(N_GRP) - 8.0, (P, 3)))
    put(gen, GEN, "ecol", np.tile(np.arange(N_EXP), (P, 1)))
    put(gen, GEN, "thr", np.tile(np.arange(MAX_PASSES) * float(SLOTS), (P, 1)))

    pos = np.concatenate([np.arange(N_PROMPT), np.tile(PAST + np.arange(DEC_T), DEC_B)]).astype(f)
    tba = np.zeros((P, TBA_W), f)
    inv = f(500000.0) ** (-np.arange(0, 16, 2, dtype=f) / f(16))
    ang = pos[:, None] * inv[None, :].astype(f)
    ca, sa = np.zeros((3 * P, 8), f), np.zeros((3 * P, 8), f)
    ca[:TOK], sa[:TOK] = np.cos(ang), np.sin(ang)
    put(tba, TBA, "cos", ca.reshape(3, P, 8).transpose(1, 0, 2))
    put(tba, TBA, "sin", sa.reshape(3, P, 8).transpose(1, 0, 2))
    put(tba, TBA, "mask", np.where(p[None, :] <= p[:, None], 0.0, NEG))
    b2, m, q = p // 64, (p // 8) % 8, p % 8
    cb, ct = np.arange(64) // 8, np.arange(64) % 8
    sm = np.stack([np.where((cb[None] == 2 * g + b2[:, None]) & (ct[None] <= q[:, None]), 0.0, NEG) for g in range(4)], 1)
    put(tba, TBA, "smask", sm)
    cols = np.arange(64)
    put(tba, TBA, "pair", (b2[:, None] == cols[None] // 32) & (m[:, None] // 2 == (cols[None] // 8) % 4)
        & (q[:, None] == cols[None] % 8))
    put(tba, TBA, "sgn", np.stack([m % 2 == 0, m % 2 == 1], 1))

    tbc = np.zeros((P, TBC_W), f)
    inv = f(10000.0) ** (-np.linspace(0.0, 1.0, DK_C // 2, dtype=f))
    ang = (pos[:, None] * inv[None, :].astype(f)).astype(f)
    put(tbc, TBC, "cos", np.cos(ang).T)
    put(tbc, TBC, "sin", np.sin(ang).T)
    d = p[None, :] - p[:, None]
    dec = np.stack([np.where(d >= 0, np.exp(np.maximum(d, 0) * LOG_G[h]), 0.0) for h in range(H)], 1)
    put(tbc, TBC, "dec", dec)
    i = np.arange(64)
    ds = i[None, :] % 8 - i[:, None] % 8
    same = i[None, :] // 8 == i[:, None] // 8
    sd = np.zeros((P, H, 64))
    sd[:64] = np.stack([np.where(same & (ds >= 0), np.exp(np.maximum(ds, 0) * LOG_G[h]), 0.0) for h in range(H)], 1)
    put(tbc, TBC, "sdec", sd)
    idx = np.concatenate([p, i % 8])
    put(tbc, TBC, "qdec", np.tile(np.stack([np.exp((idx + 1) * LOG_G[h]) for h in range(H)])[None], (P, 1, 1)))
    kd = np.zeros((P, 3, H))
    for h in range(H):
        kd[:, 0, h] = kd[:, 1, h] = np.exp((P - 1 - p) * LOG_G[h])
        kd[:64, 2, h] = np.exp((DEC_T - 1 - i % 8) * LOG_G[h])
    put(tbc, TBC, "kdec", kd)
    own = np.zeros((P, DEC_B))
    own[:64] = i[:, None] // 8 == np.arange(8)[None]
    put(tbc, TBC, "own", own)

    entry = np.zeros((P, 3, 2, 4), np.int32)
    tok = np.arange(3)[None, :, None] * P + p[:, None, None]
    entry[..., 0] = tok
    entry[..., 1] = np.arange(2)[None, None] * TOK + tok
    empty = np.zeros((NSLOT * N_EXP, 4), np.int32)
    empty[:, 1] = 1 << 20
    return {"gen": gen, "tba": tba, "tbc": tbc, "entry": entry.reshape(P, 24), "empty": empty}


def build(nc, a, o):
    with ExitStack() as ctx:
        def sb(name, shape, dt=F32):
            return ctx.enter_context(nc.sbuf_tensor(name, [P] + shape, dt))

        def sem(name):
            return ctx.enter_context(nc.semaphore(name))

        x_rows = [nc.dram_tensor(f"x_rows{l}", (TOK, D), F32, kind="Internal").ap() for l in range(2)]
        y_rows = [nc.dram_tensor(f"y_rows{l}", (2 * TOK, D), F32, kind="Internal").ap() for l in range(2)]
        table = [nc.dram_tensor(f"table{l}", (NSLOT * N_EXP, 4), I32, kind="Internal").ap() for l in range(2)]

        ring = sb("ring", [RING, 4096])
        x = sb("x", [3, D])
        xT = sb("xT", [KD, TOK])
        gen = sb("gen_sb", [GEN_W])
        wr = sb("wr", [KD, N_EXP])
        rbias = sb("rbias", [N_EXP])
        entry = sb("entry_sb", [3, 2, 4], I32)
        stat = sb("stat", [3, 2, 6])
        mv = sb("mv", [3, 2])
        rstd = sb("rstd", [3, 1])
        epsc = sb("epsc", [1])
        lgT = sb("lgT", [TOK])
        rt = sb("rt", [12, 3, N_EXP])
        rs = sb("rs", [12, 3, N_GRP])
        r1 = sb("r1", [12, 3])
        slot_i = sb("slot_i", [3, 2], I32)
        passes_i = sb("passes_i", [1], I32)
        slot_pages = sb("slot_pages", [DEC_B * PAGES], I32)
        SCR = 21184
        scratch = sb("scratch", [SCR])
        ps = ctx.enter_context(nc.psum_tensor("ps", [P, 8, 512], F32))

        def carve(*fields):
            at, out = 0, {}
            for name, n, *start in fields:
                s = out[start[0]][1] + (start[1] if len(start) > 1 else 0) if start else at
                out[name] = (scratch[:, s:s + n], s)
                if not start:
                    at += n
            assert at <= SCR, at
            return {k: v[0] for k, v in out.items()}

        A = carve(("qkv", 3 * 1536), ("qT", H * TOK), ("kT", H * TOK), ("up", CC * (HIST + N_PROMPT)),
                  ("us", CC * DEC_B * (HIST + DEC_T)), ("acc", CC * TOK), ("sig", 2 * TOK),
                  ("kp", 2 * PAGES * 512), ("vp", 2 * PAGES * 512), ("QB", 2 * H * 64),
                  ("e", 2 * 512), ("w", 256), ("wT", 256), ("es", TOK), ("wTs", 192),
                  ("ao", DEC_B * DV_A), ("tba", TBA_W), ("subln", DV_A), ("cwT", CC * 32), ("small", 128),
                  ("lam", 4 * DQK),
                  ("mixT", KD * TOK, "up"), ("clg", 1024, "up"), ("ao2", 1024, "kp"), ("lngb", 2048, "vp"),
                  ("stin", 1024, "ao"), ("cwin", 512, "es"), ("uo", 1024, "e"))
        C = carve(("q", 2 * TOK), ("k", 2 * TOK), ("qd", 2 * (TOK - P)), ("v", 3 * DV_C), ("g", 16 * TOK),
                  ("kd", 3 * DK_C), ("kdm", DEC_B * DK_C), ("sc", 2 * P + 64), ("S", 2 * DV_C), ("o", 4 * DV_C),
                  ("s0", 3 * 2 * DV_C), ("tmp", 4 * TOK), ("tbc", TBC_W), ("small", 64),
                  ("lngb", 2048, "o"))
        M = carve(("xg", 2 * D), ("xgT", 2 * KD * SLOTS), ("sg", KF * SLOTS), ("hid", KF * SLOTS), ("y", 2 * D),
                  ("tab", N_EXP * 4), ("gate", 2), ("yy", 3 * 2 * D), ("lngb", 2048))

        def gcol(name):
            at, w = GEN[name]
            return gen[:, at:at + w]

        ident, before, ones = gcol("ident"), gcol("before"), gcol("ones")

        def acol(name):
            at, w = TBA[name]
            return A["tba"][:, at:at + w]

        def ccol(name):
            at, w = TBC[name]
            return C["tbc"][:, at:at + w]

        bank_full = [sem(f"bank_full{b}") for b in range(8)]
        bank_read = [sem(f"bank_read{b}") for b in range(8)]
        jobs, turns = {}, [0] * 8

        def plan(name, bank):
            jobs[name] = (bank, turns[bank])
            turns[bank] += 1

        def plan_mixer_a():
            rot = [("cw",), ("st", 0), ("st", 1)]
            rot += [("xT0", t, i) for t in range(3) for i in range(2)]
            rot += [("a", c) for c in range(CC)] + [("g", c) for c in range(CC)]
            rot += [("qkv", n, t) for n in range(3) for t in range(3)]
            rot += [("qkT", n, t) for n in range(2) for t in range(3)]
            rot += [("uo", i) for i in range(2)]
            rot += [("cvt", t) for t in range(3)]
            for n, name in enumerate(rot):
                plan(name, n % 8)
            for it in range(9):
                if it < 8:
                    plan(("S", it, 0), 0)
                    plan(("S", it, 1), 1)
                    if it % 2 == 0:
                        for i in range(4):
                            plan(("kpT", it // 2, i), 4 + i % 2)
                        plan(("SS", it // 2), 6)
                    else:
                        plan(("wTs", it // 2), 4)
                        if it % 4 == 1:
                            plan(("AO", it // 4), 7)
                if it >= 1:
                    plan(("wT", it - 1), 2)
                    if (it - 1) % 4 == 0:
                        plan(("O", (it - 1) // 4), 3)
            for i in range(2):
                plan(("att", i), i)
                plan(("aoT", i), 4 + i)
            for t in range(3):
                plan(("cT", t), (2, 6, 7)[t])
            for n in range(2):
                for t in range(3):
                    plan(("out0", n, t), (3, 0, 1, 2, 4, 5)[3 * n + t])

        def plan_mixer_c():
            for h in range(H):
                for i in range(2):
                    for c in range(2):
                        plan(("qk", h, i, c), 2 * i + c)
                for t in range(3):
                    plan(("v", h, t), 4 + t)
                if h:
                    for e in range(4):
                        plan(("oT", h - 1, e), (7, 0, 1, 2)[e])
                for name, b in ((("sc", h), 7), (("gg", h, 0), 3), (("kd", h, 0), 0), (("kd", h, 1), 1),
                                (("gg", h, 1), 2), (("S1", h, 0), 4), (("S1", h, 1), 5), (("o", h, 0), 6),
                                (("gg", h, 2), 3), (("o", h, 1), 7), (("S2", h, 0), 4), (("S2", h, 1), 5),
                                (("gg", h, 3), 0), (("o", h, 2), 1), (("o", h, 3), 2)):
                    plan(name, b)
                for b in range(DEC_B):
                    for c in range(2):
                        plan(("sn", h, b, c), 4 + c)
            for e in range(4):
                plan(("oT", H - 1, e), (7, 0, 3, 6)[e])
            for n in range(2):
                for t in range(3):
                    plan(("out1", n, t), (1, 2, 4, 5, 7, 0)[3 * n + t])

        def plan_router(l):
            for n, name in enumerate([("xTm", l, t, i) for t in range(3) for i in range(2)] +
                                     [("lg", l), ("lgt", l), ("rank", l)]):
                plan(name, n % 8)

        turns_before_experts = []
        plan_mixer_a()
        plan_router(0)
        turns_before_experts.append(list(turns))
        for n, name in enumerate([("xT1", t, i) for t in range(3) for i in range(2)]):
            plan(name, n)
        plan_mixer_c()
        plan_router(1)
        turns_before_experts.append(list(turns))

        def bank(name):
            return ps[:, jobs[name][0], :]

        def claim(eng, name):
            b, k = jobs[name]
            if k:
                eng.wait_ge(bank_read[b], k)

        def full(name):
            return bank_full[jobs[name][0]]

        def read(name):
            return bank_read[jobs[name][0]]

        def await_full(eng, name):
            eng.wait_ge(bank_full[jobs[name][0]], jobs[name][1] + 1)

        def await_read(eng, name):
            eng.wait_ge(bank_read[jobs[name][0]], jobs[name][1] + 1)

        w_landed = [sem(f"w_landed{s}") for s in range(RING)]
        e_landed = [[sem(f"e_landed{l}_{s}") for s in range(RING)] for l in range(2)]
        last_job = {}
        for n in range(2):
            last_job[0, n] = ("ag"[n], CC - 1)
            last_job[0, 5 + n] = ("out0", n, 2)
            for r in range(2):
                last_job[1, 12 + 2 * n + r] = ("out1", n, 2)
        for n in range(3):
            last_job[0, 2 + n] = ("qkv", n, 2)
        for h in range(H):
            last_job[1, 3 * h] = ("qk", h, 1, 1)
            last_job[1, 3 * h + 1] = ("v", h, 2)
            last_job[1, 3 * h + 2] = ("gg", h, 3)
        loads, landed_at, last_in_slot = {}, [0] * RING, [{}, {}]
        for l, (count, first) in enumerate(((7, 5), (16, 2))):
            for n in range(count):
                s = (first + n) % RING
                landed_at[s] += 32 if l == 1 and n < 12 and n % 3 == 0 else 16
                loads[l, n] = (s, landed_at[s])
                last_in_slot[l][s] = last_job[l, n]

        def w_block(l, n):
            return ring[:, loads[l, n][0], :].rearrange("p (k c) -> p k c", c=512)

        def w_arrived(pe, l, n):
            pe.wait_ge(w_landed[loads[l, n][0]], loads[l, n][1])

        names = """x_in tables_in tba_in   lam_in pt_in clg_in empty_in pool_met stored kept_out
                 kv_out dve_step pool_step pads_zero conv_step conv_done rot_step lam_sums lam_exp cn_var
                 cn_std cn_pre cn_post S_bias w_done kp_in vp_in kp_new QB_set SS_bias
                 ps_done ao_zero ao_read_k att_ss att_std att_done ao_done u_out tbc_in
                 qk_rot kdm_set os_zero on_var on_std sn_done S2_done S2_out g_done ln_in
                 ln_var ln_std x_done x_stored lgs_ready lg_exp mask_ready entries rows_in passes_ready
                 yy_in u_set""".split()
        S = {n: sem(n) for n in names}
        s0_in = [sem(f"s0_in{i}") for i in range(3)]
        s0_out = [sem(f"s0_out{i}") for i in range(3)]
        loop_names = "tab_in tr_full0 tr_full1 tr_act tr_dve g_full silu_done u_full hid_done y_full0 y_full1 ya_done yd_done".split()
        L = [{n: sem(f"{n}_{l}") for n in loop_names} for l in range(2)]
        xg_in = [[sem(f"xg_in{l}_{i}") for i in range(2)] for l in range(2)]
        y_out = [[sem(f"y_out{l}_{i}") for i in range(2)] for l in range(2)]
        slot_open = [[sem(f"slot_open{l}_{i}") for i in range(2)] for l in range(2)]

        block = ctx.enter_context(nc.Block())

        qkv = A["qkv"].rearrange("p (t c) -> p t c", t=3)
        qT = A["qT"].rearrange("p (h t) -> p h t", h=H)
        kT = A["kT"].rearrange("p (h t) -> p h t", h=H)
        up = A["up"].rearrange("p (c t) -> p c t", c=CC)
        us = A["us"].rearrange("p (c b t) -> p c b t", c=CC, b=DEC_B)
        acc = A["acc"].rearrange("p (c t) -> p c t", c=CC)
        sig = A["sig"].rearrange("p (i t) -> p i t", i=2)
        un = A["sig"][:, 0:CC * N_SAMPLE].rearrange("p (c t) -> p c t", c=CC)
        kp = A["kp"].rearrange("p (b g c) -> p b g c", b=2, g=PAGES)
        vp = A["vp"].rearrange("p (b g c) -> p b g c", b=2, g=PAGES)
        QB = A["QB"].rearrange("p (b h c) -> p b h c", b=2, h=H)
        ebuf = A["e"].rearrange("p (i m k) -> p i m k", i=2, m=2)
        wbuf = A["w"]
        wT = A["wT"].rearrange("p (k q) -> p k q", k=2)
        es = A["es"]
        wTs = A["wTs"].rearrange("p (k c) -> p k c", k=3)
        ao = A["ao"].rearrange("p (b e) -> p b e", b=DEC_B)
        ao2 = A["ao2"].rearrange("p (b e) -> p b e", b=DEC_B)
        cwT = A["cwT"].rearrange("p (c j) -> p c j", c=CC)
        mixT = A["mixT"].rearrange("p (k t) -> p k t", k=KD)
        kpT = xT[:, :, :].rearrange("p (b h) t -> p b h t", b=2)
        uo = A["uo"].rearrange("p (i c) -> p i c", i=2)
        stin = A["stin"].rearrange("p (i c) -> p i c", i=2)
        cwin = A["cwin"]
        lam_in = A["lam"].rearrange("p (i d) -> p i d", i=4)
        sm = A["small"]
        mx, nb, sums = sm[:, 0:2], sm[:, 2:4], sm[:, 4:8].rearrange("p (i m) -> p i m", i=2)
        rr, smx, snb, ssum, srl = sm[:, 8:10], sm[:, 10:11], sm[:, 11:12], sm[:, 12:13], sm[:, 13:14]
        neglam, lamrow, lam2 = sm[:, 14:15], sm[:, 15:16], sm[:, 16:18]
        cvar, cstd = sm[:, 18:24].rearrange("p (t c) -> p t c", t=3), sm[:, 24:27]
        ss_att, rs_att = sm[:, 32:40], sm[:, 40:48]
        ss_ao, rs_ao = sm[:, 48:56], sm[:, 56:64]

        qr = C["q"].rearrange("p (c t) -> p c t", c=2)
        kr = C["k"].rearrange("p (c t) -> p c t", c=2)
        qd = C["qd"].rearrange("p (c t) -> p c t", c=2)
        vh = C["v"].rearrange("p (t e) -> p t e", t=3)
        gT = C["g"].rearrange("p (k t) -> p k t", k=16)
        kd = C["kd"].rearrange("p (t d) -> p t d", t=3)
        kdm = C["kdm"].rearrange("p (b d) -> p b d", b=DEC_B)
        sc = C["sc"]
        St = C["S"].rearrange("p (c e) -> p c e", c=2)
        ob = C["o"].rearrange("p (t e) -> p t e", t=4)
        s0b = C["s0"].rearrange("p (i c e) -> p i c e", i=3, c=2)
        tmp = C["tmp"].rearrange("p (i t) -> p i t", i=4)
        cm = C["small"]
        ovar, ostd, ostat = cm[:, 0:8].rearrange("p (t c) -> p t c", t=4), cm[:, 8:12], cm[:, 16:40].rearrange("p (t c) -> p t c", t=4)

        xg = M["xg"].rearrange("p (i d) -> p i d", i=2)
        xgT = M["xgT"].rearrange("p (i k s) -> p i k s", i=2, k=KD)
        sg, hid = M["sg"], M["hid"].rearrange("p (j s) -> p j s", j=KF)
        yb = M["y"].rearrange("p (i d) -> p i d", i=2)
        tab = M["tab"].bitcast(I32).rearrange("p (e w) -> p e w", e=N_EXP)
        tabf = M["tab"].rearrange("p (e w) -> p e w", e=N_EXP)
        gate = M["gate"]
        yy = M["yy"].rearrange("p (c t d) -> p c t d", c=2, t=3)

        def cols_a(t):
            return slice(OFF[t], OFF[t] + SZ[t])

        def rows(dram, t0, n):
            return dram[t0:t0 + n, :]

        def bcast(ap, shape):
            return ap.broadcast_to([P] + shape)

        def pass_count(eng):
            return eng.value_load(passes_i[0:1, 0:1], min_val=1, max_val=MAX_PASSES)

        def over_passes(l, eng, pass_body):
            eng.wait_ge(S["passes_ready"], l + 1)
            with eng.Fori(0, pass_count(eng)) as n:
                pass_body(n)

        @block.sync
        def _(sp):
            wa = a["w_in_a"][0].rearrange("(p k) c -> p k c", k=KD)
            wo = a["w_out_a"][0].rearrange("(k p) c -> p k c", p=P)
            wc = a["w_in_c"][0].rearrange("(p k) c -> p k c", k=KD)
            woc = a["w_out_c"][0].rearrange("(r k p) c -> r p k c", p=P, r=2)

            def load(l, n, parts):
                if n >= RING:
                    await_full(sp, last_job[l, n - RING])
                for c0, src in parts:
                    dst = w_block(l, n)[:, :, c0:c0 + src.shape[-1]]
                    sp.dma_start(dst, src).then_inc(w_landed[loads[l, n][0]], 16)

            def expert_loads(l, e0, used):
                gu = [a["w_e_gate"][l], a["w_e_up"][l]]
                for par in range(2):
                    e = e0 + par
                    for j in range(3):
                        s = 3 * par + j
                        if used is None:
                            await_full(sp, last_in_slot[l][s])
                        else:
                            sp.wait_ge(L[l][("g_full", "u_full", "y_full1")[j]], used + (par + 1))
                        if j < 2:
                            src = gu[j].rearrange("n (p k) f -> n p (k f)", k=KD)[bass.ds(e, 1)].rearrange("n p f -> (n p) f")
                            dst = ring[:, s, :]
                        else:
                            src = a["w_e_down"][l].rearrange("n (j p) d -> n p j d", p=P)[bass.ds(e, 1)].rearrange("n p j d -> (n p) j d")
                            dst = ring[:, s, :].rearrange("p (j d) -> p j d", j=KF)
                        sp.dma_start(dst, src).then_inc(e_landed[l][s], 16)

            def experts(l):
                expert_loads(l, 0, None)
                with sp.Fori(1, N_EXP // 2) as i:
                    expert_loads(l, i * 2, i * 2 - 2)
                sp.wait_ge(S["passes_ready"], l + 1)
                n = pass_count(sp)
                with sp.If(n > 1):
                    with sp.Fori(1, n) as q:
                        with sp.Fori(0, N_EXP // 2) as i:
                            expert_loads(l, i * 2, q * N_EXP + i * 2 - 2)
                sp.nop()
                return n

            for n, c0 in enumerate((1536, 2048, 0, 512, 1024)):
                load(0, n, [(0, wa[:, :, c0:c0 + 512])])
            for n in range(2):
                load(0, 5 + n, [(0, wo[:, :, n * 512:n * 512 + 512])])
            n_passes = experts(0)
            sp.wait_ge(L[0]["y_full1"], n_passes * N_EXP)
            for h in range(H):
                load(1, 3 * h, [(0, wc[:, :, h * DK_C:(h + 1) * DK_C]), (DK_C, wc[:, :, D + h * DK_C:D + (h + 1) * DK_C])])
                for j in range(2):
                    c0 = 2 * D + j * 2 * D + h * DV_C
                    load(1, 3 * h + 1 + j, [(0, wc[:, :, c0:c0 + DV_C])])
            for n in range(2):
                for r in range(2):
                    load(1, 12 + 2 * n + r, [(0, woc[r][:, :, n * 512:n * 512 + 512])])
            experts(1)
            sp.wait_ge(S["stored"], 16 * 2)
            sp.wait_ge(S["kept_out"], 16)

        def counted(pool, semaphore, value):
            pool.wait_ge(semaphore, value)
            pool.sem_inc(S["pool_met"], 1)

        def experts_pool(pool, l):
            Q = L[l]
            pool.wait_ge(S["entries"], l + 1)
            pool.wait_ge(S["empty_in"], 32)
            for t in range(3):
                for c in range(2):
                    pool.indirect_dma_start(
                        out=table[l], out_offset=bass.IndirectOffsetOnAxis(ap=slot_i[0:SZ[t], t, c:c + 1], axis=0),
                        in_=entry[0:SZ[t], t, c, :], in_offset=None).then_inc(S["rows_in"], 16)
            pool.wait_ge(S["rows_in"], 96 * (l + 1))
            pool.wait_ge(S["x_stored"], 32 * (l + 1))

            def one_pass(n):
                pool.dma_start(tab.rearrange("p e w -> p (e w)"),
                               table[l].rearrange("(s e) w -> s (e w)", e=N_EXP)[bass.ds(n * SLOTS, SLOTS), :]).then_inc(Q["tab_in"], 16)
                counted(pool, Q["tab_in"], n * 16 + 16)

                def open_slot(e):
                    pool.tensor_copy(gate[:, e % 2:e % 2 + 1], tabf[:, e, 2:3]).then_inc(slot_open[l][e % 2], 1)
                    if e >= 2:
                        counted(pool, Q["tr_full1"], n * N_EXP + (e - 1))
                    pool.indirect_dma_start(
                        out=xg[:, e % 2, :], out_offset=None, in_=x_rows[l],
                        in_offset=bass.IndirectOffsetOnAxis(ap=tab[:, e, 0:1], axis=0)).then_inc(xg_in[l][e % 2], 16)

                open_slot(0)
                open_slot(1)
                for e in range(N_EXP):
                    counted(pool, Q["ya_done"], n * N_EXP + (e + 1))
                    counted(pool, Q["yd_done"], n * N_EXP + (e + 1))
                    pool.indirect_dma_start(
                        out=y_rows[l], out_offset=bass.IndirectOffsetOnAxis(ap=tab[:, e, 1:2], axis=0),
                        in_=yb[:, e % 2, :], in_offset=None, bounds_check=2 * TOK - 1, oob_is_err=False).then_inc(y_out[l][e % 2], 16)
                    counted(pool, y_out[l][e % 2], n * (8 * N_EXP) + 16 * (e // 2 + 1))
                    if e + 2 < N_EXP:
                        open_slot(e + 2)

            over_passes(l, pool, one_pass)

        @block.gpsimd
        def _(pool):
            steps = [0]

            def link(ins):
                steps[0] += 1
                ins.then_inc(S["pool_step"], 1)
                pool.wait_ge(S["pool_step"], steps[0])

            pool.memset(up[:, :, 0:HIST], 0.0).then_inc(S["pads_zero"], 1)
            pool.memset(QB[:, :, :, :], 0.0).then_inc(S["pads_zero"], 1)
            pool.memset(epsc[:, :], EPS).then_inc(S["pads_zero"], 1)
            pool.memset(mv[:, :, :], 1.0).then_inc(S["pads_zero"], 1)
            pool.memset(rt[:, :, :, :], 0.0).then_inc(S["pads_zero"], 1)
            pool.memset(sm[:, :], 1.0).then_inc(S["pads_zero"], 1)
            for l in range(2):
                pool.dma_start(table[l], a["empty"]).then_inc(S["empty_in"], 16)
            pool.dma_start(slot_pages[0:1, :], a["page_table"].rearrange("b g -> (b g)").rearrange("(o n) -> o n", o=1)).then_inc(S["pt_in"], 16)
            pool.dma_start(o["conv_sample"][0][:, 0:HIST - DEC_T, :], a["state_conv"][0][:, DEC_T:HIST, :]).then_inc(S["kept_out"], 16)
            pool.wait_ge(S["pt_in"], 16)

            def load_pages(g):
                for b in range(2):
                    for pg in range(PAGES):
                        page = pool.value_load(slot_pages[0:1, (2 * g + b) * PAGES + pg:(2 * g + b) * PAGES + pg + 1],
                                               min_val=0, max_val=a["cache_k"].shape[1] - 1)
                        for dst, cache, landed in ((kp, "cache_k", "kp_in"), (vp, "cache_v", "vp_in")):
                            src = a[cache][0].rearrange("n s m d -> n s (m d)")[bass.ds(page, 1)].rearrange("n s c -> (n s) c")
                            pool.dma_start(dst[:, b, pg, :], src).then_inc(S[landed], 16)

            load_pages(0)

            cosA = acol("cos").rearrange("p (t j) -> p t j", t=3)
            sinA = acol("sin").rearrange("p (t j) -> p t j", t=3)
            tr = A["w"].rearrange("p (m j) -> p m j", j=8), A["wT"].rearrange("p (m j) -> p m j", j=8)
            pool.wait_ge(S["tba_in"], 16)
            for t in range(3):
                await_read(pool, ("qkv", 1, t))
                await_read(pool, ("qkv", 0, t))
                z = SZ[t]
                v = qkv[0:z, t, 0:1024].rearrange("p (m d) -> p m d", d=DQK)
                t1, t2 = v[:, :, 0:8], v[:, :, 8:16]
                c8 = cosA[0:z, t, :].unsqueeze(1).broadcast_to([z, 16, 8])
                s8 = sinA[0:z, t, :].unsqueeze(1).broadcast_to([z, 16, 8])
                a1, a2 = tr[0][0:z, 0:16], tr[0][0:z, 16:32]
                b1, b2 = tr[1][0:z, 0:16], tr[1][0:z, 16:32]
                pool.tensor_tensor(a1, t1, c8, ALU.mult)
                pool.tensor_tensor(a2, t2, s8, ALU.mult)
                pool.tensor_tensor(b1, t2, c8, ALU.mult)
                link(pool.tensor_tensor(b2, t1, s8, ALU.mult))
                pool.tensor_tensor(t1, a1, a2, ALU.subtract)
                ins = pool.tensor_tensor(t2, b1, b2, ALU.add)
                ins.then_inc(S["rot_step"], 1)
                pool.wait_ge(S["rot_step"], t + 1)
            kdst = [o["k_prompt"][0, 0].rearrange("(t p) m d -> p t (m d)", p=P), o["k_sample"][0].rearrange("b t m d -> (b t) (m d)")]
            vdst = [o["v_prompt"][0, 0].rearrange("(t p) m d -> p t (m d)", p=P), o["v_sample"][0].rearrange("b t m d -> (b t) (m d)")]
            for t in range(3):
                await_read(pool, ("qkv", 2, t))
            for dst, c0 in ((kdst, 512), (vdst, 1024)):
                pool.dma_start(dst[0], qkv[:, 0:2, c0:c0 + 512]).then_inc(S["kv_out"], 16)
                pool.dma_start(dst[1], qkv[0:64, 2, c0:c0 + 512]).then_inc(S["kv_out"], 16)

            for t in range(3):
                await_read(pool, ("qkT", 0, t))
            for g in range(4):
                if g:
                    await_full(pool, ("SS", g - 1))
                for h in range(H):
                    for half in range(2):
                        hp = slice(64 * half, 64 * half + 64)
                        c0 = 16 * h + 8 * half
                        src = qT[hp, h, 2 * P + 16 * g:2 * P + 16 * g + 16].rearrange("p (b q) -> p b q", b=2)
                        pool.tensor_copy(QB[hp, :, h, c0:c0 + 8], src).then_inc(S["QB_set"], 1)
                if g < 3:
                    await_full(pool, ("SS", g))
                    await_full(pool, ("wT", 2 * g))
                    load_pages(g + 1)
            experts_pool(pool, 0)
            pool.wait_ge(S["x_done"], 2)
            pool.wait_ge(S["yy_in"], 64)
            pool.wait_ge(S["tbc_in"], 16)

            def state(dram, b, h):
                return dram[0, b, h].rearrange("(c p) e -> p c e", p=P)

            def load_state(j):
                pool.dma_start(s0b[:, j % 3], state(a["state_ret"], j % DEC_B, j // DEC_B)).then_inc(s0_in[j % 3], 16)

            for j in range(3):
                load_state(j)
            own = ccol("own")
            for h in range(H):
                await_read(pool, ("kd", h, 1))
                kd_src = kd[0:64, 2, :]
                for b in range(DEC_B):
                    pool.tensor_scalar(kdm[0:64, b, :], kd_src, own[0:64, b:b + 1], None, ALU.mult).then_inc(S["kdm_set"], 1)
                for b in range(DEC_B):
                    j = h * DEC_B + b
                    pool.wait_ge(S["sn_done"], 2 * (j + 1))
                    pool.dma_start(state(o["ret_sample"], b, h), s0b[:, j % 3]).then_inc(s0_out[j % 3], 16)
                    if j >= 1 and j + 2 < H * DEC_B:
                        pool.wait_ge(s0_out[(j - 1) % 3], 16 * ((j - 1) // 3 + 1))
                        load_state(j + 2)
                    if b == 0:
                        pool.wait_ge(S["S2_done"], 2 * (h + 1))
                        pool.dma_start(o["ret_prompt"][0, 0, h].rearrange("(c p) e -> p c e", p=P), St).then_inc(S["S2_out"], 16)
            for i in range(3):
                pool.wait_ge(s0_out[i], 16 * len(range(i, H * DEC_B, 3)))
            pool.wait_ge(S["S2_out"], 16 * H)
            experts_pool(pool, 1)

        def norm_act(act, k, lngb, _):
            l, j = k // 2, k % 2
            if k == 0:
                await_full(act, ("wT", 6))
            if k == 2:
                await_full(act, ("oT", H - 1, 3))
            act.dma_start(lngb[:, 0:D], a["ln_g"][l, j].partition_broadcast(P)).then_inc(S["ln_in"], 16)
            act.dma_start(lngb[:, D:2 * D], a["ln_b"][l, j].partition_broadcast(P)).then_inc(S["ln_in"], 16)
            act.wait_ge(S["ln_var"], 3 * (k + 1))
            act.activation(rstd[:, :, 0], mv[:, :, 1], ACT.Sqrt, bias=epsc[:, 0:1]).then_inc(S["ln_std"], 1)

        def experts_act(act, l):
            Q = L[l]
            act.wait_ge(S["x_done"], 2 * l + 1)
            act.dma_start(x_rows[l][0:2 * P, :].rearrange("(t p) d -> p t d", p=P), x[:, 0:2, :]).then_inc(S["x_stored"], 16)
            act.dma_start(x_rows[l][2 * P:TOK, :], x[0:64, 2, :]).then_inc(S["x_stored"], 16)
            for t in range(3):
                await_full(act, ("xTm", l, t, 0))
                act.activation(xT[:, 0:4, cols_a(t)], bank(("xTm", l, t, 0))[:, 0:4 * SZ[t]].rearrange("p (k t) -> p k t", k=4),
                               ACT.Copy).then_inc(read(("xTm", l, t, 0)), 1)
            act.wait_ge(S["lgs_ready"], l + 1)
            act.activation(rt[:, 1, :, :], rt[:, 0, :, :], ACT.Exp).then_inc(S["lg_exp"], 1)

            def turn_rows(j, k):
                act.wait_ge(Q["tr_full0"], k)
                act.activation(xgT[:, j, 0:4, :], ps[:, 0, :].rearrange("p (k s) -> p k s", k=4), ACT.Copy).then_inc(Q["tr_act"], 1)

            def one_pass(n):
                turn_rows(0, n * N_EXP + 1)

                def expert(par, k, u, last=False):
                    act.wait_ge(Q["g_full"], k)
                    act.activation(sg, ps[:, 2, :], ACT.Silu).then_inc(Q["silu_done"], 1)
                    if not last:
                        turn_rows(1 - par, k + 1)
                    act.wait_ge(Q["y_full0"], k)
                    act.wait_ge(slot_open[l][par], u)
                    act.activation(yb[:, par, 0:512], ps[:, 4 + 2 * par, :], ACT.Copy, scale=gate[:, par:par + 1]).then_inc(Q["ya_done"], 1)

                with act.Fori(0, N_EXP // 2 - 1) as i:
                    for par in range(2):
                        expert(par, n * N_EXP + i * 2 + (par + 1), n * (N_EXP // 2) + i + 1)
                expert(0, n * N_EXP + (N_EXP - 1), n * (N_EXP // 2) + N_EXP // 2)
                expert(1, n * N_EXP + N_EXP, n * (N_EXP // 2) + N_EXP // 2, last=True)

            over_passes(l, act, one_pass)
            n = pass_count(act)
            for i in range(2):
                act.wait_ge(y_out[l][i], n * (8 * N_EXP))
            for c in range(2):
                act.dma_start(yy[:, c, 0:2, :], y_rows[l][c * TOK:c * TOK + 2 * P, :].rearrange("(t p) d -> p t d", p=P)).then_inc(S["yy_in"], 16)
                act.dma_start(yy[0:64, c, 2, :], y_rows[l][c * TOK + 2 * P:(c + 1) * TOK, :]).then_inc(S["yy_in"], 16)
            norm_act(act, 2 * l + 1, M["lngb"], None)
            if l == 1:
                act.wait_ge(S["x_done"], 4)
                act.dma_start(o["y_prompt"][0].rearrange("(t p) d -> p t d", p=P), x[:, 0:2, :]).then_inc(S["stored"], 16)
                act.dma_start(o["y_sample"].rearrange("b t d -> (b t) d"), x[0:64, 2, :]).then_inc(S["stored"], 16)
                act.wait_ge(S["kv_out"], 64)

        @block.scalar
        def _(act):
            act.dma_start(x[:, 0:2, :], a["x_prompt"][0].rearrange("(t p) d -> p t d", p=P)).then_inc(S["x_in"], 16)
            act.dma_start(x[0:64, 2, :], a["x_sample"].rearrange("b t d -> (b t) d")).then_inc(S["x_in"], 16)
            act.dma_start(gen[:, :], a["gen"]).then_inc(S["x_in"], 16)
            act.dma_start(cwin[0:CONV_W, :], a["conv_w"][0]).then_inc(S["x_in"], 16)
            act.dma_start(cwin[CONV_W:CONV_W + 1, :], a["conv_b"]).then_inc(S["x_in"], 16)
            for i in range(2):
                act.dma_start(stin[0:120, i, :], a["state_conv"][0, 4 * i:4 * i + 4].rearrange("b w c -> (b w) c")).then_inc(S["x_in"], 16)
            act.dma_start(A["tba"], a["tba"]).then_inc(S["tba_in"], 16)
            act.dma_start(lam_in, a["lambda_a"][0].partition_broadcast(P)).then_inc(S["lam_in"], 16)
            act.dma_start(A["subln"], a["subln_a"][0].partition_broadcast(P)).then_inc(S["lam_in"], 16)
            act.dma_start(wr[:, :, :], a["w_router"].rearrange("(p k) e -> p k e", k=KD)).then_inc(S["tables_in"], 16)
            act.dma_start(rbias[:, :], a["b_router"].partition_broadcast(P)).then_inc(S["tables_in"], 16)
            act.dma_start(entry[:, :, :, :].rearrange("p t c w -> p (t c w)"), a["entry"]).then_inc(S["tables_in"], 16)

            for i in range(2):
                await_full(act, ("st", i))
                act.activation(us[:, :, 4 * i:4 * i + 4, 0:HIST],
                               bank(("st", i))[:, 0:480].rearrange("p (c b w) -> p c b w", c=CC, b=4), ACT.Copy).then_inc(read(("st", i)), 1)
            for t in range(3):
                await_full(act, ("xT0", t, 0))
                act.activation(xT[:, 0:4, cols_a(t)], bank(("xT0", t, 0))[:, 0:4 * SZ[t]].rearrange("p (k t) -> p k t", k=4),
                               ACT.Copy).then_inc(read(("xT0", t, 0)), 1)
            act.wait_ge(S["lam_sums"], 1)
            act.activation(lam2, rr, ACT.Exp).then_inc(S["lam_exp"], 1)
            for c in range(CC):
                await_full(act, ("g", c))
                if c >= 2:
                    act.wait_ge(S["u_set"], 2 * (c - 1))
                act.activation(sig[:, c % 2, :], bank(("g", c))[:, 0:TOK], ACT.Sigmoid).then_inc(read(("g", c)), 1)
            for n in range(3):
                for t in range(3):
                    await_full(act, ("qkv", n, t))
                    act.activation(qkv[0:SZ[t], t, n * 512:n * 512 + 512], bank(("qkv", n, t))[0:SZ[t], :], ACT.Copy).then_inc(read(("qkv", n, t)), 1)
            for n, dst in enumerate((qT, kT)):
                for t in range(3):
                    await_full(act, ("qkT", n, t))
                    act.activation(dst[:, :, cols_a(t)], bank(("qkT", n, t))[:, 0:4 * SZ[t]].rearrange("p (k t) -> p k t", k=4),
                                   ACT.Copy).then_inc(read(("qkT", n, t)), 1)
            for i, r in enumerate((HIST, 64)):
                await_full(act, ("uo", i))
                act.activation(uo[0:r, i, :], bank(("uo", i))[0:r, :], ACT.Copy).then_inc(read(("uo", i)), 1)
                await_read(act, ("uo", i))
            act.dma_start(o["conv_prompt"][0, 0], uo[0:HIST, 0, :]).then_inc(S["u_out"], 16)
            for b in range(DEC_B):
                act.dma_start(o["conv_sample"][0, b, HIST - DEC_T:HIST, :], uo[8 * b:8 * b + 8, 1, :]).then_inc(S["u_out"], 16)
            act.wait_ge(S["conv_done"], 1)
            for i in range(2):
                await_read(act, ("uo", i))
                await_full(act, ("cvt", 2))
            act.dma_start(A["clg"][:, 0:512], a["conv_ln_g"][0].partition_broadcast(P)).then_inc(S["clg_in"], 16)
            act.dma_start(A["clg"][:, 512:1024], a["conv_ln_b"][0].partition_broadcast(P)).then_inc(S["clg_in"], 16)
            act.wait_ge(S["cn_var"], 3)
            act.activation(cstd, cvar[:, :, 1], ACT.Sqrt, bias=epsc[:, 0:1]).then_inc(S["cn_std"], 1)
            for t in range(3):
                act.wait_ge(S["cn_pre"], t + 1)
                act.activation(qkv[0:SZ[t], t, 0:512], qkv[0:SZ[t], t, 0:512], ACT.Silu).then_inc(S["cn_post"], 1)
            for it in range(9):
                g = it // 2
                if it < 8:
                    if it == 0:
                        act.wait_ge(S["u_out"], 16 * 9)
                    n = (it // 4 + 1) * P
                    act.wait_ge(S["S_bias"], it + 1)
                    if it >= 2:
                        act.wait_ge(S["w_done"], it - 1)
                    for m in range(2):
                        act.activation(ebuf[:, it % 2, m, 0:n], bank(("S", it, m))[:, 0:n], ACT.Exp, bias=nb[:, m:m + 1],
                                       scale=DQK ** -0.5, accum_out=sums[:, it % 2, m:m + 1]).then_inc(read(("S", it, m)), 1)
                    if it % 2 == 0:
                        for i in range(4):
                            await_full(act, ("kpT", g, i))
                            act.activation(kpT[:, i // 2, :, (i % 2) * P:(i % 2) * P + P],
                                           bank(("kpT", g, i)).rearrange("p (h t) -> p h t", h=H), ACT.Copy).then_inc(read(("kpT", g, i)), 1)
                        act.wait_ge(S["SS_bias"], g + 1)
                        act.activation(es, bank(("SS", g))[:, 0:TOK], ACT.Exp, bias=snb, scale=DQK ** -0.5,
                                       accum_out=ssum).then_inc(read(("SS", g)), 1)
                    else:
                        await_full(act, ("wTs", g))
                        act.activation(wTs[:, 0:2, :], bank(("wTs", g))[:, 0:128].rearrange("p (k c) -> p k c", k=2), ACT.Copy)
                        act.activation(wTs[0:64, 2, :], bank(("wTs", g))[0:64, 128:192], ACT.Copy).then_inc(read(("wTs", g)), 1)
                if it >= 1:
                    n = ((it - 1) // 4 + 1)
                    await_full(act, ("wT", it - 1))
                    act.activation(wT[:, 0:n, :], bank(("wT", it - 1))[:, 0:n * P].rearrange("p (k q) -> p k q", k=n), ACT.Copy).then_inc(read(("wT", it - 1)), 1)
            for i in range(2):
                await_read(act, ("O", i))
                for h in range(H):
                    act.activation(wbuf[:, 0:P], qkv[:, i, 512 + h * P:512 + h * P + P], ACT.Square,
                                   accum_out=ss_att[:, 4 * i + h:4 * i + h + 1]).then_inc(S["att_ss"], 1)
                    act.wait_ge(S["att_ss"], 4 * i + h + 1)
            act.wait_ge(S["ao_read_k"], 1)
            act.activation(rs_att, ss_att, ACT.Sqrt, bias=epsc[:, 0:1], scale=1.0 / DV_A).then_inc(S["att_std"], 1)
            act.activation(rs_ao, ss_ao, ACT.Sqrt, bias=epsc[:, 0:1], scale=1.0 / DV_A).then_inc(S["att_std"], 1)
            for i in range(2):
                await_full(act, ("att", i))
                act.activation(mixT[:, 0:4, cols_a(i)], bank(("att", i)).rearrange("p (h t) -> p h t", h=H), ACT.Copy).then_inc(read(("att", i)), 1)
                await_full(act, ("aoT", i))
                for h in range(H):
                    src = bank(("aoT", i)).rearrange("p (b h r) -> p b h r", b=4, h=H)[:, :, h, 0:8]
                    ins = act.activation(mixT[:, h, 2 * P + 32 * i:2 * P + 32 * i + 32].rearrange("p (b q) -> p b q", b=4), src, ACT.Copy)
                ins.then_inc(read(("aoT", i)), 1)
            for t in range(3):
                await_full(act, ("cT", t))
                act.activation(mixT[:, 4:8, cols_a(t)], bank(("cT", t))[:, 0:4 * SZ[t]].rearrange("p (k t) -> p k t", k=4), ACT.Copy).then_inc(read(("cT", t)), 1)
            norm_act(act, 0, A["lngb"], "vp")
            experts_act(act, 0)

            act.wait_ge(S["x_done"], 2)
            act.dma_start(C["tbc"], a["tbc"]).then_inc(S["tbc_in"], 16)
            for t in range(3):
                await_full(act, ("xT1", t, 0))
                act.activation(xT[:, 0:4, cols_a(t)], bank(("xT1", t, 0))[:, 0:4 * SZ[t]].rearrange("p (k t) -> p k t", k=4),
                               ACT.Copy).then_inc(read(("xT1", t, 0)), 1)
            act.wait_ge(S["tbc_in"], 16)
            kdec = ccol("kdec").rearrange("p (t h) -> p t h", t=3)

            def swish_gate(h, c):
                await_full(act, ("gg", h, c))
                act.activation(gT[:, 4 * h + c, :], bank(("gg", h, c))[:, 0:TOK], ACT.Silu).then_inc(read(("gg", h, c)), 1)

            for h in range(H):
                for t in range(3):
                    await_full(act, ("v", h, t))
                    act.activation(vh[0:SZ[t], t, :], bank(("v", h, t))[0:SZ[t], :], ACT.Copy).then_inc(read(("v", h, t)), 1)
                swish_gate(h, 0)
                await_full(act, ("kd", h, 0))
                for t in range(2):
                    ins = act.activation(kd[:, t, :], bank(("kd", h, 0))[:, t * 256:t * 256 + 256], ACT.Copy, scale=kdec[:, t, h:h + 1])
                ins.then_inc(read(("kd", h, 0)), 1)
                await_full(act, ("kd", h, 1))
                act.activation(kd[0:64, 2, :], bank(("kd", h, 1))[0:64, 0:256], ACT.Copy, scale=kdec[0:64, 2, h:h + 1]).then_inc(read(("kd", h, 1)), 1)
                for c in range(1, 4):
                    swish_gate(h, c)
                act.wait_ge(S["on_var"], 2 * h + 1)
                act.activation(ostd[:, 0:2], ovar[:, 0:2, 1], ACT.Sqrt, bias=epsc[:, 0:1]).then_inc(S["on_std"], 1)
                act.wait_ge(S["on_var"], 2 * h + 2)
                act.activation(ostd[:, 2:4], ovar[:, 2:4, 1], ACT.Sqrt, bias=epsc[:, 0:1]).then_inc(S["on_std"], 1)
            norm_act(act, 2, C["lngb"], None)
            experts_act(act, 1)

        def trunk_norm(dve, link, k, lngb):
            for t in range(3):
                z = SZ[t]
                dve.bn_stats(stat[0:z, t, 0, :], x[0:z, t, 0:512])
                link(dve.bn_stats(stat[0:z, t, 1, :], x[0:z, t, 512:1024]))
                dve.bn_aggr(mv[0:z, t, :], stat[0:z, t, :, :].rearrange("p i s -> p (i s)")).then_inc(S["ln_var"], 1)
            dve.wait_ge(S["ln_std"], k + 1)
            link(dve.reciprocal(rstd[:, :, 0], rstd[:, :, 0]))
            dve.wait_ge(S["ln_in"], 32 * (k + 1))
            for t in range(3):
                z = SZ[t]
                link(dve.tensor_scalar(x[0:z, t, :], x[0:z, t, :], mv[0:z, t, 0:1], rstd[0:z, t, :], ALU.subtract, ALU.mult))
                link(dve.tensor_tensor(x[0:z, t, :], x[0:z, t, :], lngb[0:z, 0:D], ALU.mult))
                link(dve.tensor_tensor(x[0:z, t, :], x[0:z, t, :], lngb[0:z, D:2 * D], ALU.add))
            dve.sem_inc(S["x_done"], 1)

        def residual(dve, link, name, k, lngb):
            for n in range(2):
                for t in range(3):
                    z = SZ[t]
                    j = name + (n, t)
                    await_full(dve, j)
                    xs = x[0:z, t, n * 512:n * 512 + 512]
                    dve.scalar_tensor_tensor(xs, xs, ALPHA, bank(j)[0:z, :], ALU.mult, ALU.add).then_inc(read(j), 1)
                    await_read(dve, j)
            trunk_norm(dve, link, k, lngb)

        def experts_dve(dve, link, l):
            Q = L[l]
            for t in range(3):
                await_full(dve, ("xTm", l, t, 1))
                dve.tensor_copy(xT[:, 4:8, cols_a(t)], bank(("xTm", l, t, 1))[:, 0:4 * SZ[t]].rearrange("p (k t) -> p k t", k=4)).then_inc(read(("xTm", l, t, 1)), 1)
            await_full(dve, ("lg", l))
            dve.tensor_copy(lgT[0:N_EXP, :], bank(("lg", l))[0:N_EXP, 0:TOK]).then_inc(read(("lg", l)), 1)
            T3, T4 = [3, N_EXP], [3, N_GRP]
            lg, ex, probs, sel, sel2, oh1, sel3, oh2, both, w1, rank, t9 = (rt[:, i, :, :] for i in range(12))

            def col(i):
                return r1[:, i, :]

            def wide(ap, n=N_EXP):
                return ap.unsqueeze(2).broadcast_to([P, 3, n])

            await_full(dve, ("lgt", l))
            lb = bank(("lgt", l))
            dve.tensor_copy(lg[:, 0:2, :], lb[:, 0:32].rearrange("p (t e) -> p t e", t=2))
            dve.tensor_copy(lg[0:64, 2, :], lb[0:64, 32:48]).then_inc(read(("lgt", l)), 1)
            await_read(dve, ("lgt", l))
            link(dve.tensor_reduce(col(0), lg, X, ALU.max))
            dve.tensor_tensor(lg, lg, wide(col(0)), ALU.subtract).then_inc(S["lgs_ready"], 1)
            dve.wait_ge(S["lg_exp"], l + 1)
            link(dve.tensor_reduce(col(1), ex, X, ALU.add))
            link(dve.reciprocal(col(1), col(1)))
            link(dve.tensor_tensor(probs, ex, wide(col(1)), ALU.mult))
            dve.wait_ge(S["tables_in"], 48)
            link(dve.tensor_tensor(sel, probs, rbias[:, :].unsqueeze(1).broadcast_to([P] + T3), ALU.add))
            g4 = sel.rearrange("p t (g j) -> p t g j", j=PER_GRP)
            m1, n1, m2, n2, top, mm, nn, sec, gs, eq, oh, pen = (rs[:, i, :, :] for i in range(12))
            dve.tensor_tensor(m1, g4[:, :, :, 0], g4[:, :, :, 1], ALU.max)
            dve.tensor_tensor(n1, g4[:, :, :, 0], g4[:, :, :, 1], ALU.min)
            dve.tensor_tensor(m2, g4[:, :, :, 2], g4[:, :, :, 3], ALU.max)
            link(dve.tensor_tensor(n2, g4[:, :, :, 2], g4[:, :, :, 3], ALU.min))
            dve.tensor_tensor(top, m1, m2, ALU.max)
            dve.tensor_tensor(mm, m1, m2, ALU.min)
            link(dve.tensor_tensor(nn, n1, n2, ALU.max))
            link(dve.tensor_tensor(sec, mm, nn, ALU.max))
            link(dve.tensor_tensor(gs, top, sec, ALU.add))
            gidx = gcol("gidx").rearrange("p (t g) -> p t g", t=3)
            eidx = gcol("eidx").rearrange("p (t e) -> p t e", t=3)
            link(dve.tensor_reduce(col(2), gs, X, ALU.max))
            link(dve.tensor_tensor(eq, gs, wide(col(2), N_GRP), ALU.is_equal))
            link(dve.tensor_tensor(eq, eq, gidx, ALU.mult))
            link(dve.tensor_reduce(col(3), eq, X, ALU.min))
            link(dve.tensor_tensor(oh, gidx, wide(col(3), N_GRP), ALU.is_equal))
            link(dve.tensor_scalar(pen, oh, 1.0, -NEG, ALU.subtract, ALU.mult))
            s2 = sel2.rearrange("p t (g j) -> p t g j", j=PER_GRP)
            link(dve.tensor_tensor(s2, g4, pen.unsqueeze(3).broadcast_to([P, 3, N_GRP, PER_GRP]), ALU.add))

            def best(src, dst, c):
                link(dve.tensor_reduce(col(c), src, X, ALU.max))
                link(dve.tensor_tensor(t9, src, wide(col(c)), ALU.is_equal))
                link(dve.tensor_tensor(t9, t9, eidx, ALU.mult))
                link(dve.tensor_reduce(col(c), t9, X, ALU.min))
                link(dve.tensor_tensor(dst, eidx, wide(col(c)), ALU.is_equal))

            best(sel2, oh1, 4)
            link(dve.scalar_tensor_tensor(sel3, oh1, 3 * NEG, sel2, ALU.mult, ALU.add))
            best(sel3, oh2, 5)
            dve.tensor_tensor(both, oh1, oh2, ALU.add).then_inc(S["mask_ready"], 1)
            for c, hot in ((6, oh1), (7, oh2)):
                link(dve.tensor_tensor(w1, hot, probs, ALU.mult))
                link(dve.tensor_reduce(col(c), w1, X, ALU.add))
            link(dve.tensor_tensor(col(8), col(6), col(7), ALU.add))
            link(dve.reciprocal(col(8), col(8)))
            if l:
                dve.wait_ge(S["rows_in"], 96)
            ef = entry[:, :, :, :].bitcast(F32)
            for c in range(2):
                dve.tensor_tensor(ef[:, :, c, 2], col(6 + c), col(8), ALU.mult).then_inc(S["rot_step"], 1)
            await_full(dve, ("rank", l))
            rb = bank(("rank", l))
            ecol = gcol("ecol")
            dve.scalar_tensor_tensor(rank[:, 0:2, :], rb[:, 0:32].rearrange("p (t e) -> p t e", t=2), float(N_EXP),
                                     ecol.unsqueeze(1).broadcast_to([P, 2, N_EXP]), ALU.mult, ALU.add)
            dve.scalar_tensor_tensor(rank[0:64, 2, :], rb[0:64, 32:48], float(N_EXP), ecol[0:64, :], ALU.mult, ALU.add)
            link(dve.tensor_reduce(r1[:, 11, 0:1], rb[:, 48:64], X, ALU.max))
            dve.sem_inc(read(("rank", l)), 1)
            for c, hot in ((9, oh1), (10, oh2)):
                link(dve.tensor_tensor(w1, hot, rank, ALU.mult))
                link(dve.tensor_reduce(col(c), w1, X, ALU.add))
            for c in range(2):
                dve.tensor_copy(slot_i[:, :, c], col(9 + c)).then_inc(S["rot_step"], 1)
            thr = gcol("thr")
            link(dve.tensor_scalar(w1[:, 0, 0:MAX_PASSES], thr, r1[:, 11, 0:1], None, ALU.is_lt))
            link(dve.tensor_reduce(r1[:, 11, 1:2], w1[:, 0, 0:MAX_PASSES], X, ALU.add))
            dve.tensor_copy(passes_i[:, :], r1[:, 11, 1:2]).then_inc(S["passes_ready"], 1)
            dve.wait_ge(S["rot_step"], 3 + 4 * (l + 1))
            dve.sem_inc(S["entries"], 1)

            def turn_rows(j, k):
                dve.wait_ge(Q["tr_full1"], k)
                dve.tensor_copy(xgT[:, j, 4:8, :], ps[:, 1, :].rearrange("p (k s) -> p k s", k=4)).then_inc(Q["tr_dve"], 1)

            def one_pass(n):
                turn_rows(0, n * N_EXP + 1)

                def expert(par, k, u, last=False):
                    dve.wait_ge(Q["u_full"], k)
                    dve.wait_ge(Q["silu_done"], k)
                    dve.tensor_tensor(hid.rearrange("p j s -> p (j s)"), sg, ps[:, 3, :], ALU.mult).then_inc(Q["hid_done"], 1)
                    if not last:
                        turn_rows(1 - par, k + 1)
                    dve.wait_ge(Q["y_full1"], k)
                    dve.wait_ge(slot_open[l][par], u)
                    dve.tensor_scalar(yb[:, par, 512:1024], ps[:, 5 + 2 * par, :], gate[:, par:par + 1], None, ALU.mult).then_inc(Q["yd_done"], 1)

                with dve.Fori(0, N_EXP // 2 - 1) as i:
                    for par in range(2):
                        expert(par, n * N_EXP + i * 2 + (par + 1), n * (N_EXP // 2) + i + 1)
                expert(0, n * N_EXP + (N_EXP - 1), n * (N_EXP // 2) + N_EXP // 2)
                expert(1, n * N_EXP + N_EXP, n * (N_EXP // 2) + N_EXP // 2, last=True)

            over_passes(l, dve, one_pass)
            dve.wait_ge(S["yy_in"], 64 * (l + 1))
            for t in range(3):
                z = SZ[t]
                link(dve.scalar_tensor_tensor(x[0:z, t, :], x[0:z, t, :], ALPHA, yy[0:z, 0, t, :], ALU.mult, ALU.add))
                link(dve.tensor_tensor(x[0:z, t, :], x[0:z, t, :], yy[0:z, 1, t, :], ALU.add))
            trunk_norm(dve, link, 2 * l + 1, M["lngb"])

        @block.vector
        def _(dve):
            steps = [0]

            def link(ins):
                steps[0] += 1
                ins.then_inc(S["dve_step"], 1)
                dve.wait_ge(S["dve_step"], steps[0])

            def half_of_xT(name, dst):
                for t in range(3):
                    await_full(dve, name + (t, 1))
                    dve.tensor_copy(dst[:, 4:8, cols_a(t)], bank(name + (t, 1))[:, 0:4 * SZ[t]].rearrange("p (k t) -> p k t", k=4)).then_inc(read(name + (t, 1)), 1)

            await_full(dve, ("cw",))
            dve.tensor_copy(cwT, bank(("cw",))[:, 0:128].rearrange("p (c j) -> p c j", c=CC)).then_inc(read(("cw",)), 1)
            half_of_xT(("xT0",), xT)
            dve.wait_ge(S["lam_in"], 32)
            dve.wait_ge(S["pads_zero"], 6)
            dve.tensor_scalar(A["subln"], A["subln"], 1.0 - LAM_INIT, None, ALU.mult)
            lp = lam_in.rearrange("p (i j) d -> p i j d", i=2)
            link(dve.tensor_tensor(lp[:, :, 0, :], lp[:, :, 0, :], lp[:, :, 1, :], ALU.mult))
            dve.tensor_reduce(rr, lp[:, :, 0, :], X, ALU.add).then_inc(S["lam_sums"], 1)
            dve.wait_ge(S["lam_exp"], 1)
            link(dve.tensor_tensor(neglam, lam2[:, 1:2], lam2[:, 0:1], ALU.subtract))
            link(dve.tensor_scalar(neglam, neglam, -LAM_INIT, None, ALU.add))
            dve.wait_ge(S["tba_in"], 16)
            sgn = acol("sgn")
            link(dve.scalar_tensor_tensor(lamrow, sgn[:, 1:2], neglam, sgn[:, 0:1], ALU.mult, ALU.add))

            for c in range(CC):
                await_full(dve, ("a", c))
                await_read(dve, ("g", c))
                ab = bank(("a", c))
                dve.tensor_tensor(up[:, c, HIST:], ab[:, 0:N_PROMPT], sig[:, c % 2, 0:N_PROMPT], ALU.mult).then_inc(S["u_set"], 1)
                dve.tensor_tensor(us[:, c, :, HIST:], ab[:, N_PROMPT:TOK].rearrange("p (b t) -> p b t", b=DEC_B),
                                  sig[:, c % 2, N_PROMPT:].rearrange("p (b t) -> p b t", b=DEC_B), ALU.mult).then_inc(S["u_set"], 1)
                dve.wait_ge(S["u_set"], 2 * c + 2)
                dve.sem_inc(read(("a", c)), 1)
            dve.tensor_copy(un.rearrange("p c (b t) -> p c b t", b=DEC_B), us[:, :, :, HIST:]).then_inc(S["u_set"], 1)
            await_read(dve, ("cw",))
            for i in range(2):
                await_read(dve, ("st", i))
            n = 0
            for j in range(CONV_W):
                for c in range(CC):
                    for ext, out in ((up[:, c, j:j + N_PROMPT], acc[:, c, 0:N_PROMPT]),
                                     (us[:, c, :, j:j + DEC_T], acc[:, c, N_PROMPT:].rearrange("p (b t) -> p b t", b=DEC_B))):
                        if j == 0:
                            ins = dve.tensor_scalar(out, ext, cwT[:, c, 0:1], cwT[:, c, CONV_W:CONV_W + 1], ALU.mult, ALU.add)
                        else:
                            dve.wait_ge(S["conv_step"], n - 2 * CC + 1)
                            ins = dve.scalar_tensor_tensor(out, ext, cwT[:, c, j:j + 1], out, ALU.mult, ALU.add)
                        ins.then_inc(S["conv_step"], 1)
                        n += 1
            dve.wait_ge(S["conv_step"], n)
            dve.sem_inc(S["conv_done"], 1)
            for t in range(3):
                await_full(dve, ("cvt", t))
                z = SZ[t]
                link(dve.bn_stats(stat[0:z, t, 0, :], bank(("cvt", t))[0:z, :]))
                dve.bn_aggr(cvar[0:z, t, :], stat[0:z, t, 0, :]).then_inc(S["cn_var"], 1)
            dve.wait_ge(S["cn_std"], 1)
            link(dve.reciprocal(cstd, cstd))
            dve.wait_ge(S["clg_in"], 32)
            for t in range(3):
                z = SZ[t]
                c = qkv[0:z, t, 0:512]
                await_full(dve, ("qkT", 0, t))
                dve.tensor_scalar(c, bank(("cvt", t))[0:z, :], cvar[0:z, t, 0:1], cstd[0:z, t:t + 1], ALU.subtract, ALU.mult).then_inc(read(("cvt", t)), 1)
                await_read(dve, ("cvt", t))
                link(dve.tensor_tensor(c, c, A["clg"][0:z, 0:512], ALU.mult))
                dve.tensor_tensor(c, c, A["clg"][0:z, 512:1024], ALU.add).then_inc(S["cn_pre"], 1)
            for t in range(3):
                await_full(dve, ("qkv", 2, t))
            await_read(dve, ("qkT", 1, 2))
            for b in range(2):
                dve.tensor_copy(kpT[:, b, :, PAST:], kT[:, :, N_PROMPT:]).then_inc(S["kp_new"], 1)
            causal = acol("mask")
            smask = acol("smask").rearrange("p (g c) -> p g c", g=4)
            for it in range(9):
                g = it // 2
                if it >= 1:
                    s = it - 1
                    n = (s // 4 + 1) * P
                    await_read(dve, ("S", s, 0))
                    await_read(dve, ("S", s, 1))
                    link(dve.reciprocal(rr, sums[:, s % 2, :]))
                    link(dve.tensor_scalar(rr[:, 1:2], rr[:, 1:2], neglam, None, ALU.mult))
                    if s:
                        await_full(dve, ("wT", s - 1))
                    link(dve.tensor_scalar(wbuf[:, 0:n], ebuf[:, s % 2, 0, 0:n], rr[:, 0:1], None, ALU.mult))
                    dve.scalar_tensor_tensor(wbuf[:, 0:n], ebuf[:, s % 2, 1, 0:n], rr[:, 1:2], wbuf[:, 0:n], ALU.mult, ALU.add).then_inc(S["w_done"], 1)
                if it < 8:
                    i = it // 4
                    n = (i + 1) * P
                    await_full(dve, ("S", it, 0))
                    await_full(dve, ("S", it, 1))
                    diag = ps[:, 0:2, i * P:i * P + P]
                    link(dve.tensor_tensor(diag, diag, causal.unsqueeze(1).broadcast_to([P, 2, P]), ALU.add))
                    link(dve.tensor_reduce(mx, ps[:, 0:2, 0:n], X, ALU.max))
                    dve.tensor_scalar(nb, mx, -DQK ** -0.5, None, ALU.mult).then_inc(S["S_bias"], 1)
                    if it % 2 == 0:
                        if it % 4 == 0:
                            claim(dve, ("AO", it // 4))
                            dve.memset(ps[:, 7, :], 0.0).then_inc(S["ao_zero"], 1)
                        await_full(dve, ("SS", g))
                        sb_ = bank(("SS", g))
                        link(dve.tensor_tensor(sb_[:, PAST:TOK], sb_[:, PAST:TOK], smask[:, g, :], ALU.add))
                        link(dve.tensor_reduce(smx, sb_[:, 0:TOK], X, ALU.max))
                        dve.tensor_scalar(snb, smx, -DQK ** -0.5, None, ALU.mult).then_inc(S["SS_bias"], 1)
                    else:
                        await_read(dve, ("SS", g))
                        link(dve.reciprocal(srl, ssum))
                        link(dve.tensor_tensor(srl, srl, lamrow, ALU.mult))
                        dve.tensor_scalar(es, es, srl, None, ALU.mult).then_inc(S["ps_done"], 1)
                        if it % 4 == 3:
                            k = it // 4
                            await_full(dve, ("AO", k))
                            dve.tensor_copy(ao[:, 4 * k:4 * k + 4, :], bank(("AO", k)).rearrange("p (b e) -> p b e", b=4)).then_inc(read(("AO", k)), 1)
                if it in (4, 8):
                    i = it // 4 - 1
                    await_full(dve, ("O", i))
                    if i == 0:
                        dve.wait_ge(S["kv_out"], 64)
                    dve.tensor_copy(qkv[:, i, 512:1024], bank(("O", i))).then_inc(read(("O", i)), 1)
            await_read(dve, ("AO", 1))
            link(dve.tensor_tensor(ao2, ao, ao, ALU.mult))
            dve.tensor_reduce(ss_ao, ao2, X, ALU.add).then_inc(S["ao_read_k"], 1)
            g08 = A["subln"]
            dve.wait_ge(S["att_std"], 2)
            link(dve.reciprocal(rs_att, rs_att))
            link(dve.reciprocal(rs_ao, rs_ao))
            for i in range(2):
                v = qkv[:, i, 512:1024].rearrange("p (h e) -> p h e", h=H)
                link(dve.tensor_tensor(v, v, rs_att[:, 4 * i:4 * i + 4].unsqueeze(2).broadcast_to([P, H, P]), ALU.mult))
                dve.tensor_tensor(v, v, g08.unsqueeze(1).broadcast_to([P, H, P]), ALU.mult).then_inc(S["att_done"], 1)
            link(dve.tensor_tensor(ao, ao, rs_ao.unsqueeze(2).broadcast_to([P, DEC_B, P]), ALU.mult))
            dve.tensor_tensor(ao, ao, g08.unsqueeze(1).broadcast_to([P, DEC_B, P]), ALU.mult).then_inc(S["ao_done"], 1)
            residual(dve, link, ("out0",), 0, A["lngb"])
            experts_dve(dve, link, 0)

            half_of_xT(("xT1",), xT)
            dve.wait_ge(S["tbc_in"], 16)
            cosC, sinC = ccol("cos"), ccol("sin")
            dec = ccol("dec").rearrange("p (h i) -> p h i", h=H)
            sdec = ccol("sdec").rearrange("p (h i) -> p h i", h=H)
            qdec = ccol("qdec").rearrange("p (h i) -> p h i", h=H)

            def gate_out(h):
                for e in range(4):
                    await_full(dve, ("oT", h, e))
                    await_read(dve, ("gg", h, e))
                    b = bank(("oT", h, e))
                    g = gT[:, 4 * h + e, :]
                    dve.tensor_tensor(g[:, 0:N_PROMPT], g[:, 0:N_PROMPT], b[:, 0:N_PROMPT], ALU.mult)
                    gs = g[:, N_PROMPT:].rearrange("p (i q t) -> p i q t", i=2, q=4)
                    bs = b[:, 2 * P:].rearrange("p (i q r) -> p i q r", i=2, q=4)[:, :, :, 0:8]
                    dve.tensor_tensor(gs, gs, bs, ALU.mult).then_inc(read(("oT", h, e)), 1)

            for h in range(H):
                for i, (dst, s) in enumerate(((qr, 1.0), (kr, 1.0 / 16))):
                    if h or i:
                        dve.wait_ge(S["qk_rot"], 2 * (2 * h + i))
                    for c in range(2):
                        await_full(dve, ("qk", h, i, c))
                        b = bank(("qk", h, i, c))[:, 0:TOK]
                        dve.scalar_tensor_tensor(tmp[:, 2 * c, :], b, s, cosC, ALU.mult, ALU.mult)
                        link(dve.scalar_tensor_tensor(tmp[:, 2 * c + 1, :], b, s, sinC, ALU.mult, ALU.mult))
                        dve.sem_inc(read(("qk", h, i, c)), 1)
                    dve.tensor_tensor(dst[:, 0, :], tmp[:, 0, :], tmp[:, 3, :], ALU.subtract).then_inc(S["qk_rot"], 1)
                    dve.tensor_tensor(dst[:, 1, :], tmp[:, 2, :], tmp[:, 1, :], ALU.add).then_inc(S["qk_rot"], 1)
                dve.wait_ge(S["qk_rot"], 4 * h + 4)
                dve.tensor_tensor(qd, qr[:, :, P:], qdec[:, h, :].unsqueeze(1).broadcast_to([P, 2, TOK - P]), ALU.mult).then_inc(S["g_done"], 1)
                if h:
                    gate_out(h - 1)
                await_full(dve, ("sc", h))
                b = bank(("sc", h))
                dve.tensor_tensor(sc[:, 0:256].rearrange("p (c i) -> p c i", c=2), b[:, 0:256].rearrange("p (c i) -> p c i", c=2),
                                  dec[:, h, :].unsqueeze(1).broadcast_to([P, 2, P]), ALU.mult)
                dve.tensor_tensor(sc[0:64, 256:320], b[0:64, 256:320], sdec[0:64, h, :], ALU.mult).then_inc(read(("sc", h)), 1)
                if h:
                    dve.wait_ge(S["S2_out"], 16 * h)
                for c in range(2):
                    await_full(dve, ("S1", h, c))
                    dve.tensor_copy(St[:, c, :], bank(("S1", h, c))).then_inc(read(("S1", h, c)), 1)
                claim(dve, ("o", h, 2))
                claim(dve, ("o", h, 3))
                dve.memset(ps[:, 1:3, :], 0.0).then_inc(S["os_zero"], 1)

                def norm_o(lo, hi):
                    for t in range(lo, hi):
                        await_full(dve, ("o", h, t))
                        link(dve.bn_stats(ostat[:, t, :], bank(("o", h, t))))
                        link(dve.bn_aggr(ovar[:, t, :], ostat[:, t, :]))
                    dve.sem_inc(S["on_var"], 1)
                    dve.wait_ge(S["on_std"], 2 * h + 1 + lo // 2)
                    link(dve.reciprocal(ostd[:, lo:hi], ostd[:, lo:hi]))
                    for t in range(lo, hi):
                        dve.tensor_scalar(ob[:, t, :], bank(("o", h, t)), ovar[:, t, 0:1], ostd[:, t:t + 1], ALU.subtract, ALU.mult).then_inc(read(("o", h, t)), 1)

                norm_o(0, 2)
                for c in range(2):
                    await_full(dve, ("S2", h, c))
                    dve.scalar_tensor_tensor(St[:, c, :], St[:, c, :], float(np.exp(P * LOG_G[h])), bank(("S2", h, c)), ALU.mult, ALU.add).then_inc(read(("S2", h, c)), 1)
                    await_read(dve, ("S2", h, c))
                    dve.sem_inc(S["S2_done"], 1)
                for bq in range(DEC_B):
                    for c in range(2):
                        await_full(dve, ("sn", h, bq, c))
                        s = s0b[:, (h * DEC_B + bq) % 3, c, :]
                        dve.scalar_tensor_tensor(s, s, float(np.exp(DEC_T * LOG_G[h])), bank(("sn", h, bq, c)), ALU.mult, ALU.add).then_inc(read(("sn", h, bq, c)), 1)
                        await_read(dve, ("sn", h, bq, c))
                        dve.sem_inc(S["sn_done"], 1)
                norm_o(2, 4)
            gate_out(H - 1)
            residual(dve, link, ("out1",), 2, C["lngb"])
            experts_dve(dve, link, 1)

        def experts_pe(pe, l, turn_x):
            Q = L[l]
            turn_x(("xTm", l))
            for t in range(3):
                for i in range(2):
                    await_read(pe, ("xTm", l, t, i))
            pe.wait_ge(S["tables_in"], 48)
            claim(pe, ("lg", l))
            for k in range(KD):
                ins = pe.matmul(bank(("lg", l))[0:N_EXP, 0:TOK], wr[:, k, :], xT[:, k, :], start=k == 0, stop=k == KD - 1)
            ins.then_inc(full(("lg", l)), 1)
            await_read(pe, ("lg", l))
            claim(pe, ("lgt", l))
            for t in range(3):
                ins = pe.transpose(bank(("lgt", l))[0:SZ[t], t * 16:t * 16 + 16], lgT[0:N_EXP, cols_a(t)], ident[0:N_EXP, 0:N_EXP])
            ins.then_inc(full(("lgt", l)), 1)
            pe.wait_ge(S["mask_ready"], l + 1)
            both = rt[:, 8, :, :]
            claim(pe, ("rank", l))
            rb = bank(("rank", l))
            for t in range(3):
                for s in range(t + 1):
                    z = SZ[s]
                    pe.matmul(rb[0:SZ[t], t * 16:t * 16 + 16], (ones if s < t else before)[0:z, 0:SZ[t]], both[0:z, s, :], start=s == 0, stop=s == t)
            for s in range(3):
                ins = pe.matmul(rb[:, 48:64], ones[0:SZ[s], :], both[0:SZ[s], s, :], start=s == 0, stop=s == 2)
            ins.then_inc(full(("rank", l)), 1)
            for b in range(8):
                pe.wait_ge(bank_read[b], turns_before_experts[l][b])

            def turn_rows(par, k, u):
                pe.wait_ge(xg_in[l][par], u * 16)
                xv = xg[:, par, :].rearrange("p (q k) -> p k q", k=KD)
                for i in range(2):
                    for c in range(4):
                        ins = pe.transpose(ps[:, i, c * P:c * P + P], xv[:, 4 * i + c, :], ident)
                    ins.then_inc(Q[f"tr_full{i}"], 1)

            def one_pass(n):
                turn_rows(0, n * N_EXP + 1, n * (N_EXP // 2) + 1)

                def expert(par, k, u, u_next, last=False):
                    pe.wait_ge(Q["tr_act"], k)
                    pe.wait_ge(Q["tr_dve"], k)
                    for m in range(2):
                        s = 3 * par + m
                        w = ring[:, s, :].rearrange("p (k f) -> p k f", k=KD)
                        pe.wait_ge(e_landed[l][s], u * 16)
                        for f in range(KF):
                            for c in range(KD):
                                ins = pe.matmul(ps[:, 2 + m, f * P:f * P + P], w[:, c, f * P:f * P + P], xgT[:, par, c, :], start=c == 0, stop=c == KD - 1)
                        ins.then_inc(Q[("g_full", "u_full")[m]], 1)
                    if not last:
                        turn_rows(1 - par, k + 1, u_next)
                    s = 3 * par + 2
                    w = ring[:, s, :].rearrange("p (j d) -> p j d", j=KF)
                    pe.wait_ge(e_landed[l][s], u * 16)
                    pe.wait_ge(Q["hid_done"], k)
                    for i in range(2):
                        for c in range(KF):
                            ins = pe.matmul(ps[:, 4 + 2 * par + i, :], hid[:, c, :], w[:, c, i * 512:i * 512 + 512], start=c == 0, stop=c == KF - 1)
                        ins.then_inc(Q[f"y_full{i}"], 1)

                with pe.Fori(0, N_EXP // 2 - 1) as i:
                    for par in range(2):
                        expert(par, n * N_EXP + i * 2 + (par + 1), n * (N_EXP // 2) + i + 1, n * (N_EXP // 2) + i + 1 + par)
                u = n * (N_EXP // 2) + N_EXP // 2
                expert(0, n * N_EXP + (N_EXP - 1), u, u)
                expert(1, n * N_EXP + N_EXP, u, u, last=True)

            over_passes(l, pe, one_pass)
            if l == 0:
                n = pass_count(pe)
                pe.wait_ge(Q["ya_done"], n * N_EXP)
                pe.wait_ge(Q["yd_done"], n * N_EXP)

        @block.tensor
        def _(pe):
            def turn_x(name):
                for t in range(3):
                    xv = x[0:SZ[t], t, :].rearrange("p (q k) -> p k q", k=KD)
                    for i in range(2):
                        j = name + (t, i)
                        claim(pe, j)
                        for c in range(4):
                            ins = pe.transpose(bank(j)[:, c * SZ[t]:(c + 1) * SZ[t]], xv[:, 4 * i + c, :], ident[0:SZ[t], 0:SZ[t]])
                        ins.then_inc(full(j), 1)

            def feature_major(j, w, k0):
                claim(pe, j)
                for k in range(KD):
                    ins = pe.matmul(bank(j)[:, 0:TOK], w[:, k, k0:k0 + P], xT[:, k, :], start=k == 0, stop=k == KD - 1)
                ins.then_inc(full(j), 1)
                return ins

            pe.wait_ge(S["x_in"], 16 * 7)
            for c in range(CC):
                ins = pe.transpose(bank(("cw",))[:, c * 32:c * 32 + 32], cwin[0:32, c * P:c * P + P], ident[0:32, 0:32])
            ins.then_inc(full(("cw",)), 1)
            for i in range(2):
                for c in range(CC):
                    ins = pe.transpose(bank(("st", i))[:, c * 120:c * 120 + 120], stin[0:120, i, c * P:c * P + P], ident[0:120, 0:120])
                ins.then_inc(full(("st", i)), 1)
            turn_x(("xT0",))
            for t in range(3):
                for i in range(2):
                    await_read(pe, ("xT0", t, i))
            for n, name in enumerate(("a", "g")):
                w_arrived(pe, 0, n)
                for c in range(CC):
                    ins = feature_major((name, c), w_block(0, n), c * P)
            for n in range(3):
                w_arrived(pe, 0, 2 + n)
                w = w_block(0, 2 + n)
                for t in range(3):
                    j = ("qkv", n, t)
                    claim(pe, j)
                    for k in range(KD):
                        ins = pe.matmul(bank(j)[0:SZ[t], :], xT[:, k, cols_a(t)], w[:, k, :], start=k == 0, stop=k == KD - 1)
                    ins.then_inc(full(j), 1)
            for n in range(2):
                for t in range(3):
                    z = SZ[t]
                    pe.wait_ge(S["rot_step"], t + 1)
                    j = ("qkT", n, t)
                    claim(pe, j)
                    for h in range(H):
                        ins = pe.transpose(bank(j)[:, h * z:h * z + z], qkv[0:z, t, n * 512 + h * P:n * 512 + h * P + P], ident[0:z, 0:z])
                    ins.then_inc(full(j), 1)
            pe.wait_ge(S["u_set"], 2 * CC + 1)
            for i in range(2):
                j = ("uo", i)
                claim(pe, j)
                for c in range(CC):
                    if i == 0:
                        ins = pe.transpose(bank(j)[0:HIST, c * P:c * P + P], up[:, c, N_PROMPT:N_PROMPT + HIST], ident)
                    else:
                        ins = pe.transpose(bank(j)[0:64, c * P:c * P + P], un[:, c, :], ident)
                ins.then_inc(full(j), 1)
            pe.wait_ge(S["conv_done"], 1)
            for t in range(3):
                j = ("cvt", t)
                claim(pe, j)
                for c in range(CC):
                    ins = pe.transpose(bank(j)[0:SZ[t], c * P:c * P + P], acc[:, c, cols_a(t)], ident)
                ins.then_inc(full(j), 1)
            for t in range(3):
                for n in range(2):
                    await_read(pe, ("qkT", n, t))
            pair = acol("pair")
            for it in range(9):
                g = it // 2
                if it < 8:
                    i, h = it // 4, it % 4
                    n = (i + 1) * P
                    for m in range(2):
                        hp = slice(64 * m, 64 * m + 64)
                        claim(pe, ("S", it, m))
                        pe.matmul(bank(("S", it, m))[:, 0:n], qT[hp, h, cols_a(i)], kT[hp, h, 0:n], start=True, stop=True).then_inc(full(("S", it, m)), 1)
                    if it % 2 == 0:
                        pe.wait_ge(S["kp_in"], 64 * (g + 1))
                        for j4 in range(4):
                            j = ("kpT", g, j4)
                            claim(pe, j)
                            for hh in range(H):
                                ins = pe.transpose(bank(j)[:, hh * P:hh * P + P], kp[:, j4 // 2, j4 % 2, hh * P:hh * P + P], ident)
                            ins.then_inc(full(j), 1)
                        for j4 in range(4):
                            await_read(pe, ("kpT", g, j4))
                        pe.wait_ge(S["kp_new"], 2)
                        pe.wait_ge(S["QB_set"], 8 * (g + 1))
                        j = ("SS", g)
                        claim(pe, j)
                        for b in range(2):
                            for hh in range(H):
                                ins = pe.matmul(bank(j)[64 * b:64 * b + 64, 0:TOK], QB[:, b, hh, :], kpT[:, b, hh, :], start=hh == 0, stop=hh == H - 1)
                        ins.then_inc(full(j), 1)
                    else:
                        j = ("wTs", g)
                        pe.wait_ge(S["ps_done"], g + 1)
                        claim(pe, j)
                        for pg in range(2):
                            pe.matmul(bank(j)[:, pg * 64:pg * 64 + 64], es[:, pg * P:pg * P + P], pair, start=True, stop=True)
                        pe.matmul(bank(j)[0:64, 128:192], es[:, PAST:TOK], pair, start=True, stop=True).then_inc(full(j), 1)
                        await_read(pe, j)
                        pe.wait_ge(S["vp_in"], 64 * (g + 1))
                        j = ("AO", it // 4)
                        pe.wait_ge(S["ao_zero"], it // 4 + 1)
                        for b in range(2):
                            col = (2 * g + b) % 4 * P
                            for hh in range(H):
                                out = bank(j)[32 * hh:32 * hh + 8, col:col + P]
                                c0 = b * 32 + hh * 8
                                for pg in range(2):
                                    pe.matmul(out, wTs[:, pg, c0:c0 + 8], vp[:, b, pg, hh * P:hh * P + P], start=pg == 0, stop=False)
                                ins = pe.matmul(out, wTs[0:64, 2, c0:c0 + 8], qkv[0:64, 2, 1024 + hh * P:1024 + hh * P + P], start=False, stop=True)
                        if it % 4 == 3:
                            ins.then_inc(full(j), 1)
                if it >= 1:
                    s = it - 1
                    i, h = s // 4, s % 4
                    j = ("wT", s)
                    pe.wait_ge(S["w_done"], s + 1)
                    claim(pe, j)
                    for k in range(i + 1):
                        ins = pe.transpose(bank(j)[:, k * P:k * P + P], wbuf[:, k * P:k * P + P], ident)
                    ins.then_inc(full(j), 1)
                    await_read(pe, j)
                    j = ("O", i)
                    if h == 0:
                        claim(pe, j)
                    for k in range(i + 1):
                        ins = pe.matmul(bank(j)[:, h * P:h * P + P], wT[:, k, :], qkv[:, k, 1024 + h * P:1024 + h * P + P], start=k == 0, stop=k == i)
                    if h == 3:
                        ins.then_inc(full(j), 1)
            for i in range(2):
                pe.wait_ge(S["att_done"], i + 1)
                claim(pe, ("att", i))
                for h in range(H):
                    ins = pe.transpose(bank(("att", i))[:, h * P:h * P + P], qkv[:, i, 512 + h * P:512 + h * P + P], ident)
                ins.then_inc(full(("att", i)), 1)
                if i == 0:
                    pe.wait_ge(S["ao_done"], 1)
                claim(pe, ("aoT", i))
                for b in range(4):
                    ins = pe.transpose(bank(("aoT", i))[:, b * P:b * P + P], ao[:, 4 * i + b, :], ident)
                ins.then_inc(full(("aoT", i)), 1)
            pe.wait_ge(S["cn_post"], 3)
            for t in range(3):
                z = SZ[t]
                claim(pe, ("cT", t))
                for c in range(CC):
                    ins = pe.transpose(bank(("cT", t))[:, c * z:c * z + z], qkv[0:z, t, c * P:c * P + P], ident[0:z, 0:z])
                ins.then_inc(full(("cT", t)), 1)
            for i in range(2):
                await_read(pe, ("att", i))
                await_read(pe, ("aoT", i))
            for t in range(3):
                await_read(pe, ("cT", t))
            for n in range(2):
                w_arrived(pe, 0, 5 + n)
                w = w_block(0, 5 + n)
                for t in range(3):
                    j = ("out0", n, t)
                    claim(pe, j)
                    for k in range(KD):
                        ins = pe.matmul(bank(j)[0:SZ[t], :], mixT[:, k, cols_a(t)], w[:, k, :], start=k == 0, stop=k == KD - 1)
                    ins.then_inc(full(j), 1)
            pe.wait_ge(S["x_done"], 1)
            experts_pe(pe, 0, turn_x)

            pe.wait_ge(S["x_done"], 2)
            turn_x(("xT1",))
            for t in range(3):
                for i in range(2):
                    await_read(pe, ("xT1", t, i))

            def turn_out(h):
                for t in range(4):
                    await_read(pe, ("o", h, t))
                for e in range(4):
                    j = ("oT", h, e)
                    claim(pe, j)
                    for t in range(4):
                        ins = pe.transpose(bank(j)[:, t * P:t * P + P], ob[:, t, e * P:e * P + P], ident)
                    ins.then_inc(full(j), 1)

            for h in range(H):
                w_arrived(pe, 1, 3 * h)
                w = w_block(1, 3 * h)
                for i in range(2):
                    for c in range(2):
                        ins = feature_major(("qk", h, i, c), w, i * DK_C + c * P)
                w_arrived(pe, 1, 3 * h + 1)
                w = w_block(1, 3 * h + 1)
                for t in range(3):
                    j = ("v", h, t)
                    claim(pe, j)
                    for k in range(KD):
                        ins = pe.matmul(bank(j)[0:SZ[t], :], xT[:, k, cols_a(t)], w[:, k, :], start=k == 0, stop=k == KD - 1)
                    ins.then_inc(full(j), 1)
                if h:
                    turn_out(h - 1)
                w_arrived(pe, 1, 3 * h + 2)
                w = w_block(1, 3 * h + 2)
                pe.wait_ge(S["qk_rot"], 4 * h + 4)
                j = ("sc", h)
                claim(pe, j)
                for t in range(3):
                    for c in range(2):
                        ins = pe.matmul(bank(j)[0:SZ[t], cols_a(t)], kr[:, c, cols_a(t)], qr[:, c, cols_a(t)], start=c == 0, stop=c == 1)
                ins.then_inc(full(j), 1)
                feature_major(("gg", h, 0), w, 0)
                for i in range(2):
                    j = ("kd", h, i)
                    claim(pe, j)
                    for t in ((0, 1), (2,))[i]:
                        for c in range(2):
                            at = (t % 2) * 256 + c * P
                            ins = pe.transpose(bank(j)[0:SZ[t], at:at + P], kr[:, c, cols_a(t)], ident)
                    ins.then_inc(full(j), 1)
                feature_major(("gg", h, 1), w, P)
                for t in range(3):
                    await_read(pe, ("v", h, t))
                await_read(pe, ("sc", h))
                await_read(pe, ("kd", h, 0))
                for c in range(2):
                    j = ("S1", h, c)
                    claim(pe, j)
                    pe.matmul(bank(j), kd[:, 0, c * P:c * P + P], vh[:, 0, :], start=True, stop=True).then_inc(full(j), 1)
                j = ("o", h, 0)
                claim(pe, j)
                pe.matmul(bank(j), sc[:, 0:P], vh[:, 0, :], start=True, stop=True).then_inc(full(j), 1)
                feature_major(("gg", h, 2), w, 2 * P)
                j = ("o", h, 1)
                claim(pe, j)
                pe.matmul(bank(j), sc[:, P:2 * P], vh[:, 1, :], start=True, stop=False)
                pe.wait_ge(S["g_done"], h + 1)
                for c in range(2):
                    await_read(pe, ("S1", h, c))
                for c in range(2):
                    ins = pe.matmul(bank(j), qd[:, c, 0:P], St[:, c, :], start=False, stop=c == 1)
                ins.then_inc(full(j), 1)
                for c in range(2):
                    j = ("S2", h, c)
                    claim(pe, j)
                    pe.matmul(bank(j), kd[:, 1, c * P:c * P + P], vh[:, 1, :], start=True, stop=True).then_inc(full(j), 1)
                ins = feature_major(("gg", h, 3), w, 3 * P)
                pe.wait_ge(S["os_zero"], h + 1)
                pe.wait_ge(S["kdm_set"], DEC_B * (h + 1))
                for b in range(DEC_B):
                    n = h * DEC_B + b
                    pe.wait_ge(s0_in[n % 3], 16 * (n // 3 + 1))
                    j = ("o", h, 2 + b // 4)
                    out = bank(j)[32 * (b % 4):32 * (b % 4) + 8, :]
                    for c in range(2):
                        pe.matmul(out, qd[:, c, P + b * 8:P + b * 8 + 8], s0b[:, n % 3, c, :], start=c == 0, stop=False)
                    ins = pe.matmul(out, sc[0:64, 256 + b * 8:256 + b * 8 + 8], vh[0:64, 2, :], start=False, stop=True)
                    if b % 4 == 3:
                        ins.then_inc(full(j), 1)
                    for c in range(2):
                        j = ("sn", h, b, c)
                        claim(pe, j)
                        pe.matmul(bank(j), kdm[0:64, b, c * P:c * P + P], vh[0:64, 2, :], start=True, stop=True).then_inc(full(j), 1)
            turn_out(H - 1)
            for e in range(4):
                await_read(pe, ("oT", H - 1, e))
            for n in range(2):
                for r in range(2):
                    w_arrived(pe, 1, 12 + 2 * n + r)
                for t in range(3):
                    j = ("out1", n, t)
                    claim(pe, j)
                    for r in range(2):
                        w = w_block(1, 12 + 2 * n + r)
                        for k in range(KD):
                            ins = pe.matmul(bank(j)[0:SZ[t], :], gT[:, r * KD + k, cols_a(t)], w[:, k, :], start=r + k == 0, stop=r + k == KD)
                    ins.then_inc(full(j), 1)
            pe.wait_ge(S["x_done"], 3)
            experts_pe(pe, 1, turn_x)



_INS = ["x_prompt", "x_sample", "cache_k", "cache_v", "page_table", "state_conv", "state_ret", "w_in_a", "lambda_a",
        "subln_a", "conv_w", "conv_b", "conv_ln_g", "conv_ln_b", "w_out_a", "w_in_c", "w_out_c", "ln_g", "ln_b",
        "w_router", "b_router", "w_e_gate", "w_e_up", "w_e_down"]
_OUTS = [("y_prompt", (1, 256, 1024)), ("y_sample", (8, 8, 1024)), ("k_prompt", (1, 1, 256, 8, 64)),
         ("v_prompt", (1, 1, 256, 4, 128)), ("conv_prompt", (1, 1, 30, 512)), ("ret_prompt", (1, 1, 4, 256, 512)),
         ("k_sample", (1, 8, 8, 8, 64)), ("v_sample", (1, 8, 8, 4, 128)), ("conv_sample", (1, 8, 30, 512)),
         ("ret_sample", (1, 8, 4, 256, 512))]


def kernel(**inputs):
    import numpy as _np
    import concourse.bacc as _bacc
    from concourse import mybir as _mybir
    from concourse.bass_utils import run_bass_kernel_spmd as _run

    nc = _bacc.Bacc("TRN2", target_bir_lowering=False, num_devices=1)
    data = {name: _np.ascontiguousarray(inputs[name]) for name in _INS}
    data.update(host_tables())
    arrays, a, o = {}, {}, {}
    for name, v in data.items():
        arrays[f"in_{name}_dram"] = v
        a[name] = nc.dram_tensor(f"in_{name}_dram", v.shape, _mybir.dt.from_np(v.dtype), kind="ExternalInput").ap()
    for name, shape in _OUTS:
        o[name] = nc.dram_tensor(f"out_{name}_dram", shape, _mybir.dt.float32, kind="ExternalOutput").ap()
    build(nc, a, o)
    r = _run(nc, [arrays], core_ids=[0])
    return tuple(r.results[0][f"out_{name}_dram"] for name, _ in _OUTS)
```

```python
import math
from contextlib import ExitStack

import numpy as np

import concourse.bass as bass
from concourse import mybir

F32 = mybir.dt.float32
I32 = mybir.dt.int32
ALU = mybir.AluOpType
ACT = mybir.ActivationFunctionType
X = mybir.AxisListType.X

P = 128
D = 1024
N_PROMPT = 256
DEC_B, DEC_T = 8, 8
N_SAMPLE = DEC_B * DEC_T
TOK = N_PROMPT + N_SAMPLE
SZ = [P, P, N_SAMPLE]
OFF = [0, P, 2 * P]
KD = D // P
PAST, PAGE = 256, 128
PAGES = PAST // PAGE
H = 4
DQK, DV_A = 64, 128
ATT_W = H * DV_A
CONV_CH, CONV_W = 512, 31
CC = CONV_CH // P
HIST = CONV_W - 1
DK_C, DV_C = 256, 512
N_EXP, N_GRP, PER_GRP = 16, 4, 4
D_FF = 512
KF = D_FF // P
ALPHA = float((2 * 2) ** 0.25)
EPS = 1e-5
CHUNK = 64
CUTS = TOK // CHUNK
MAX_PAIRS = ((2 * TOK + N_EXP * (CHUNK - 1)) // CHUNK + 1) // 2
MAX_CHUNKS = 2 * MAX_PAIRS
RING = 6
LAM_INIT = 0.8 - 0.6 * math.exp(-0.3 * 0)
NEG = -1e30

LOG_G = np.log1p(-np.exp2(-5.0 - np.arange(H, dtype=np.float64)))


def layout(*fields):
    at, out = 0, {}
    for name, width in fields:
        out[name] = (at, width)
        at += width
    return out, at


GEN, GEN_W = layout(("ident", P), ("before", P), ("ones", P), ("eidx", 3 * N_EXP), ("gidx", 3 * N_GRP),
                    ("cuts", CUTS))
PLN, PLN_W = layout(("earlier", N_EXP * N_EXP), ("seq", MAX_CHUNKS), ("pairs", MAX_PAIRS))
TBA, TBA_W = layout(("cos", 3 * 8), ("sin", 3 * 8), ("mask", P), ("smask", 4 * N_SAMPLE), ("pair", N_SAMPLE),
                    ("sgn", 2))
TBC, TBC_W = layout(("cos", TOK), ("sin", TOK), ("dec", H * P), ("sdec", H * N_SAMPLE), ("qdec", H * (TOK - P)),
                    ("kdec", 3 * H), ("own", DEC_B))


def host_tables():
    f = np.float32
    p = np.arange(P)
    gen = np.zeros((P, GEN_W), f)

    def put(t, lay, name, a):
        at, w = lay[name]
        t[:, at:at + w] = np.asarray(a, f).reshape(P, w)

    put(gen, GEN, "ident", np.eye(P))
    put(gen, GEN, "before", p[:, None] < p[None, :])
    put(gen, GEN, "ones", np.ones((P, P)))
    put(gen, GEN, "eidx", np.tile(np.arange(N_EXP) - 32.0, (P, 3)))
    put(gen, GEN, "gidx", np.tile(np.arange(N_GRP) - 8.0, (P, 3)))
    put(gen, GEN, "cuts", np.tile(np.arange(CUTS) * float(CHUNK), (P, 1)))
    pln = np.zeros((P, PLN_W), f)
    e = np.arange(N_EXP)
    put(pln, PLN, "earlier", np.tile((e[None, :] < e[:, None]).reshape(1, -1), (P, 1)))
    put(pln, PLN, "seq", np.tile(np.arange(MAX_CHUNKS), (P, 1)))
    put(pln, PLN, "pairs", np.tile(np.arange(MAX_PAIRS) * 2, (P, 1)))

    pos = np.concatenate([np.arange(N_PROMPT), np.tile(PAST + np.arange(DEC_T), DEC_B)]).astype(f)
    tba = np.zeros((P, TBA_W), f)
    inv = f(500000.0) ** (-np.arange(0, 16, 2, dtype=f) / f(16))
    ang = pos[:, None] * inv[None, :].astype(f)
    ca, sa = np.zeros((3 * P, 8), f), np.zeros((3 * P, 8), f)
    ca[:TOK], sa[:TOK] = np.cos(ang), np.sin(ang)
    put(tba, TBA, "cos", ca.reshape(3, P, 8).transpose(1, 0, 2))
    put(tba, TBA, "sin", sa.reshape(3, P, 8).transpose(1, 0, 2))
    put(tba, TBA, "mask", np.where(p[None, :] <= p[:, None], 0.0, NEG))
    b2, m, q = p // 64, (p // 8) % 8, p % 8
    cb, ct = np.arange(64) // 8, np.arange(64) % 8
    sm = np.stack([np.where((cb[None] == 2 * g + b2[:, None]) & (ct[None] <= q[:, None]), 0.0, NEG) for g in range(4)], 1)
    put(tba, TBA, "smask", sm)
    cols = np.arange(64)
    put(tba, TBA, "pair", (b2[:, None] == cols[None] // 32) & (m[:, None] // 2 == (cols[None] // 8) % 4)
        & (q[:, None] == cols[None] % 8))
    put(tba, TBA, "sgn", np.stack([m % 2 == 0, m % 2 == 1], 1))

    tbc = np.zeros((P, TBC_W), f)
    inv = f(10000.0) ** (-np.linspace(0.0, 1.0, DK_C // 2, dtype=f))
    ang = (pos[:, None] * inv[None, :].astype(f)).astype(f)
    put(tbc, TBC, "cos", np.cos(ang).T)
    put(tbc, TBC, "sin", np.sin(ang).T)
    d = p[None, :] - p[:, None]
    dec = np.stack([np.where(d >= 0, np.exp(np.maximum(d, 0) * LOG_G[h]), 0.0) for h in range(H)], 1)
    put(tbc, TBC, "dec", dec)
    i = np.arange(64)
    ds = i[None, :] % 8 - i[:, None] % 8
    same = i[None, :] // 8 == i[:, None] // 8
    sd = np.zeros((P, H, 64))
    sd[:64] = np.stack([np.where(same & (ds >= 0), np.exp(np.maximum(ds, 0) * LOG_G[h]), 0.0) for h in range(H)], 1)
    put(tbc, TBC, "sdec", sd)
    idx = np.concatenate([p, i % 8])
    put(tbc, TBC, "qdec", np.tile(np.stack([np.exp((idx + 1) * LOG_G[h]) for h in range(H)])[None], (P, 1, 1)))
    kd = np.zeros((P, 3, H))
    for h in range(H):
        kd[:, 0, h] = kd[:, 1, h] = np.exp((P - 1 - p) * LOG_G[h])
        kd[:64, 2, h] = np.exp((DEC_T - 1 - i % 8) * LOG_G[h])
    put(tbc, TBC, "kdec", kd)
    own = np.zeros((P, DEC_B))
    own[:64] = i[:, None] // 8 == np.arange(8)[None]
    put(tbc, TBC, "own", own)

    entry = np.zeros((P, 3, 2, 4), np.int32)
    tok = np.arange(3)[None, :, None] * P + p[:, None, None]
    entry[..., 0] = tok
    entry[..., 1] = np.arange(2)[None, None] * TOK + tok
    empty = np.zeros((P * MAX_PAIRS, 4), np.int32)
    empty[:, 1] = 1 << 20
    return {"gen": gen, "tba": tba, "tbc": tbc, "pln": pln, "entry": entry.reshape(P, 24), "empty": empty}


def build(nc, a, o):
    with ExitStack() as ctx:
        def sb(name, shape, dt=F32):
            return ctx.enter_context(nc.sbuf_tensor(name, [P] + shape, dt))

        def sem(name):
            return ctx.enter_context(nc.semaphore(name))

        x_rows = [nc.dram_tensor(f"x_rows{l}", (TOK, D), F32, kind="Internal").ap() for l in range(2)]
        y_rows = [nc.dram_tensor(f"y_rows{l}", (2 * TOK, D), F32, kind="Internal").ap() for l in range(2)]
        table = [nc.dram_tensor(f"table{l}", (P * MAX_PAIRS, 4), I32, kind="Internal").ap() for l in range(2)]

        ring = sb("ring", [RING, 4096])
        x = sb("x", [3, D])
        xT = sb("xT", [KD, TOK])
        gen = sb("gen_sb", [GEN_W])
        wr = sb("wr", [KD, N_EXP])
        rbias = sb("rbias", [N_EXP])
        entry = sb("entry_sb", [3, 2, 4], I32)
        stat = sb("stat", [3, 2, 6])
        mv = sb("mv", [3, 2])
        rstd = sb("rstd", [3, 1])
        epsc = sb("epsc", [1])
        rt = sb("rt", [12, 3, N_EXP])
        rs = sb("rs", [12, 3, N_GRP])
        r1 = sb("r1", [12, 3])
        slot_i = sb("slot_i", [3, 2], I32)
        pairs_i = sb("pairs_i", [2], I32)
        slot_pages = sb("slot_pages", [DEC_B * PAGES], I32)
        SCR = 21184
        scratch = sb("scratch", [SCR])
        ps = ctx.enter_context(nc.psum_tensor("ps", [P, 8, 512], F32))

        def carve(*fields):
            at, out = 0, {}
            for name, n, *start in fields:
                s = out[start[0]][1] + (start[1] if len(start) > 1 else 0) if start else at
                out[name] = (scratch[:, s:s + n], s)
                if not start:
                    at += n
            assert at <= SCR, at
            return {k: v[0] for k, v in out.items()}

        A = carve(("qkv", 3 * 1536), ("qT", H * TOK), ("kT", H * TOK), ("up", CC * (HIST + N_PROMPT)),
                  ("us", CC * DEC_B * (HIST + DEC_T)), ("acc", CC * TOK), ("sig", 2 * TOK),
                  ("kp", 2 * PAGES * 512), ("vp", 2 * PAGES * 512), ("QB", 2 * H * 64),
                  ("e", 2 * 512), ("w", 256), ("wT", 256), ("es", TOK), ("wTs", 192),
                  ("ao", DEC_B * DV_A), ("tba", TBA_W), ("subln", DV_A), ("cwT", CC * 32), ("small", 128),
                  ("lam", 4 * DQK),
                  ("mixT", KD * TOK, "up"), ("clg", 1024, "up"), ("ao2", 1024, "kp"), ("lngb", 2048, "vp"),
                  ("stin", 1024, "ao"), ("cwin", 512, "es"), ("uo", 1024, "e"))
        C = carve(("q", 2 * TOK), ("k", 2 * TOK), ("qd", 2 * (TOK - P)), ("v", 3 * DV_C), ("g", 16 * TOK),
                  ("kd", 3 * DK_C), ("kdm", DEC_B * DK_C), ("sc", 2 * P + 64), ("S", 2 * DV_C), ("o", 4 * DV_C),
                  ("s0", 3 * 2 * DV_C), ("tmp", 4 * TOK), ("tbc", TBC_W), ("small", 64),
                  ("lngb", 2048, "o"))
        M = carve(("xg", D), ("xgT", KD * P), ("sg", D_FF), ("hid", D_FF), ("hidT", 2 * KF * CHUNK), ("y", D),
                  ("tab", MAX_PAIRS * 4), ("pln", PLN_W), ("ptmp", N_EXP * N_EXP), ("ch", 3 * N_EXP), ("gidx", 1), ("sidx", 1), ("done", N_EXP),
                  ("evens", MAX_CHUNKS), ("odds", MAX_CHUNKS),
                  ("side", MAX_CHUNKS), ("yy", 3 * 2 * D),
                  ("lngb", 2048))

        def gcol(name):
            at, w = GEN[name]
            return gen[:, at:at + w]

        ident, before, ones = gcol("ident"), gcol("before"), gcol("ones")

        def acol(name):
            at, w = TBA[name]
            return A["tba"][:, at:at + w]

        def ccol(name):
            at, w = TBC[name]
            return C["tbc"][:, at:at + w]

        bank_full = [sem(f"bank_full{b}") for b in range(8)]
        bank_read = [sem(f"bank_read{b}") for b in range(8)]
        jobs, turns = {}, [0] * 8

        def plan(name, bank):
            jobs[name] = (bank, turns[bank])
            turns[bank] += 1

        def plan_mixer_a():
            rot = [("xT0", t, i) for t in range(3) for i in range(2)]
            rot += [("a", c) for c in range(CC)] + [("g", c) for c in range(CC)]
            rot += [("cw",), ("st", 0), ("st", 1)]
            rot += [("qkv", n, t) for n in range(3) for t in range(3)]
            rot += [("qkT", n, t) for n in range(2) for t in range(3)]
            rot += [("uo", i) for i in range(2)]
            rot += [("cvt", t) for t in range(3)]
            for n, name in enumerate(rot):
                plan(name, n % 8)
            for it in range(9):
                if it < 8:
                    plan(("S", it, 0), 0)
                    plan(("S", it, 1), 1)
                    if it % 2 == 0:
                        for i in range(4):
                            plan(("kpT", it // 2, i), 4 + i % 2)
                        plan(("SS", it // 2), 6)
                    else:
                        plan(("wTs", it // 2), 4)
                        if it % 4 == 1:
                            plan(("AO", it // 4), 7)
                if it >= 1:
                    plan(("wT", it - 1), 2)
                    if (it - 1) % 4 == 0:
                        plan(("O", (it - 1) // 4), 3)
            for i in range(2):
                plan(("att", i), i)
                plan(("aoT", i), 4 + i)
            for t in range(3):
                plan(("cT", t), (2, 6, 7)[t])
            for n in range(2):
                for t in range(3):
                    plan(("out0", n, t), (3, 0, 1, 2, 4, 5)[3 * n + t])

        def plan_mixer_c():
            for h in range(H):
                for i in range(2):
                    for c in range(2):
                        plan(("qk", h, i, c), 2 * i + c)
                for t in range(3):
                    plan(("v", h, t), 4 + t)
                if h:
                    for e in range(4):
                        plan(("oT", h - 1, e), (7, 0, 1, 2)[e])
                for name, b in ((("sc", h), 7), (("gg", h, 0), 3), (("kd", h, 0), 0), (("kd", h, 1), 1),
                                (("gg", h, 1), 2), (("S1", h, 0), 4), (("S1", h, 1), 5), (("o", h, 0), 6),
                                (("gg", h, 2), 3), (("o", h, 1), 7), (("S2", h, 0), 4), (("S2", h, 1), 5),
                                (("gg", h, 3), 0), (("o", h, 2), 1), (("o", h, 3), 2)):
                    plan(name, b)
                for b in range(DEC_B):
                    for c in range(2):
                        plan(("sn", h, b, c), 4 + c)
            for e in range(4):
                plan(("oT", H - 1, e), (7, 0, 3, 6)[e])
            for n in range(2):
                for t in range(3):
                    plan(("out1", n, t), (1, 2, 4, 5, 7, 0)[3 * n + t])

        def plan_router(l):
            for n, name in enumerate([("xTm", l, t, i) for t in range(3) for i in range(2)] +
                                     [("lgt", l), ("rank", l)]):
                plan(name, n % 8)

        turns_before_experts = []
        plan_mixer_a()
        plan_router(0)
        turns_before_experts.append(list(turns))
        for n, name in enumerate([("xT1", t, i) for t in range(3) for i in range(2)]):
            plan(name, n)
        plan_mixer_c()
        plan_router(1)
        turns_before_experts.append(list(turns))

        def bank(name):
            return ps[:, jobs[name][0], :]

        def claim(eng, name):
            b, k = jobs[name]
            if k:
                eng.wait_ge(bank_read[b], k)

        def full(name):
            return bank_full[jobs[name][0]]

        def read(name):
            return bank_read[jobs[name][0]]

        def await_full(eng, name):
            eng.wait_ge(bank_full[jobs[name][0]], jobs[name][1] + 1)

        def await_read(eng, name):
            eng.wait_ge(bank_read[jobs[name][0]], jobs[name][1] + 1)

        w_landed = [sem(f"w_landed{s}") for s in range(RING)]
        e_landed = [[sem(f"e_landed{l}_{s}") for s in range(RING)] for l in range(2)]
        last_job = {}
        for n in range(2):
            last_job[0, n] = ("ag"[n], CC - 1)
            last_job[0, 5 + n] = ("out0", n, 2)
            for r in range(2):
                last_job[1, 12 + 2 * n + r] = ("out1", n, 2)
        for n in range(3):
            last_job[0, 2 + n] = ("qkv", n, 2)
        for h in range(H):
            last_job[1, 3 * h] = ("qk", h, 1, 1)
            last_job[1, 3 * h + 1] = ("v", h, 2)
            last_job[1, 3 * h + 2] = ("gg", h, 3)
        loads, landed_at, last_in_slot = {}, [0] * RING, [{}, {}]
        for l, (count, first) in enumerate(((7, 5), (16, 2))):
            for n in range(count):
                s = (first + n) % RING
                landed_at[s] += 32 if l == 1 and n < 12 and n % 3 == 0 else 16
                loads[l, n] = (s, landed_at[s])
                last_in_slot[l][s] = last_job[l, n]

        def w_block(l, n):
            return ring[:, loads[l, n][0], :].rearrange("p (k c) -> p k c", c=512)

        def w_arrived(pe, l, n):
            pe.wait_ge(w_landed[loads[l, n][0]], loads[l, n][1])

        names = """x_in tables_in tba_in   lam_in pt_in clg_in empty_in pool_met stored kept_out
                 kv_out dve_step pool_step pads_zero conv_step conv_done rot_step lam_sums lam_exp cn_var
                 cn_std cn_pre cn_post S_bias w_done kp_in vp_in kp_new QB_set SS_bias
                 ps_done ao_zero ao_read_k att_ss att_std att_done ao_done u_out tbc_in
                 qk_rot kdm_set os_zero on_var on_std sn_done S2_done S2_out g_done ln_in
                 ln_var ln_std x_done x_stored lgs_ready lg_exp mask_ready entries rows_in plan_ready
                 plan_in yy_in0 yy_in1 yy_in2 yy_asked cw_in u_set pe_met""".split()
        S = {n: sem(n) for n in names}
        s0_in = [sem(f"s0_in{i}") for i in range(3)]
        s0_out = [sem(f"s0_out{i}") for i in range(3)]
        loop_names = """tab_in gidx_set sidx_set yb_open xg_in y_out tr_full xa_done xd_done gu_full silu_done ht_full ht_read y_full
                        hid_done0 hid_done1 ya_done0 ya_done1 yd_done0 yd_done1""".split()
        L = [{n: sem(f"{n}_{l}") for n in loop_names} for l in range(2)]

        block = ctx.enter_context(nc.Block())

        qkv = A["qkv"].rearrange("p (t c) -> p t c", t=3)
        qT = A["qT"].rearrange("p (h t) -> p h t", h=H)
        kT = A["kT"].rearrange("p (h t) -> p h t", h=H)
        up = A["up"].rearrange("p (c t) -> p c t", c=CC)
        us = A["us"].rearrange("p (c b t) -> p c b t", c=CC, b=DEC_B)
        acc = A["acc"].rearrange("p (c t) -> p c t", c=CC)
        sig = A["sig"].rearrange("p (i t) -> p i t", i=2)
        un = A["sig"][:, 0:CC * N_SAMPLE].rearrange("p (c t) -> p c t", c=CC)
        kp = A["kp"].rearrange("p (b g c) -> p b g c", b=2, g=PAGES)
        vp = A["vp"].rearrange("p (b g c) -> p b g c", b=2, g=PAGES)
        QB = A["QB"].rearrange("p (b h c) -> p b h c", b=2, h=H)
        ebuf = A["e"].rearrange("p (i m k) -> p i m k", i=2, m=2)
        wbuf = A["w"]
        wT = A["wT"].rearrange("p (k q) -> p k q", k=2)
        es = A["es"]
        wTs = A["wTs"].rearrange("p (k c) -> p k c", k=3)
        ao = A["ao"].rearrange("p (b e) -> p b e", b=DEC_B)
        ao2 = A["ao2"].rearrange("p (b e) -> p b e", b=DEC_B)
        cwT = A["cwT"].rearrange("p (c j) -> p c j", c=CC)
        mixT = A["mixT"].rearrange("p (k t) -> p k t", k=KD)
        kpT = xT[:, :, :].rearrange("p (b h) t -> p b h t", b=2)
        uo = A["uo"].rearrange("p (i c) -> p i c", i=2)
        stin = A["stin"].rearrange("p (i c) -> p i c", i=2)
        cwin = A["cwin"]
        lam_in = A["lam"].rearrange("p (i d) -> p i d", i=4)
        sm = A["small"]
        mx, nb, sums = sm[:, 0:2], sm[:, 2:4], sm[:, 4:8].rearrange("p (i m) -> p i m", i=2)
        rr, smx, snb, ssum, srl = sm[:, 8:10], sm[:, 10:11], sm[:, 11:12], sm[:, 12:13], sm[:, 13:14]
        neglam, lamrow, lam2 = sm[:, 14:15], sm[:, 15:16], sm[:, 16:18]
        cvar, cstd = sm[:, 18:24].rearrange("p (t c) -> p t c", t=3), sm[:, 24:27]
        ss_att, rs_att = sm[:, 32:40], sm[:, 40:48]
        ss_ao, rs_ao = sm[:, 48:56], sm[:, 56:64]

        qr = C["q"].rearrange("p (c t) -> p c t", c=2)
        kr = C["k"].rearrange("p (c t) -> p c t", c=2)
        qd = C["qd"].rearrange("p (c t) -> p c t", c=2)
        vh = C["v"].rearrange("p (t e) -> p t e", t=3)
        gT = C["g"].rearrange("p (k t) -> p k t", k=16)
        kd = C["kd"].rearrange("p (t d) -> p t d", t=3)
        kdm = C["kdm"].rearrange("p (b d) -> p b d", b=DEC_B)
        sc = C["sc"]
        St = C["S"].rearrange("p (c e) -> p c e", c=2)
        ob = C["o"].rearrange("p (t e) -> p t e", t=4)
        s0b = C["s0"].rearrange("p (i c e) -> p i c e", i=3, c=2)
        tmp = C["tmp"].rearrange("p (i t) -> p i t", i=4)
        cm = C["small"]
        ovar, ostd, ostat = cm[:, 0:8].rearrange("p (t c) -> p t c", t=4), cm[:, 8:12], cm[:, 16:40].rearrange("p (t c) -> p t c", t=4)

        xg = M["xg"]
        xgT = M["xgT"].rearrange("p (k s) -> p k s", k=KD)
        done_i, evens_i, odds_i, side_i = (M[n].bitcast(I32) for n in ("done", "evens", "odds", "side"))
        gidx, sidx = M["gidx"].bitcast(I32), M["sidx"].bitcast(I32)
        sg, hid, yb = M["sg"], M["hid"], M["y"]
        hidT = M["hidT"].rearrange("p (i j s) -> p i j s", i=2, j=KF)
        tab = M["tab"].bitcast(I32).rearrange("p (i w) -> p i w", i=MAX_PAIRS)
        tabf = M["tab"].rearrange("p (i w) -> p i w", i=MAX_PAIRS)
        yy = M["yy"].rearrange("p (c t d) -> p c t d", c=2, t=3)
        HALF = [slice(0, CHUNK), slice(CHUNK, P)]
        B_TR, B_GU, B_HT, B_Y = 0, 2, 4, 6

        def cols_a(t):
            return slice(OFF[t], OFF[t] + SZ[t])

        def rows(dram, t0, n):
            return dram[t0:t0 + n, :]

        def bcast(ap, shape):
            return ap.broadcast_to([P] + shape)

        def last_pair(eng, l, back=0):
            eng.wait_ge(S["plan_ready"], l + 1)
            return eng.value_load(pairs_i[0:1, back:back + 1], min_val=2 * TOK // P - 1 - back, max_val=MAX_PAIRS - 1 - back)

        @block.sync
        def _(sp):
            wa = a["w_in_a"][0].rearrange("(p k) c -> p k c", k=KD)
            wo = a["w_out_a"][0].rearrange("(k p) c -> p k c", p=P)
            wc = a["w_in_c"][0].rearrange("(p k) c -> p k c", k=KD)
            woc = a["w_out_c"][0].rearrange("(r k p) c -> r p k c", p=P, r=2)

            def load(l, n, parts):
                if n >= RING:
                    await_full(sp, last_job[l, n - RING])
                for c0, src in parts:
                    dst = w_block(l, n)[:, :, c0:c0 + src.shape[-1]]
                    sp.dma_start(dst, src).then_inc(w_landed[loads[l, n][0]], 16)

            def expert_loads(l, e0, first=False):
                gu = [a["w_e_gate"][l], a["w_e_up"][l]]
                for par in range(2):
                    e = e0 + par
                    if not first:
                        chunks = sp.value_load(done_i[0:1, bass.ds(e - 2, 1)], min_val=1, max_val=MAX_CHUNKS + 1)
                    for j in range(3):
                        s = 3 * par + j
                        if first:
                            await_full(sp, last_in_slot[l][s])
                        else:
                            sp.wait_ge(e_landed[l][s], e0 * 8)
                            sp.wait_ge(L[l][("gu_full", "gu_full", "y_full")[j]], chunks)
                        if j < 2:
                            src = gu[j].rearrange("n (p k) f -> n p (k f)", k=KD)[bass.ds(e, 1)].rearrange("n p f -> (n p) f")
                            dst = ring[:, s, :]
                        else:
                            src = a["w_e_down"][l].rearrange("n (j p) d -> n p j d", p=P)[bass.ds(e, 1)].rearrange("n p j d -> (n p) j d")
                            dst = ring[:, s, :].rearrange("p (j d) -> p j d", j=KF)
                        sp.dma_start(dst, src).then_inc(e_landed[l][s], 16)

            def experts(l):
                expert_loads(l, 0, first=True)
                sp.wait_ge(S["plan_ready"], l + 1)
                with sp.Fori(1, N_EXP // 2) as i:
                    expert_loads(l, i * 2)

            sp.dma_start(x[:, 0:2, :], a["x_prompt"][0].rearrange("(t p) d -> p t d", p=P)).then_inc(S["x_in"], 16)
            sp.dma_start(x[0:64, 2, :], a["x_sample"].rearrange("b t d -> (b t) d")).then_inc(S["x_in"], 16)
            sp.dma_start(gen[:, :], a["gen"]).then_inc(S["x_in"], 16)
            for n, c0 in enumerate((1536, 2048, 0, 512, 1024)):
                load(0, n, [(0, wa[:, :, c0:c0 + 512])])
            for n in range(2):
                load(0, 5 + n, [(0, wo[:, :, n * 512:n * 512 + 512])])
            experts(0)

            def load_c(n):
                h, j = n // 3, n % 3
                if j == 0:
                    load(1, n, [(0, wc[:, :, h * DK_C:(h + 1) * DK_C]), (DK_C, wc[:, :, D + h * DK_C:D + (h + 1) * DK_C])])
                else:
                    c0 = 2 * D + (j - 1) * 2 * D + h * DV_C
                    load(1, n, [(0, wc[:, :, c0:c0 + DV_C])])

            chunks = sp.value_load(done_i[0:1, N_EXP - 2:N_EXP - 1], min_val=1, max_val=MAX_CHUNKS + 1)
            for n in (4, 5, 0):
                s = loads[1, n][0]
                sp.wait_ge(e_landed[0][s], 16 * N_EXP // 2)
                sp.wait_ge(L[0]["gu_full" if s < 2 else "y_full"], chunks)
                load_c(n)
            sp.wait_ge(S["yy_asked"], 1)
            for n in (1, 2, 3):
                sp.wait_ge(e_landed[0][loads[1, n][0]], 16 * N_EXP // 2)
                load_c(n)
            for n in range(RING, 3 * H):
                load_c(n)
            for n in range(2):
                for r in range(2):
                    load(1, 12 + 2 * n + r, [(0, woc[r][:, :, n * 512:n * 512 + 512])])
            experts(1)
            for s in range(RING):
                sp.wait_ge(e_landed[1][s], 16 * N_EXP // 2)
            sp.wait_ge(S["stored"], 16 * 3)
            sp.wait_ge(S["kept_out"], 16)

        def counted(pool, semaphore, value):
            pool.wait_ge(semaphore, value)
            pool.sem_inc(S["pool_met"], 1)

        def experts_pool(pool, l):
            Q = L[l]
            pool.wait_ge(S["entries"], l + 1)
            pool.wait_ge(S["empty_in"], 32)
            for t in range(3):
                for c in range(2):
                    pool.indirect_dma_start(
                        out=table[l], out_offset=bass.IndirectOffsetOnAxis(ap=slot_i[0:SZ[t], t, c:c + 1], axis=0),
                        in_=entry[0:SZ[t], t, c, :], in_offset=None).then_inc(S["rows_in"], 16)
            pool.wait_ge(S["rows_in"], 96 * (l + 1))
            pool.wait_ge(S["x_stored"], 48 * (l + 1))

            pool.dma_start(tab.rearrange("p i w -> p (i w)"), table[l].rearrange("(p i) w -> p (i w)", i=MAX_PAIRS)).then_inc(Q["tab_in"], 16)
            pool.wait_ge(Q["tab_in"], 16)

            pool.tensor_copy(gidx, tab[:, 0, 0:1]).then_inc(Q["gidx_set"], 1)
            pool.wait_ge(Q["gidx_set"], 1)

            def gather():
                pool.indirect_dma_start(
                    out=xg, out_offset=None, in_=x_rows[l],
                    in_offset=bass.IndirectOffsetOnAxis(ap=gidx, axis=0)).then_inc(Q["xg_in"], 16)

            def scatter(i):
                pool.tensor_copy(sidx, tab[:, bass.ds(i, 1), 1]).then_inc(Q["sidx_set"], 1)
                counted(pool, Q["sidx_set"], i + 1)
                for hf in range(2):
                    counted(pool, Q[f"ya_done{hf}"], i + 2)
                    counted(pool, Q[f"yd_done{hf}"], i + 2)
                pool.indirect_dma_start(
                    out=y_rows[l], out_offset=bass.IndirectOffsetOnAxis(ap=sidx, axis=0),
                    in_=yb, in_offset=None, bounds_check=2 * TOK - 1, oob_is_err=False).then_inc(Q["y_out"], 16)
                counted(pool, Q["y_out"], i * 16 + 16)
                pool.sem_inc(Q["yb_open"], 1)

            def gather_next(i):
                counted(pool, Q["tr_full"], i + 1)
                pool.tensor_copy(gidx, tab[:, bass.ds(i + 1, 1), 0]).then_inc(Q["gidx_set"], 1)
                counted(pool, Q["gidx_set"], i + 2)
                gather()

            gather()
            pool.sem_inc(Q["yb_open"], 1)
            last = last_pair(pool, l)
            gather_next(0)
            last_but_one = last_pair(pool, l, 1)
            with pool.Fori(0, last_but_one) as i:
                gather_next(i + 1)
                scatter(i)
            scatter(last_but_one)
            scatter(last)

        @block.gpsimd
        def _(pool):
            steps = [0]

            def link(ins):
                steps[0] += 1
                ins.then_inc(S["pool_step"], 1)
                pool.wait_ge(S["pool_step"], steps[0])

            pool.memset(up[:, :, 0:HIST], 0.0).then_inc(S["pads_zero"], 1)
            pool.memset(QB[:, :, :, :], 0.0).then_inc(S["pads_zero"], 1)
            pool.memset(epsc[:, :], EPS).then_inc(S["pads_zero"], 1)
            pool.memset(mv[:, :, :], 1.0).then_inc(S["pads_zero"], 1)
            pool.memset(rt[:, :, :, :], 0.0).then_inc(S["pads_zero"], 1)
            pool.memset(sm[:, :], 1.0).then_inc(S["pads_zero"], 1)
            await_full(pool, ("a", 0))
            for l in range(2):
                pool.dma_start(table[l], a["empty"]).then_inc(S["empty_in"], 16)
            pool.dma_start(slot_pages[0:1, :], a["page_table"].rearrange("b g -> (b g)").rearrange("(o n) -> o n", o=1)).then_inc(S["pt_in"], 16)
            pool.dma_start(o["conv_sample"][0][:, 0:HIST - DEC_T, :], a["state_conv"][0][:, DEC_T:HIST, :]).then_inc(S["kept_out"], 16)
            pool.wait_ge(S["pt_in"], 16)

            def load_pages(g):
                for b in range(2):
                    for pg in range(PAGES):
                        page = pool.value_load(slot_pages[0:1, (2 * g + b) * PAGES + pg:(2 * g + b) * PAGES + pg + 1],
                                               min_val=0, max_val=a["cache_k"].shape[1] - 1)
                        for dst, cache, landed in ((kp, "cache_k", "kp_in"), (vp, "cache_v", "vp_in")):
                            src = a[cache][0].rearrange("n s m d -> n s (m d)")[bass.ds(page, 1)].rearrange("n s c -> (n s) c")
                            pool.dma_start(dst[:, b, pg, :], src).then_inc(S[landed], 16)

            load_pages(0)

            cosA = acol("cos").rearrange("p (t j) -> p t j", t=3)
            sinA = acol("sin").rearrange("p (t j) -> p t j", t=3)
            tr = A["w"].rearrange("p (m j) -> p m j", j=8), A["wT"].rearrange("p (m j) -> p m j", j=8)
            pool.wait_ge(S["tba_in"], 16)
            for t in range(3):
                await_read(pool, ("qkv", 1, t))
                await_read(pool, ("qkv", 0, t))
                z = SZ[t]
                v = qkv[0:z, t, 0:1024].rearrange("p (m d) -> p m d", d=DQK)
                t1, t2 = v[:, :, 0:8], v[:, :, 8:16]
                c8 = cosA[0:z, t, :].unsqueeze(1).broadcast_to([z, 16, 8])
                s8 = sinA[0:z, t, :].unsqueeze(1).broadcast_to([z, 16, 8])
                a1, a2 = tr[0][0:z, 0:16], tr[0][0:z, 16:32]
                b1, b2 = tr[1][0:z, 0:16], tr[1][0:z, 16:32]
                pool.tensor_tensor(a1, t1, c8, ALU.mult)
                pool.tensor_tensor(a2, t2, s8, ALU.mult)
                pool.tensor_tensor(b1, t2, c8, ALU.mult)
                link(pool.tensor_tensor(b2, t1, s8, ALU.mult))
                pool.tensor_tensor(t1, a1, a2, ALU.subtract)
                ins = pool.tensor_tensor(t2, b1, b2, ALU.add)
                ins.then_inc(S["rot_step"], 1)
                pool.wait_ge(S["rot_step"], t + 1)
            kdst = [o["k_prompt"][0, 0].rearrange("(t p) m d -> p t (m d)", p=P), o["k_sample"][0].rearrange("b t m d -> (b t) (m d)")]
            vdst = [o["v_prompt"][0, 0].rearrange("(t p) m d -> p t (m d)", p=P), o["v_sample"][0].rearrange("b t m d -> (b t) (m d)")]
            for t in range(3):
                await_read(pool, ("qkv", 2, t))
            for dst, c0 in ((kdst, 512), (vdst, 1024)):
                pool.dma_start(dst[0], qkv[:, 0:2, c0:c0 + 512]).then_inc(S["kv_out"], 16)
                pool.dma_start(dst[1], qkv[0:64, 2, c0:c0 + 512]).then_inc(S["kv_out"], 16)

            for t in range(3):
                await_read(pool, ("qkT", 0, t))
            for g in range(4):
                if g:
                    await_full(pool, ("SS", g - 1))
                for h in range(H):
                    for half in range(2):
                        hp = slice(64 * half, 64 * half + 64)
                        c0 = 16 * h + 8 * half
                        src = qT[hp, h, 2 * P + 16 * g:2 * P + 16 * g + 16].rearrange("p (b q) -> p b q", b=2)
                        pool.tensor_copy(QB[hp, :, h, c0:c0 + 8], src).then_inc(S["QB_set"], 1)
                if g < 3:
                    await_full(pool, ("SS", g))
                    await_full(pool, ("wT", 2 * g))
                    load_pages(g + 1)
            def state(dram, b, h):
                return dram[0, b, h].rearrange("(c p) e -> p c e", p=P)

            def load_state(j):
                pool.dma_start(s0b[:, j % 3], state(a["state_ret"], j % DEC_B, j // DEC_B)).then_inc(s0_in[j % 3], 16)

            pool.wait_ge(S["x_done"], 3)
            for j in range(3):
                load_state(j)
            experts_pool(pool, 0)
            pool.wait_ge(S["tbc_in"], 16)
            own = ccol("own")
            for h in range(H):
                await_read(pool, ("kd", h, 1))
                kd_src = kd[0:64, 2, :]
                for b in range(DEC_B):
                    pool.tensor_scalar(kdm[0:64, b, :], kd_src, own[0:64, b:b + 1], None, ALU.mult).then_inc(S["kdm_set"], 1)
                for b in range(DEC_B):
                    j = h * DEC_B + b
                    pool.wait_ge(S["sn_done"], 2 * (j + 1))
                    pool.dma_start(state(o["ret_sample"], b, h), s0b[:, j % 3]).then_inc(s0_out[j % 3], 16)
                    if j >= 1 and j + 2 < H * DEC_B:
                        pool.wait_ge(s0_out[(j - 1) % 3], 16 * ((j - 1) // 3 + 1))
                        load_state(j + 2)
                    if b == 0:
                        pool.wait_ge(S["S2_done"], 2 * (h + 1))
                        pool.dma_start(o["ret_prompt"][0, 0, h].rearrange("(c p) e -> p c e", p=P), St).then_inc(S["S2_out"], 16)
            for i in range(3):
                pool.wait_ge(s0_out[i], 16 * len(range(i, H * DEC_B, 3)))
            pool.wait_ge(S["S2_out"], 16 * H)
            experts_pool(pool, 1)

        def load_norm(act, k, lngb):
            for i, name in enumerate(("ln_g", "ln_b")):
                act.dma_start(lngb[:, i * D:(i + 1) * D], a[name][k // 2, k % 2].partition_broadcast(P)).then_inc(S["ln_in"], 16)

        def root(act, k, t):
            act.wait_ge(S["ln_var"], 3 * k + t + 1)
            act.activation(rstd[0:SZ[t], t, :], mv[0:SZ[t], t, 1:2], ACT.Sqrt, bias=epsc[0:SZ[t], 0:1]).then_inc(S["ln_std"], 1)

        def turned_x(act, name, t):
            for i in range(2):
                await_full(act, name + (t, i))
                act.activation(xT[:, 4 * i:4 * i + 4, cols_a(t)], bank(name + (t, i))[:, 0:4 * SZ[t]].rearrange("p (k t) -> p k t", k=4),
                               ACT.Copy).then_inc(read(name + (t, i)), 1)

        def experts_act(act, l):
            Q = L[l]
            root(act, 2 * l, 0)
            for t in range(3):
                act.wait_ge(S["x_done"], 6 * l + t + 1)
                act.dma_start(x_rows[l][OFF[t]:OFF[t] + SZ[t], :], x[0:SZ[t], t, :]).then_inc(S["x_stored"], 16)
                if t < 2:
                    root(act, 2 * l, t + 1)
                turned_x(act, ("xTm", l), t)
            load_norm(act, 2 * l + 1, M["lngb"])
            act.dma_start(M["pln"], a["pln"]).then_inc(S["plan_in"], 16)
            if l == 0:
                act.dma_start(C["tbc"], a["tbc"]).then_inc(S["tbc_in"], 16)
            act.wait_ge(S["lgs_ready"], l + 1)
            act.activation(rt[:, 1, :, :], rt[:, 0, :, :], ACT.Exp).then_inc(S["lg_exp"], 1)

            def turned(i):
                act.wait_ge(Q["tr_full"], i + 1)
                act.activation(xgT[:, 0:4, :], ps[:, B_TR, :].rearrange("p (k s) -> p k s", k=4), ACT.Copy).then_inc(Q["xa_done"], 1)

            def swish(i, hf):
                act.wait_ge(Q["gu_full"], i * 2 + (hf + 2))
                act.activation(sg[HALF[hf], :], ps[HALF[1 - hf], B_GU + hf, :], ACT.Silu).then_inc(Q["silu_done"], 1)

            def hidden(i, hf):
                act.wait_ge(Q["ht_full"], i * 2 + (hf + 1))
                act.activation(hidT[:, hf, :, :], ps[:, B_HT + hf, 0:KF * CHUNK].rearrange("p (j s) -> p j s", j=KF), ACT.Copy).then_inc(Q["ht_read"], 1)

            def result(i, hf):
                act.wait_ge(Q["y_full"], i * 2 + (hf + 2))
                act.wait_ge(Q["yb_open"], i + 1)
                act.activation(yb[HALF[hf], 0:512], ps[HALF[hf], B_Y + hf, :], ACT.Copy).then_inc(Q[f"ya_done{hf}"], 1)

            for hf in range(2):
                act.sem_inc(Q[f"ya_done{hf}"], 1)
            last = last_pair(act, l)
            turned(0)
            swish(0, 0)
            hidden(0, 0)
            with act.Fori(0, last) as i:
                swish(i, 1)
                result(i, 0)
                turned(i + 1)
                hidden(i, 1)
                swish(i + 1, 0)
                result(i, 1)
                hidden(i + 1, 0)
            swish(last, 1)
            result(last, 0)
            hidden(last, 1)
            result(last, 1)
            act.wait_ge(Q["y_out"], last * 16 + 16)
            for t in range(3):
                for c in range(2):
                    act.dma_start(yy[0:SZ[t], c, t, :], y_rows[l][c * TOK + OFF[t]:c * TOK + OFF[t] + SZ[t], :]).then_inc(S[f"yy_in{t}"], 16)
            act.sem_inc(S["yy_asked"], 1)
            if l == 1:
                root(act, 3, 0)
                for t in range(3):
                    if t < 2:
                        root(act, 3, t + 1)
                    act.wait_ge(S["x_done"], 9 + t + 1)
                    dst = o["y_sample"].rearrange("b t d -> (b t) d") if t == 2 else o["y_prompt"][0][t * P:(t + 1) * P, :]
                    act.dma_start(dst, x[0:SZ[t], t, :]).then_inc(S["stored"], 16)
                act.wait_ge(S["kv_out"], 64)

        @block.scalar
        def _(act):
            act.dma_start(cwin[0:CONV_W, :], a["conv_w"][0]).then_inc(S["cw_in"], 16)
            act.dma_start(cwin[CONV_W:CONV_W + 1, :], a["conv_b"]).then_inc(S["cw_in"], 16)
            for i in range(2):
                act.dma_start(stin[0:120, i, :], a["state_conv"][0, 4 * i:4 * i + 4].rearrange("b w c -> (b w) c")).then_inc(S["cw_in"], 16)
            act.dma_start(A["tba"], a["tba"]).then_inc(S["tba_in"], 16)
            act.dma_start(lam_in, a["lambda_a"][0].partition_broadcast(P)).then_inc(S["lam_in"], 16)
            act.dma_start(A["subln"], a["subln_a"][0].partition_broadcast(P)).then_inc(S["lam_in"], 16)
            act.dma_start(wr[:, :, :], a["w_router"].rearrange("(p k) e -> p k e", k=KD)).then_inc(S["tables_in"], 16)
            act.dma_start(rbias[:, :], a["b_router"].partition_broadcast(P)).then_inc(S["tables_in"], 16)
            act.dma_start(entry[:, :, :, :].rearrange("p t c w -> p (t c w)"), a["entry"]).then_inc(S["tables_in"], 16)

            for t in range(3):
                await_full(act, ("xT0", t, 0))
                act.activation(xT[:, 0:4, cols_a(t)], bank(("xT0", t, 0))[:, 0:4 * SZ[t]].rearrange("p (k t) -> p k t", k=4),
                               ACT.Copy).then_inc(read(("xT0", t, 0)), 1)
            act.wait_ge(S["lam_sums"], 1)
            act.activation(lam2, rr, ACT.Exp).then_inc(S["lam_exp"], 1)
            for c in range(CC):
                await_full(act, ("g", c))
                if c >= 2:
                    act.wait_ge(S["u_set"], 2 * (c - 1))
                act.activation(sig[:, c % 2, :], bank(("g", c))[:, 0:TOK], ACT.Sigmoid).then_inc(read(("g", c)), 1)
            for i in range(2):
                await_full(act, ("st", i))
                act.activation(us[:, :, 4 * i:4 * i + 4, 0:HIST],
                               bank(("st", i))[:, 0:480].rearrange("p (c b w) -> p c b w", c=CC, b=4), ACT.Copy).then_inc(read(("st", i)), 1)
            for n in range(3):
                for t in range(3):
                    await_full(act, ("qkv", n, t))
                    act.activation(qkv[0:SZ[t], t, n * 512:n * 512 + 512], bank(("qkv", n, t))[0:SZ[t], :], ACT.Copy).then_inc(read(("qkv", n, t)), 1)
            for n, dst in enumerate((qT, kT)):
                for t in range(3):
                    await_full(act, ("qkT", n, t))
                    act.activation(dst[:, :, cols_a(t)], bank(("qkT", n, t))[:, 0:4 * SZ[t]].rearrange("p (k t) -> p k t", k=4),
                                   ACT.Copy).then_inc(read(("qkT", n, t)), 1)
            for i, r in enumerate((HIST, 64)):
                await_full(act, ("uo", i))
                act.activation(uo[0:r, i, :], bank(("uo", i))[0:r, :], ACT.Copy).then_inc(read(("uo", i)), 1)
                await_read(act, ("uo", i))
            act.dma_start(o["conv_prompt"][0, 0], uo[0:HIST, 0, :]).then_inc(S["u_out"], 16)
            for b in range(DEC_B):
                act.dma_start(o["conv_sample"][0, b, HIST - DEC_T:HIST, :], uo[8 * b:8 * b + 8, 1, :]).then_inc(S["u_out"], 16)
            act.wait_ge(S["conv_done"], 1)
            for i in range(2):
                await_read(act, ("uo", i))
                await_full(act, ("cvt", 2))
            act.dma_start(A["clg"][:, 0:512], a["conv_ln_g"][0].partition_broadcast(P)).then_inc(S["clg_in"], 16)
            act.dma_start(A["clg"][:, 512:1024], a["conv_ln_b"][0].partition_broadcast(P)).then_inc(S["clg_in"], 16)
            act.wait_ge(S["cn_var"], 3)
            act.activation(cstd, cvar[:, :, 1], ACT.Sqrt, bias=epsc[:, 0:1]).then_inc(S["cn_std"], 1)
            for t in range(3):
                act.wait_ge(S["cn_pre"], t + 1)
                act.activation(qkv[0:SZ[t], t, 0:512], qkv[0:SZ[t], t, 0:512], ACT.Silu).then_inc(S["cn_post"], 1)
            for it in range(9):
                g = it // 2
                if it < 8:
                    if it == 0:
                        act.wait_ge(S["u_out"], 16 * 9)
                    n = (it // 4 + 1) * P
                    act.wait_ge(S["S_bias"], it + 1)
                    if it >= 2:
                        act.wait_ge(S["w_done"], it - 1)
                    for m in range(2):
                        act.activation(ebuf[:, it % 2, m, 0:n], bank(("S", it, m))[:, 0:n], ACT.Exp, bias=nb[:, m:m + 1],
                                       scale=DQK ** -0.5, accum_out=sums[:, it % 2, m:m + 1]).then_inc(read(("S", it, m)), 1)
                    if it % 2 == 0:
                        for i in range(4):
                            await_full(act, ("kpT", g, i))
                            act.activation(kpT[:, i // 2, :, (i % 2) * P:(i % 2) * P + P],
                                           bank(("kpT", g, i)).rearrange("p (h t) -> p h t", h=H), ACT.Copy).then_inc(read(("kpT", g, i)), 1)
                        act.wait_ge(S["SS_bias"], g + 1)
                        act.activation(es, bank(("SS", g))[:, 0:TOK], ACT.Exp, bias=snb, scale=DQK ** -0.5,
                                       accum_out=ssum).then_inc(read(("SS", g)), 1)
                    else:
                        await_full(act, ("wTs", g))
                        act.activation(wTs[:, 0:2, :], bank(("wTs", g))[:, 0:128].rearrange("p (k c) -> p k c", k=2), ACT.Copy)
                        act.activation(wTs[0:64, 2, :], bank(("wTs", g))[0:64, 128:192], ACT.Copy).then_inc(read(("wTs", g)), 1)
                if it >= 1:
                    n = ((it - 1) // 4 + 1)
                    await_full(act, ("wT", it - 1))
                    act.activation(wT[:, 0:n, :], bank(("wT", it - 1))[:, 0:n * P].rearrange("p (k q) -> p k q", k=n), ACT.Copy).then_inc(read(("wT", it - 1)), 1)
            load_norm(act, 0, A["lngb"])
            for i in range(2):
                await_read(act, ("O", i))
                for h in range(H):
                    act.activation(wbuf[:, 0:P], qkv[:, i, 512 + h * P:512 + h * P + P], ACT.Square,
                                   accum_out=ss_att[:, 4 * i + h:4 * i + h + 1]).then_inc(S["att_ss"], 1)
                    act.wait_ge(S["att_ss"], 4 * i + h + 1)
            act.wait_ge(S["ao_read_k"], 1)
            act.activation(rs_att, ss_att, ACT.Sqrt, bias=epsc[:, 0:1], scale=1.0 / DV_A).then_inc(S["att_std"], 1)
            act.activation(rs_ao, ss_ao, ACT.Sqrt, bias=epsc[:, 0:1], scale=1.0 / DV_A).then_inc(S["att_std"], 1)
            for i in range(2):
                await_full(act, ("att", i))
                act.activation(mixT[:, 0:4, cols_a(i)], bank(("att", i)).rearrange("p (h t) -> p h t", h=H), ACT.Copy).then_inc(read(("att", i)), 1)
                await_full(act, ("aoT", i))
                for h in range(H):
                    src = bank(("aoT", i)).rearrange("p (b h r) -> p b h r", b=4, h=H)[:, :, h, 0:8]
                    ins = act.activation(mixT[:, h, 2 * P + 32 * i:2 * P + 32 * i + 32].rearrange("p (b q) -> p b q", b=4), src, ACT.Copy)
                ins.then_inc(read(("aoT", i)), 1)
            for t in range(3):
                await_full(act, ("cT", t))
                act.activation(mixT[:, 4:8, cols_a(t)], bank(("cT", t))[:, 0:4 * SZ[t]].rearrange("p (k t) -> p k t", k=4), ACT.Copy).then_inc(read(("cT", t)), 1)
            experts_act(act, 0)

            root(act, 1, 0)
            for t in range(3):
                if t < 2:
                    root(act, 1, t + 1)
                turned_x(act, ("xT1",), t)
            act.wait_ge(S["tbc_in"], 16)
            kdec = ccol("kdec").rearrange("p (t h) -> p t h", t=3)

            def swish_gate(h, c):
                await_full(act, ("gg", h, c))
                act.activation(gT[:, 4 * h + c, :], bank(("gg", h, c))[:, 0:TOK], ACT.Silu).then_inc(read(("gg", h, c)), 1)

            for h in range(H):
                for t in range(3):
                    await_full(act, ("v", h, t))
                    act.activation(vh[0:SZ[t], t, :], bank(("v", h, t))[0:SZ[t], :], ACT.Copy).then_inc(read(("v", h, t)), 1)
                swish_gate(h, 0)
                await_full(act, ("kd", h, 0))
                for t in range(2):
                    ins = act.activation(kd[:, t, :], bank(("kd", h, 0))[:, t * 256:t * 256 + 256], ACT.Copy, scale=kdec[:, t, h:h + 1])
                ins.then_inc(read(("kd", h, 0)), 1)
                await_full(act, ("kd", h, 1))
                act.activation(kd[0:64, 2, :], bank(("kd", h, 1))[0:64, 0:256], ACT.Copy, scale=kdec[0:64, 2, h:h + 1]).then_inc(read(("kd", h, 1)), 1)
                for c in range(1, 4):
                    swish_gate(h, c)
                act.wait_ge(S["on_var"], 2 * h + 1)
                act.activation(ostd[:, 0:2], ovar[:, 0:2, 1], ACT.Sqrt, bias=epsc[:, 0:1]).then_inc(S["on_std"], 1)
                act.wait_ge(S["on_var"], 2 * h + 2)
                act.activation(ostd[:, 2:4], ovar[:, 2:4, 1], ACT.Sqrt, bias=epsc[:, 0:1]).then_inc(S["on_std"], 1)
            await_full(act, ("oT", H - 1, 3))
            load_norm(act, 2, C["lngb"])
            experts_act(act, 1)

        def tile_norm(dve, link, k, lngb, t):
            z = SZ[t]
            dve.bn_aggr(mv[0:z, t, :], stat[0:z, t, :, :].rearrange("p i s -> p (i s)")).then_inc(S["ln_var"], 1)
            dve.wait_ge(S["ln_var"], 3 * k + t + 1)
            dve.wait_ge(S["ln_in"], 32 * (k + 1))
            xs = x[0:z, t, :]
            link(dve.scalar_tensor_tensor(xs, xs, mv[0:z, t, 0:1], lngb[0:z, 0:D], ALU.subtract, ALU.mult))
            dve.wait_ge(S["ln_std"], 3 * k + t + 1)
            link(dve.reciprocal(rstd[0:z, t, :], rstd[0:z, t, :]))
            dve.scalar_tensor_tensor(xs, xs, rstd[0:z, t, :], lngb[0:z, D:2 * D], ALU.mult, ALU.add).then_inc(S["x_done"], 1)

        def residual(dve, link, name, k, lngb):
            for n in range(2):
                for t in range(3):
                    z = SZ[t]
                    j = name + (n, t)
                    await_full(dve, j)
                    xs = x[0:z, t, n * 512:n * 512 + 512]
                    dve.scalar_tensor_tensor(xs, xs, ALPHA, bank(j)[0:z, :], ALU.mult, ALU.add).then_inc(read(j), 1)
                    await_read(dve, j)
                    link(dve.bn_stats(stat[0:z, t, n, :], xs))
                    if n == 1:
                        tile_norm(dve, link, k, lngb, t)

        def experts_dve(dve, link, l):
            Q = L[l]
            T3, T4 = [3, N_EXP], [3, N_GRP]
            lg, ex, probs, sel, sel2, oh1, sel3, oh2, both, w1, rank, t9 = (rt[:, i, :, :] for i in range(12))

            def col(i):
                return r1[:, i, :]

            def wide(ap, n=N_EXP):
                return ap.unsqueeze(2).broadcast_to([P, 3, n])

            await_full(dve, ("lgt", l))
            lb = bank(("lgt", l))
            dve.tensor_copy(lg[:, 0:2, :], lb[:, 0:32].rearrange("p (t e) -> p t e", t=2))
            dve.tensor_copy(lg[0:64, 2, :], lb[0:64, 32:48]).then_inc(read(("lgt", l)), 1)
            await_read(dve, ("lgt", l))
            link(dve.tensor_reduce(col(0), lg, X, ALU.max))
            dve.tensor_tensor(lg, lg, wide(col(0)), ALU.subtract).then_inc(S["lgs_ready"], 1)
            dve.wait_ge(S["lg_exp"], l + 1)
            link(dve.tensor_reduce(col(1), ex, X, ALU.add))
            link(dve.reciprocal(col(1), col(1)))
            link(dve.tensor_tensor(probs, ex, wide(col(1)), ALU.mult))
            dve.wait_ge(S["tables_in"], 48)
            link(dve.tensor_tensor(sel, probs, rbias[:, :].unsqueeze(1).broadcast_to([P] + T3), ALU.add))
            g4 = sel.rearrange("p t (g j) -> p t g j", j=PER_GRP)
            m1, n1, m2, n2, top, mm, nn, sec, gs, eq, oh, pen = (rs[:, i, :, :] for i in range(12))
            dve.tensor_tensor(m1, g4[:, :, :, 0], g4[:, :, :, 1], ALU.max)
            dve.tensor_tensor(n1, g4[:, :, :, 0], g4[:, :, :, 1], ALU.min)
            dve.tensor_tensor(m2, g4[:, :, :, 2], g4[:, :, :, 3], ALU.max)
            link(dve.tensor_tensor(n2, g4[:, :, :, 2], g4[:, :, :, 3], ALU.min))
            dve.tensor_tensor(top, m1, m2, ALU.max)
            dve.tensor_tensor(mm, m1, m2, ALU.min)
            link(dve.tensor_tensor(nn, n1, n2, ALU.max))
            link(dve.tensor_tensor(sec, mm, nn, ALU.max))
            link(dve.tensor_tensor(gs, top, sec, ALU.add))
            gidx = gcol("gidx").rearrange("p (t g) -> p t g", t=3)
            eidx = gcol("eidx").rearrange("p (t e) -> p t e", t=3)
            link(dve.tensor_reduce(col(2), gs, X, ALU.max))
            link(dve.tensor_tensor(eq, gs, wide(col(2), N_GRP), ALU.is_equal))
            link(dve.tensor_tensor(eq, eq, gidx, ALU.mult))
            link(dve.tensor_reduce(col(3), eq, X, ALU.min))
            link(dve.tensor_tensor(oh, gidx, wide(col(3), N_GRP), ALU.is_equal))
            link(dve.tensor_scalar(pen, oh, 1.0, -NEG, ALU.subtract, ALU.mult))
            s2 = sel2.rearrange("p t (g j) -> p t g j", j=PER_GRP)
            link(dve.tensor_tensor(s2, g4, pen.unsqueeze(3).broadcast_to([P, 3, N_GRP, PER_GRP]), ALU.add))

            def best(src, dst, c):
                link(dve.tensor_reduce(col(c), src, X, ALU.max))
                link(dve.tensor_tensor(t9, src, wide(col(c)), ALU.is_equal))
                link(dve.tensor_tensor(t9, t9, eidx, ALU.mult))
                link(dve.tensor_reduce(col(c), t9, X, ALU.min))
                link(dve.tensor_tensor(dst, eidx, wide(col(c)), ALU.is_equal))

            best(sel2, oh1, 4)
            link(dve.scalar_tensor_tensor(sel3, oh1, 3 * NEG, sel2, ALU.mult, ALU.add))
            best(sel3, oh2, 5)
            dve.tensor_tensor(both, oh1, oh2, ALU.add).then_inc(S["mask_ready"], 1)
            for c, hot in ((6, oh1), (7, oh2)):
                link(dve.tensor_tensor(w1, hot, probs, ALU.mult))
                link(dve.tensor_reduce(col(c), w1, X, ALU.add))
            link(dve.tensor_tensor(col(8), col(6), col(7), ALU.add))
            link(dve.reciprocal(col(8), col(8)))
            if l:
                dve.wait_ge(S["rows_in"], 96)
            ef = entry[:, :, :, :].bitcast(F32)
            for c in range(2):
                dve.tensor_tensor(ef[:, :, c, 2], col(6 + c), col(8), ALU.mult).then_inc(S["rot_step"], 1)
            await_full(dve, ("rank", l))
            rb = bank(("rank", l))
            dve.wait_ge(S["plan_in"], 16 * (l + 1))
            pt, ch, first_ch, end_ch = M["ptmp"], M["ch"][:, 0:N_EXP], M["ch"][:, N_EXP:2 * N_EXP], M["ch"][:, 2 * N_EXP:]

            def pcol(name):
                at, w = PLN[name]
                return M["pln"][:, at:at + w]

            many = pt[:, 0:N_EXP * CUTS].rearrange("p (e k) -> p e k", e=N_EXP)
            link(dve.tensor_tensor(many, rb[:, 48:64].unsqueeze(2).broadcast_to([P, N_EXP, CUTS]),
                                   gcol("cuts").unsqueeze(1).broadcast_to([P, N_EXP, CUTS]), ALU.is_gt))
            link(dve.tensor_reduce(ch, many, X, ALU.add))
            before_e = pt.rearrange("p (e f) -> p e f", e=N_EXP)
            link(dve.tensor_tensor(before_e, ch.unsqueeze(1).broadcast_to([P, N_EXP, N_EXP]),
                                   pcol("earlier").rearrange("p (e f) -> p e f", e=N_EXP), ALU.mult))
            link(dve.tensor_reduce(first_ch, before_e, X, ALU.add))
            dve.tensor_tensor(end_ch, first_ch, ch, ALU.add)
            dve.scalar_tensor_tensor(rank[:, 0:2, :], rb[:, 0:32].rearrange("p (t e) -> p t e", t=2), 1.0 / CHUNK,
                                     first_ch.unsqueeze(1).broadcast_to([P, 2, N_EXP]), ALU.mult, ALU.add)
            link(dve.scalar_tensor_tensor(rank[0:64, 2, :], rb[0:64, 32:48], 1.0 / CHUNK, first_ch[0:64, :], ALU.mult, ALU.add))
            dve.sem_inc(read(("rank", l)), 1)
            for c, hot in ((9, oh1), (10, oh2)):
                link(dve.tensor_tensor(w1, hot, rank, ALU.mult))
                link(dve.tensor_reduce(col(c), w1, X, ALU.add))
            flat = r1[:, 9:11, :]
            passed = pt[:, 0:6 * MAX_PAIRS].rearrange("p (c t i) -> p c t i", c=2, t=3)
            pair = r1[:, 6:8, :]
            link(dve.tensor_tensor(passed, flat.unsqueeze(3).broadcast_to([P, 2, 3, MAX_PAIRS]),
                                   pcol("pairs").unsqueeze(1).unsqueeze(1).broadcast_to([P, 2, 3, MAX_PAIRS]), ALU.is_ge))
            link(dve.tensor_reduce(pair, passed, X, ALU.add))
            link(dve.tensor_scalar(pair, pair, 1.0, 1.0 - P * MAX_PAIRS, ALU.subtract, ALU.mult))
            link(dve.scalar_tensor_tensor(flat, flat, float(CHUNK * MAX_PAIRS), pair, ALU.mult, ALU.add))
            for c in range(2):
                dve.tensor_copy(slot_i[:, :, c], col(9 + c)).then_inc(S["rot_step"], 1)
            dve.wait_ge(S["rot_step"], 3 + 4 * (l + 1))
            dve.sem_inc(S["entries"], 1)
            dve.tensor_scalar(done_i, end_ch, 1.0, None, ALU.add)
            by_parity = end_ch.rearrange("p (j q) -> p q j", q=2)
            for q, dst in ((0, evens_i), (1, odds_i)):
                past = pt[:, 0:MAX_CHUNKS * 8].rearrange("p (c j) -> p c j", j=8)
                link(dve.tensor_tensor(past, by_parity[:, q, :].unsqueeze(1).broadcast_to([P, MAX_CHUNKS, 8]),
                                       pcol("seq").unsqueeze(2).broadcast_to([P, MAX_CHUNKS, 8]), ALU.is_le))
                link(dve.tensor_reduce(w1.rearrange("p t e -> p (t e)")[:, 0:MAX_CHUNKS], past, X, ALU.add))
                link(dve.tensor_scalar(dst, w1.rearrange("p t e -> p (t e)")[:, 0:MAX_CHUNKS], 8.0 - q, None, ALU.min))
            dve.tensor_tensor(side_i, evens_i, odds_i, ALU.subtract)
            some = pt[:, 0:MAX_PAIRS]
            link(dve.tensor_scalar(some, pcol("pairs"), end_ch[:, N_EXP - 1:N_EXP], None, ALU.is_lt))
            link(dve.tensor_reduce(r1[:, 11, 1:2], some, X, ALU.add))
            link(dve.tensor_scalar(pairs_i[:, 1:2], r1[:, 11, 1:2], -2.0, None, ALU.add))
            dve.tensor_scalar(pairs_i[:, 0:1], r1[:, 11, 1:2], -1.0, None, ALU.add).then_inc(S["plan_ready"], 1)

            def turned(i):
                dve.wait_ge(Q["tr_full"], i + 1)
                dve.tensor_copy(xgT[:, 4:8, :], ps[:, B_TR + 1, :].rearrange("p (k s) -> p k s", k=4)).then_inc(Q["xd_done"], 1)

            def hidden(i, hf):
                dve.wait_ge(Q["silu_done"], i * 2 + (hf + 1))
                dve.wait_ge(Q["tab_in"], 16)
                dve.scalar_tensor_tensor(hid[HALF[hf], :], sg[HALF[hf], :], tabf[HALF[hf], bass.ds(i, 1), 2],
                                         ps[HALF[hf], B_GU + hf, :], ALU.mult, ALU.mult).then_inc(Q[f"hid_done{hf}"], 1)

            def result(i, hf):
                dve.wait_ge(Q["y_full"], i * 2 + (hf + 2))
                dve.wait_ge(Q["yb_open"], i + 1)
                dve.tensor_copy(yb[HALF[hf], 512:1024], ps[HALF[1 - hf], B_Y + hf, :]).then_inc(Q[f"yd_done{hf}"], 1)

            for hf in range(2):
                dve.sem_inc(Q[f"yd_done{hf}"], 1)
                dve.sem_inc(Q[f"hid_done{hf}"], 1)
            last = last_pair(dve, l)
            turned(0)
            hidden(0, 0)
            with dve.Fori(0, last) as i:
                hidden(i, 1)
                result(i, 0)
                turned(i + 1)
                hidden(i + 1, 0)
                result(i, 1)
            hidden(last, 1)
            result(last, 0)
            result(last, 1)
            for t in range(3):
                z = SZ[t]
                dve.wait_ge(S[f"yy_in{t}"], 32 * (l + 1))
                link(dve.scalar_tensor_tensor(x[0:z, t, :], x[0:z, t, :], ALPHA, yy[0:z, 0, t, :], ALU.mult, ALU.add))
                link(dve.tensor_tensor(x[0:z, t, :], x[0:z, t, :], yy[0:z, 1, t, :], ALU.add))
                dve.bn_stats(stat[0:z, t, 0, :], x[0:z, t, 0:512])
                link(dve.bn_stats(stat[0:z, t, 1, :], x[0:z, t, 512:1024]))
                tile_norm(dve, link, 2 * l + 1, M["lngb"], t)

        @block.vector
        def _(dve):
            steps = [0]

            def link(ins):
                steps[0] += 1
                ins.then_inc(S["dve_step"], 1)
                dve.wait_ge(S["dve_step"], steps[0])

            def half_of_xT(name, dst):
                for t in range(3):
                    await_full(dve, name + (t, 1))
                    dve.tensor_copy(dst[:, 4:8, cols_a(t)], bank(name + (t, 1))[:, 0:4 * SZ[t]].rearrange("p (k t) -> p k t", k=4)).then_inc(read(name + (t, 1)), 1)

            half_of_xT(("xT0",), xT)
            dve.wait_ge(S["lam_in"], 32)
            dve.wait_ge(S["pads_zero"], 6)
            dve.tensor_scalar(A["subln"], A["subln"], 1.0 - LAM_INIT, None, ALU.mult)
            lp = lam_in.rearrange("p (i j) d -> p i j d", i=2)
            link(dve.tensor_tensor(lp[:, :, 0, :], lp[:, :, 0, :], lp[:, :, 1, :], ALU.mult))
            dve.tensor_reduce(rr, lp[:, :, 0, :], X, ALU.add).then_inc(S["lam_sums"], 1)
            dve.wait_ge(S["lam_exp"], 1)
            link(dve.tensor_tensor(neglam, lam2[:, 1:2], lam2[:, 0:1], ALU.subtract))
            link(dve.tensor_scalar(neglam, neglam, -LAM_INIT, None, ALU.add))
            dve.wait_ge(S["tba_in"], 16)
            sgn = acol("sgn")
            link(dve.scalar_tensor_tensor(lamrow, sgn[:, 1:2], neglam, sgn[:, 0:1], ALU.mult, ALU.add))

            for c in range(CC):
                await_full(dve, ("a", c))
                await_read(dve, ("g", c))
                ab = bank(("a", c))
                dve.tensor_tensor(up[:, c, HIST:], ab[:, 0:N_PROMPT], sig[:, c % 2, 0:N_PROMPT], ALU.mult).then_inc(S["u_set"], 1)
                dve.tensor_tensor(us[:, c, :, HIST:], ab[:, N_PROMPT:TOK].rearrange("p (b t) -> p b t", b=DEC_B),
                                  sig[:, c % 2, N_PROMPT:].rearrange("p (b t) -> p b t", b=DEC_B), ALU.mult).then_inc(S["u_set"], 1)
                dve.wait_ge(S["u_set"], 2 * c + 2)
                dve.sem_inc(read(("a", c)), 1)
            dve.tensor_copy(un.rearrange("p c (b t) -> p c b t", b=DEC_B), us[:, :, :, HIST:]).then_inc(S["u_set"], 1)
            await_full(dve, ("cw",))
            dve.tensor_copy(cwT, bank(("cw",))[:, 0:128].rearrange("p (c j) -> p c j", c=CC)).then_inc(read(("cw",)), 1)
            await_read(dve, ("cw",))
            for i in range(2):
                await_read(dve, ("st", i))
            n = 0
            for j in range(CONV_W):
                for c in range(CC):
                    for ext, out in ((up[:, c, j:j + N_PROMPT], acc[:, c, 0:N_PROMPT]),
                                     (us[:, c, :, j:j + DEC_T], acc[:, c, N_PROMPT:].rearrange("p (b t) -> p b t", b=DEC_B))):
                        if j == 0:
                            ins = dve.tensor_scalar(out, ext, cwT[:, c, 0:1], cwT[:, c, CONV_W:CONV_W + 1], ALU.mult, ALU.add)
                        else:
                            dve.wait_ge(S["conv_step"], n - 2 * CC + 1)
                            ins = dve.scalar_tensor_tensor(out, ext, cwT[:, c, j:j + 1], out, ALU.mult, ALU.add)
                        ins.then_inc(S["conv_step"], 1)
                        n += 1
            dve.wait_ge(S["conv_step"], n)
            dve.sem_inc(S["conv_done"], 1)
            for t in range(3):
                await_full(dve, ("cvt", t))
                z = SZ[t]
                link(dve.bn_stats(stat[0:z, t, 0, :], bank(("cvt", t))[0:z, :]))
                dve.bn_aggr(cvar[0:z, t, :], stat[0:z, t, 0, :]).then_inc(S["cn_var"], 1)
            dve.wait_ge(S["cn_std"], 1)
            link(dve.reciprocal(cstd, cstd))
            dve.wait_ge(S["clg_in"], 32)
            for t in range(3):
                z = SZ[t]
                c = qkv[0:z, t, 0:512]
                await_full(dve, ("qkT", 0, t))
                dve.tensor_scalar(c, bank(("cvt", t))[0:z, :], cvar[0:z, t, 0:1], cstd[0:z, t:t + 1], ALU.subtract, ALU.mult).then_inc(read(("cvt", t)), 1)
                await_read(dve, ("cvt", t))
                link(dve.tensor_tensor(c, c, A["clg"][0:z, 0:512], ALU.mult))
                dve.tensor_tensor(c, c, A["clg"][0:z, 512:1024], ALU.add).then_inc(S["cn_pre"], 1)
            for t in range(3):
                await_full(dve, ("qkv", 2, t))
            await_read(dve, ("qkT", 1, 2))
            for b in range(2):
                dve.tensor_copy(kpT[:, b, :, PAST:], kT[:, :, N_PROMPT:]).then_inc(S["kp_new"], 1)
            causal = acol("mask")
            smask = acol("smask").rearrange("p (g c) -> p g c", g=4)
            for it in range(9):
                g = it // 2
                if it >= 1:
                    s = it - 1
                    n = (s // 4 + 1) * P
                    await_read(dve, ("S", s, 0))
                    await_read(dve, ("S", s, 1))
                    link(dve.reciprocal(rr, sums[:, s % 2, :]))
                    link(dve.tensor_scalar(rr[:, 1:2], rr[:, 1:2], neglam, None, ALU.mult))
                    if s:
                        await_full(dve, ("wT", s - 1))
                    link(dve.tensor_scalar(wbuf[:, 0:n], ebuf[:, s % 2, 0, 0:n], rr[:, 0:1], None, ALU.mult))
                    dve.scalar_tensor_tensor(wbuf[:, 0:n], ebuf[:, s % 2, 1, 0:n], rr[:, 1:2], wbuf[:, 0:n], ALU.mult, ALU.add).then_inc(S["w_done"], 1)
                if it < 8:
                    i = it // 4
                    n = (i + 1) * P
                    await_full(dve, ("S", it, 0))
                    await_full(dve, ("S", it, 1))
                    diag = ps[:, 0:2, i * P:i * P + P]
                    link(dve.tensor_tensor(diag, diag, causal.unsqueeze(1).broadcast_to([P, 2, P]), ALU.add))
                    link(dve.tensor_reduce(mx, ps[:, 0:2, 0:n], X, ALU.max))
                    dve.tensor_scalar(nb, mx, -DQK ** -0.5, None, ALU.mult).then_inc(S["S_bias"], 1)
                    if it % 2 == 0:
                        if it % 4 == 0:
                            claim(dve, ("AO", it // 4))
                            dve.memset(ps[:, 7, :], 0.0).then_inc(S["ao_zero"], 1)
                        await_full(dve, ("SS", g))
                        sb_ = bank(("SS", g))
                        link(dve.tensor_tensor(sb_[:, PAST:TOK], sb_[:, PAST:TOK], smask[:, g, :], ALU.add))
                        link(dve.tensor_reduce(smx, sb_[:, 0:TOK], X, ALU.max))
                        dve.tensor_scalar(snb, smx, -DQK ** -0.5, None, ALU.mult).then_inc(S["SS_bias"], 1)
                    else:
                        await_read(dve, ("SS", g))
                        link(dve.reciprocal(srl, ssum))
                        link(dve.tensor_tensor(srl, srl, lamrow, ALU.mult))
                        dve.tensor_scalar(es, es, srl, None, ALU.mult).then_inc(S["ps_done"], 1)
                        if it % 4 == 3:
                            k = it // 4
                            await_full(dve, ("AO", k))
                            dve.tensor_copy(ao[:, 4 * k:4 * k + 4, :], bank(("AO", k)).rearrange("p (b e) -> p b e", b=4)).then_inc(read(("AO", k)), 1)
                if it in (4, 8):
                    i = it // 4 - 1
                    await_full(dve, ("O", i))
                    if i == 0:
                        dve.wait_ge(S["kv_out"], 64)
                    dve.tensor_copy(qkv[:, i, 512:1024], bank(("O", i))).then_inc(read(("O", i)), 1)
            await_read(dve, ("AO", 1))
            link(dve.tensor_tensor(ao2, ao, ao, ALU.mult))
            dve.tensor_reduce(ss_ao, ao2, X, ALU.add).then_inc(S["ao_read_k"], 1)
            g08 = A["subln"]
            dve.wait_ge(S["att_std"], 2)
            link(dve.reciprocal(rs_att, rs_att))
            link(dve.reciprocal(rs_ao, rs_ao))
            for i in range(2):
                v = qkv[:, i, 512:1024].rearrange("p (h e) -> p h e", h=H)
                link(dve.tensor_tensor(v, v, rs_att[:, 4 * i:4 * i + 4].unsqueeze(2).broadcast_to([P, H, P]), ALU.mult))
                dve.tensor_tensor(v, v, g08.unsqueeze(1).broadcast_to([P, H, P]), ALU.mult).then_inc(S["att_done"], 1)
            link(dve.tensor_tensor(ao, ao, rs_ao.unsqueeze(2).broadcast_to([P, DEC_B, P]), ALU.mult))
            dve.tensor_tensor(ao, ao, g08.unsqueeze(1).broadcast_to([P, DEC_B, P]), ALU.mult).then_inc(S["ao_done"], 1)
            residual(dve, link, ("out0",), 0, A["lngb"])
            experts_dve(dve, link, 0)

            dve.wait_ge(S["tbc_in"], 16)
            cosC, sinC = ccol("cos"), ccol("sin")
            dec = ccol("dec").rearrange("p (h i) -> p h i", h=H)
            sdec = ccol("sdec").rearrange("p (h i) -> p h i", h=H)
            qdec = ccol("qdec").rearrange("p (h i) -> p h i", h=H)

            def gate_out(h):
                for e in range(4):
                    await_full(dve, ("oT", h, e))
                    await_read(dve, ("gg", h, e))
                    b = bank(("oT", h, e))
                    g = gT[:, 4 * h + e, :]
                    dve.tensor_tensor(g[:, 0:N_PROMPT], g[:, 0:N_PROMPT], b[:, 0:N_PROMPT], ALU.mult)
                    gs = g[:, N_PROMPT:].rearrange("p (i q t) -> p i q t", i=2, q=4)
                    bs = b[:, 2 * P:].rearrange("p (i q r) -> p i q r", i=2, q=4)[:, :, :, 0:8]
                    dve.tensor_tensor(gs, gs, bs, ALU.mult).then_inc(read(("oT", h, e)), 1)

            for h in range(H):
                for i, (dst, s) in enumerate(((qr, 1.0), (kr, 1.0 / 16))):
                    if h or i:
                        dve.wait_ge(S["qk_rot"], 2 * (2 * h + i))
                    for c in range(2):
                        await_full(dve, ("qk", h, i, c))
                        b = bank(("qk", h, i, c))[:, 0:TOK]
                        dve.scalar_tensor_tensor(tmp[:, 2 * c, :], b, s, cosC, ALU.mult, ALU.mult)
                        link(dve.scalar_tensor_tensor(tmp[:, 2 * c + 1, :], b, s, sinC, ALU.mult, ALU.mult))
                        dve.sem_inc(read(("qk", h, i, c)), 1)
                    dve.tensor_tensor(dst[:, 0, :], tmp[:, 0, :], tmp[:, 3, :], ALU.subtract).then_inc(S["qk_rot"], 1)
                    dve.tensor_tensor(dst[:, 1, :], tmp[:, 2, :], tmp[:, 1, :], ALU.add).then_inc(S["qk_rot"], 1)
                dve.wait_ge(S["qk_rot"], 4 * h + 4)
                dve.tensor_tensor(qd, qr[:, :, P:], qdec[:, h, :].unsqueeze(1).broadcast_to([P, 2, TOK - P]), ALU.mult).then_inc(S["g_done"], 1)
                if h:
                    gate_out(h - 1)
                await_full(dve, ("sc", h))
                b = bank(("sc", h))
                dve.tensor_tensor(sc[:, 0:256].rearrange("p (c i) -> p c i", c=2), b[:, 0:256].rearrange("p (c i) -> p c i", c=2),
                                  dec[:, h, :].unsqueeze(1).broadcast_to([P, 2, P]), ALU.mult)
                dve.tensor_tensor(sc[0:64, 256:320], b[0:64, 256:320], sdec[0:64, h, :], ALU.mult).then_inc(read(("sc", h)), 1)
                if h:
                    dve.wait_ge(S["S2_out"], 16 * h)
                for c in range(2):
                    await_full(dve, ("S1", h, c))
                    dve.tensor_copy(St[:, c, :], bank(("S1", h, c))).then_inc(read(("S1", h, c)), 1)
                claim(dve, ("o", h, 2))
                claim(dve, ("o", h, 3))
                dve.memset(ps[:, 1:3, :], 0.0).then_inc(S["os_zero"], 1)

                def norm_o(lo, hi):
                    for t in range(lo, hi):
                        await_full(dve, ("o", h, t))
                        link(dve.bn_stats(ostat[:, t, :], bank(("o", h, t))))
                        link(dve.bn_aggr(ovar[:, t, :], ostat[:, t, :]))
                    dve.sem_inc(S["on_var"], 1)
                    dve.wait_ge(S["on_std"], 2 * h + 1 + lo // 2)
                    link(dve.reciprocal(ostd[:, lo:hi], ostd[:, lo:hi]))
                    for t in range(lo, hi):
                        dve.tensor_scalar(ob[:, t, :], bank(("o", h, t)), ovar[:, t, 0:1], ostd[:, t:t + 1], ALU.subtract, ALU.mult).then_inc(read(("o", h, t)), 1)

                norm_o(0, 2)
                for c in range(2):
                    await_full(dve, ("S2", h, c))
                    dve.scalar_tensor_tensor(St[:, c, :], St[:, c, :], float(np.exp(P * LOG_G[h])), bank(("S2", h, c)), ALU.mult, ALU.add).then_inc(read(("S2", h, c)), 1)
                    await_read(dve, ("S2", h, c))
                    dve.sem_inc(S["S2_done"], 1)
                for bq in range(DEC_B):
                    for c in range(2):
                        await_full(dve, ("sn", h, bq, c))
                        s = s0b[:, (h * DEC_B + bq) % 3, c, :]
                        dve.scalar_tensor_tensor(s, s, float(np.exp(DEC_T * LOG_G[h])), bank(("sn", h, bq, c)), ALU.mult, ALU.add).then_inc(read(("sn", h, bq, c)), 1)
                        await_read(dve, ("sn", h, bq, c))
                        dve.sem_inc(S["sn_done"], 1)
                norm_o(2, 4)
            gate_out(H - 1)
            residual(dve, link, ("out1",), 2, C["lngb"])
            experts_dve(dve, link, 1)

        def experts_pe(pe, l, turn_x):
            Q = L[l]
            turn_x(("xTm", l), 6 * l)
            pe.wait_ge(S["tables_in"], 48)
            claim(pe, ("lgt", l))
            for t in range(3):
                for i in range(2):
                    await_read(pe, ("xTm", l, t, i))
                for k in range(KD):
                    ins = pe.matmul(bank(("lgt", l))[0:SZ[t], t * 16:t * 16 + 16], xT[:, k, cols_a(t)], wr[:, k, :], start=k == 0, stop=k == KD - 1)
            ins.then_inc(full(("lgt", l)), 1)
            pe.wait_ge(S["mask_ready"], l + 1)
            both = rt[:, 8, :, :]
            claim(pe, ("rank", l))
            rb = bank(("rank", l))
            for t in range(3):
                for s in range(t + 1):
                    z = SZ[s]
                    pe.matmul(rb[0:SZ[t], t * 16:t * 16 + 16], (ones if s < t else before)[0:z, 0:SZ[t]], both[0:z, s, :], start=s == 0, stop=s == t)
            for s in range(3):
                ins = pe.matmul(rb[:, 48:64], ones[0:SZ[s], :], both[0:SZ[s], s, :], start=s == 0, stop=s == 2)
            ins.then_inc(full(("rank", l)), 1)
            for b in range(8):
                pe.wait_ge(bank_read[b], turns_before_experts[l][b])

            def chunk_weights(i, hf):
                c = i * 2 + hf
                at = bass.ds(c, 1)
                evens = pe.value_load(evens_i[0:1, at], min_val=0, max_val=8)
                odds = pe.value_load(odds_i[0:1, at], min_val=0, max_val=7)
                side = pe.value_load(side_i[0:1, at], min_val=0, max_val=1)
                return side, (odds * 16 + 16, evens * 16)

            def by_side(side, products):
                with pe.If(side == 0):
                    products(0)
                with pe.If(side == 1):
                    products(3)

            def arrived(slot, arrivals):
                pe.wait_ge(e_landed[l][slot], arrivals[slot // 3])

            def turn_rows(i):
                pe.wait_ge(Q["xg_in"], i * 16 + 16)
                xv = xg.rearrange("p (q k) -> p k q", k=KD)
                for k in range(KD):
                    ins = pe.transpose(ps[:, B_TR + k // 4, k % 4 * P:k % 4 * P + P], xv[:, k, :], ident)
                ins.then_inc(Q["tr_full"], 1)

            def gate_up(i, hf):
                side, arrivals = chunk_weights(i, hf)
                pe.wait_ge(Q["xa_done"], i + 1)
                pe.wait_ge(Q["xd_done"], i + 1)
                pe.wait_ge(Q[f"hid_done{hf}"], i + 1)

                def products(slot):
                    arrived(slot, arrivals)
                    arrived(slot + 1, arrivals)
                    for k in range(KD):
                        for j in range(2):
                            ins = pe.matmul(ps[HALF[hf if j else 1 - hf], B_GU + hf, :], xgT[:, k, HALF[hf]],
                                            ring[:, slot + j, k * D_FF:(k + 1) * D_FF], start=k == 0, stop=k == KD - 1)
                    ins.then_inc(Q["gu_full"], 1)

                by_side(side, products)

            def turn_hidden(i, hf):
                pe.wait_ge(Q[f"hid_done{hf}"], i + 2)
                pe.sem_inc(S["pe_met"], 1)
                for j in range(KF):
                    ins = pe.transpose(ps[:, B_HT + hf, j * CHUNK:(j + 1) * CHUNK], hid[HALF[hf], j * P:j * P + P], ident[HALF[hf], HALF[hf]])
                ins.then_inc(Q["ht_full"], 1)

            def down(i, hf):
                side, arrivals = chunk_weights(i, hf)
                pe.wait_ge(Q["ht_read"], i * 2 + (hf + 1))
                pe.wait_ge(Q[f"ya_done{hf}"], i + 1)
                pe.wait_ge(Q[f"yd_done{hf}"], i + 1)

                def products(slot):
                    arrived(slot + 2, arrivals)
                    for j in range(KF):
                        for n in range(2):
                            ins = pe.matmul(ps[HALF[1 - hf if n else hf], B_Y + hf, :], hidT[:, hf, j, :],
                                            ring[:, slot + 2, j * D + n * 512:j * D + n * 512 + 512], start=j == 0, stop=j == KF - 1)
                    ins.then_inc(Q["y_full"], 1)

                by_side(side, products)

            pe.sem_inc(Q["gu_full"], 1)
            pe.sem_inc(Q["y_full"], 1)
            last = last_pair(pe, l)
            turn_rows(0)
            gate_up(0, 0)
            turn_hidden(0, 0)
            with pe.Fori(0, last) as i:
                gate_up(i, 1)
                down(i, 0)
                turn_rows(i + 1)
                turn_hidden(i, 1)
                gate_up(i + 1, 0)
                down(i, 1)
                turn_hidden(i + 1, 0)
            gate_up(last, 1)
            down(last, 0)
            turn_hidden(last, 1)
            down(last, 1)
            if l == 0:
                for hf in range(2):
                    pe.wait_ge(Q[f"ya_done{hf}"], last + 2)
                    pe.wait_ge(Q[f"yd_done{hf}"], last + 2)

        @block.tensor
        def _(pe):
            def turn_x(name, done=None):
                for t in range(3):
                    if done is not None:
                        pe.wait_ge(S["x_done"], done + t + 1)
                    xv = x[0:SZ[t], t, :].rearrange("p (q k) -> p k q", k=KD)
                    for i in range(2):
                        j = name + (t, i)
                        claim(pe, j)
                        for c in range(4):
                            ins = pe.transpose(bank(j)[:, c * SZ[t]:(c + 1) * SZ[t]], xv[:, 4 * i + c, :], ident[0:SZ[t], 0:SZ[t]])
                        ins.then_inc(full(j), 1)

            def feature_major(j, w, k0):
                claim(pe, j)
                for k in range(KD):
                    ins = pe.matmul(bank(j)[:, 0:TOK], w[:, k, k0:k0 + P], xT[:, k, :], start=k == 0, stop=k == KD - 1)
                ins.then_inc(full(j), 1)
                return ins

            pe.wait_ge(S["x_in"], 16 * 3)
            turn_x(("xT0",))
            for t in range(3):
                for i in range(2):
                    await_read(pe, ("xT0", t, i))
            for n, name in enumerate(("a", "g")):
                w_arrived(pe, 0, n)
                for c in range(CC):
                    ins = feature_major((name, c), w_block(0, n), c * P)
            pe.wait_ge(S["cw_in"], 16 * 4)
            claim(pe, ("cw",))
            for c in range(CC):
                ins = pe.transpose(bank(("cw",))[:, c * 32:c * 32 + 32], cwin[0:32, c * P:c * P + P], ident[0:32, 0:32])
            ins.then_inc(full(("cw",)), 1)
            for i in range(2):
                claim(pe, ("st", i))
                for c in range(CC):
                    ins = pe.transpose(bank(("st", i))[:, c * 120:c * 120 + 120], stin[0:120, i, c * P:c * P + P], ident[0:120, 0:120])
                ins.then_inc(full(("st", i)), 1)
            for n in range(3):
                w_arrived(pe, 0, 2 + n)
                w = w_block(0, 2 + n)
                for t in range(3):
                    j = ("qkv", n, t)
                    claim(pe, j)
                    for k in range(KD):
                        ins = pe.matmul(bank(j)[0:SZ[t], :], xT[:, k, cols_a(t)], w[:, k, :], start=k == 0, stop=k == KD - 1)
                    ins.then_inc(full(j), 1)
            for n in range(2):
                for t in range(3):
                    z = SZ[t]
                    pe.wait_ge(S["rot_step"], t + 1)
                    j = ("qkT", n, t)
                    claim(pe, j)
                    for h in range(H):
                        ins = pe.transpose(bank(j)[:, h * z:h * z + z], qkv[0:z, t, n * 512 + h * P:n * 512 + h * P + P], ident[0:z, 0:z])
                    ins.then_inc(full(j), 1)
            pe.wait_ge(S["u_set"], 2 * CC + 1)
            for i in range(2):
                j = ("uo", i)
                claim(pe, j)
                for c in range(CC):
                    if i == 0:
                        ins = pe.transpose(bank(j)[0:HIST, c * P:c * P + P], up[:, c, N_PROMPT:N_PROMPT + HIST], ident)
                    else:
                        ins = pe.transpose(bank(j)[0:64, c * P:c * P + P], un[:, c, :], ident)
                ins.then_inc(full(j), 1)
            pe.wait_ge(S["conv_done"], 1)
            for t in range(3):
                j = ("cvt", t)
                claim(pe, j)
                for c in range(CC):
                    ins = pe.transpose(bank(j)[0:SZ[t], c * P:c * P + P], acc[:, c, cols_a(t)], ident)
                ins.then_inc(full(j), 1)
            for t in range(3):
                for n in range(2):
                    await_read(pe, ("qkT", n, t))
            pair = acol("pair")
            for it in range(9):
                g = it // 2
                if it < 8:
                    i, h = it // 4, it % 4
                    n = (i + 1) * P
                    for m in range(2):
                        hp = slice(64 * m, 64 * m + 64)
                        claim(pe, ("S", it, m))
                        pe.matmul(bank(("S", it, m))[:, 0:n], qT[hp, h, cols_a(i)], kT[hp, h, 0:n], start=True, stop=True).then_inc(full(("S", it, m)), 1)
                    if it % 2 == 0:
                        pe.wait_ge(S["kp_in"], 64 * (g + 1))
                        for j4 in range(4):
                            j = ("kpT", g, j4)
                            claim(pe, j)
                            for hh in range(H):
                                ins = pe.transpose(bank(j)[:, hh * P:hh * P + P], kp[:, j4 // 2, j4 % 2, hh * P:hh * P + P], ident)
                            ins.then_inc(full(j), 1)
                        for j4 in range(4):
                            await_read(pe, ("kpT", g, j4))
                        pe.wait_ge(S["kp_new"], 2)
                        pe.wait_ge(S["QB_set"], 8 * (g + 1))
                        j = ("SS", g)
                        claim(pe, j)
                        for b in range(2):
                            for hh in range(H):
                                ins = pe.matmul(bank(j)[64 * b:64 * b + 64, 0:TOK], QB[:, b, hh, :], kpT[:, b, hh, :], start=hh == 0, stop=hh == H - 1)
                        ins.then_inc(full(j), 1)
                    else:
                        j = ("wTs", g)
                        pe.wait_ge(S["ps_done"], g + 1)
                        claim(pe, j)
                        for pg in range(2):
                            pe.matmul(bank(j)[:, pg * 64:pg * 64 + 64], es[:, pg * P:pg * P + P], pair, start=True, stop=True)
                        pe.matmul(bank(j)[0:64, 128:192], es[:, PAST:TOK], pair, start=True, stop=True).then_inc(full(j), 1)
                        await_read(pe, j)
                        pe.wait_ge(S["vp_in"], 64 * (g + 1))
                        j = ("AO", it // 4)
                        pe.wait_ge(S["ao_zero"], it // 4 + 1)
                        for b in range(2):
                            col = (2 * g + b) % 4 * P
                            for hh in range(H):
                                out = bank(j)[32 * hh:32 * hh + 8, col:col + P]
                                c0 = b * 32 + hh * 8
                                for pg in range(2):
                                    pe.matmul(out, wTs[:, pg, c0:c0 + 8], vp[:, b, pg, hh * P:hh * P + P], start=pg == 0, stop=False)
                                ins = pe.matmul(out, wTs[0:64, 2, c0:c0 + 8], qkv[0:64, 2, 1024 + hh * P:1024 + hh * P + P], start=False, stop=True)
                        if it % 4 == 3:
                            ins.then_inc(full(j), 1)
                if it >= 1:
                    s = it - 1
                    i, h = s // 4, s % 4
                    j = ("wT", s)
                    pe.wait_ge(S["w_done"], s + 1)
                    claim(pe, j)
                    for k in range(i + 1):
                        ins = pe.transpose(bank(j)[:, k * P:k * P + P], wbuf[:, k * P:k * P + P], ident)
                    ins.then_inc(full(j), 1)
                    await_read(pe, j)
                    j = ("O", i)
                    if h == 0:
                        claim(pe, j)
                    for k in range(i + 1):
                        ins = pe.matmul(bank(j)[:, h * P:h * P + P], wT[:, k, :], qkv[:, k, 1024 + h * P:1024 + h * P + P], start=k == 0, stop=k == i)
                    if h == 3:
                        ins.then_inc(full(j), 1)
            for i in range(2):
                pe.wait_ge(S["att_done"], i + 1)
                claim(pe, ("att", i))
                for h in range(H):
                    ins = pe.transpose(bank(("att", i))[:, h * P:h * P + P], qkv[:, i, 512 + h * P:512 + h * P + P], ident)
                ins.then_inc(full(("att", i)), 1)
                if i == 0:
                    pe.wait_ge(S["ao_done"], 1)
                claim(pe, ("aoT", i))
                for b in range(4):
                    ins = pe.transpose(bank(("aoT", i))[:, b * P:b * P + P], ao[:, 4 * i + b, :], ident)
                ins.then_inc(full(("aoT", i)), 1)
            pe.wait_ge(S["cn_post"], 3)
            for t in range(3):
                z = SZ[t]
                claim(pe, ("cT", t))
                for c in range(CC):
                    ins = pe.transpose(bank(("cT", t))[:, c * z:c * z + z], qkv[0:z, t, c * P:c * P + P], ident[0:z, 0:z])
                ins.then_inc(full(("cT", t)), 1)
            for i in range(2):
                await_read(pe, ("att", i))
                await_read(pe, ("aoT", i))
            for t in range(3):
                await_read(pe, ("cT", t))
            for n in range(2):
                w_arrived(pe, 0, 5 + n)
                w = w_block(0, 5 + n)
                for t in range(3):
                    j = ("out0", n, t)
                    claim(pe, j)
                    for k in range(KD):
                        ins = pe.matmul(bank(j)[0:SZ[t], :], mixT[:, k, cols_a(t)], w[:, k, :], start=k == 0, stop=k == KD - 1)
                    ins.then_inc(full(j), 1)
            experts_pe(pe, 0, turn_x)

            turn_x(("xT1",), 3)
            for t in range(3):
                for i in range(2):
                    await_read(pe, ("xT1", t, i))

            def turn_out(h):
                for t in range(4):
                    await_read(pe, ("o", h, t))
                for e in range(4):
                    j = ("oT", h, e)
                    claim(pe, j)
                    for t in range(4):
                        ins = pe.transpose(bank(j)[:, t * P:t * P + P], ob[:, t, e * P:e * P + P], ident)
                    ins.then_inc(full(j), 1)

            for h in range(H):
                w_arrived(pe, 1, 3 * h)
                w = w_block(1, 3 * h)
                for i in range(2):
                    for c in range(2):
                        ins = feature_major(("qk", h, i, c), w, i * DK_C + c * P)
                w_arrived(pe, 1, 3 * h + 1)
                w = w_block(1, 3 * h + 1)
                for t in range(3):
                    j = ("v", h, t)
                    claim(pe, j)
                    for k in range(KD):
                        ins = pe.matmul(bank(j)[0:SZ[t], :], xT[:, k, cols_a(t)], w[:, k, :], start=k == 0, stop=k == KD - 1)
                    ins.then_inc(full(j), 1)
                if h:
                    turn_out(h - 1)
                w_arrived(pe, 1, 3 * h + 2)
                w = w_block(1, 3 * h + 2)
                pe.wait_ge(S["qk_rot"], 4 * h + 4)
                j = ("sc", h)
                claim(pe, j)
                for t in range(3):
                    for c in range(2):
                        ins = pe.matmul(bank(j)[0:SZ[t], cols_a(t)], kr[:, c, cols_a(t)], qr[:, c, cols_a(t)], start=c == 0, stop=c == 1)
                ins.then_inc(full(j), 1)
                feature_major(("gg", h, 0), w, 0)
                for i in range(2):
                    j = ("kd", h, i)
                    claim(pe, j)
                    for t in ((0, 1), (2,))[i]:
                        for c in range(2):
                            at = (t % 2) * 256 + c * P
                            ins = pe.transpose(bank(j)[0:SZ[t], at:at + P], kr[:, c, cols_a(t)], ident)
                    ins.then_inc(full(j), 1)
                feature_major(("gg", h, 1), w, P)
                for t in range(3):
                    await_read(pe, ("v", h, t))
                await_read(pe, ("sc", h))
                await_read(pe, ("kd", h, 0))
                for c in range(2):
                    j = ("S1", h, c)
                    claim(pe, j)
                    pe.matmul(bank(j), kd[:, 0, c * P:c * P + P], vh[:, 0, :], start=True, stop=True).then_inc(full(j), 1)
                j = ("o", h, 0)
                claim(pe, j)
                pe.matmul(bank(j), sc[:, 0:P], vh[:, 0, :], start=True, stop=True).then_inc(full(j), 1)
                feature_major(("gg", h, 2), w, 2 * P)
                j = ("o", h, 1)
                claim(pe, j)
                pe.matmul(bank(j), sc[:, P:2 * P], vh[:, 1, :], start=True, stop=False)
                pe.wait_ge(S["g_done"], h + 1)
                for c in range(2):
                    await_read(pe, ("S1", h, c))
                for c in range(2):
                    ins = pe.matmul(bank(j), qd[:, c, 0:P], St[:, c, :], start=False, stop=c == 1)
                ins.then_inc(full(j), 1)
                for c in range(2):
                    j = ("S2", h, c)
                    claim(pe, j)
                    pe.matmul(bank(j), kd[:, 1, c * P:c * P + P], vh[:, 1, :], start=True, stop=True).then_inc(full(j), 1)
                ins = feature_major(("gg", h, 3), w, 3 * P)
                pe.wait_ge(S["os_zero"], h + 1)
                pe.wait_ge(S["kdm_set"], DEC_B * (h + 1))
                for b in range(DEC_B):
                    n = h * DEC_B + b
                    pe.wait_ge(s0_in[n % 3], 16 * (n // 3 + 1))
                    j = ("o", h, 2 + b // 4)
                    out = bank(j)[32 * (b % 4):32 * (b % 4) + 8, :]
                    for c in range(2):
                        pe.matmul(out, qd[:, c, P + b * 8:P + b * 8 + 8], s0b[:, n % 3, c, :], start=c == 0, stop=False)
                    ins = pe.matmul(out, sc[0:64, 256 + b * 8:256 + b * 8 + 8], vh[0:64, 2, :], start=False, stop=True)
                    if b % 4 == 3:
                        ins.then_inc(full(j), 1)
                    for c in range(2):
                        j = ("sn", h, b, c)
                        claim(pe, j)
                        pe.matmul(bank(j), kdm[0:64, b, c * P:c * P + P], vh[0:64, 2, :], start=True, stop=True).then_inc(full(j), 1)
            turn_out(H - 1)
            for e in range(4):
                await_read(pe, ("oT", H - 1, e))
            for n in range(2):
                for r in range(2):
                    w_arrived(pe, 1, 12 + 2 * n + r)
                for t in range(3):
                    j = ("out1", n, t)
                    claim(pe, j)
                    for r in range(2):
                        w = w_block(1, 12 + 2 * n + r)
                        for k in range(KD):
                            ins = pe.matmul(bank(j)[0:SZ[t], :], gT[:, r * KD + k, cols_a(t)], w[:, k, :], start=r + k == 0, stop=r + k == KD)
                    ins.then_inc(full(j), 1)
            experts_pe(pe, 1, turn_x)



_INS = ["x_prompt", "x_sample", "cache_k", "cache_v", "page_table", "state_conv", "state_ret", "w_in_a", "lambda_a",
        "subln_a", "conv_w", "conv_b", "conv_ln_g", "conv_ln_b", "w_out_a", "w_in_c", "w_out_c", "ln_g", "ln_b",
        "w_router", "b_router", "w_e_gate", "w_e_up", "w_e_down"]
_OUTS = [("y_prompt", (1, 256, 1024)), ("y_sample", (8, 8, 1024)), ("k_prompt", (1, 1, 256, 8, 64)),
         ("v_prompt", (1, 1, 256, 4, 128)), ("conv_prompt", (1, 1, 30, 512)), ("ret_prompt", (1, 1, 4, 256, 512)),
         ("k_sample", (1, 8, 8, 8, 64)), ("v_sample", (1, 8, 8, 4, 128)), ("conv_sample", (1, 8, 30, 512)),
         ("ret_sample", (1, 8, 4, 256, 512))]


def kernel(**inputs):
    import numpy as _np
    import concourse.bacc as _bacc
    from concourse import mybir as _mybir
    from concourse.bass_utils import run_bass_kernel_spmd as _run

    nc = _bacc.Bacc("TRN2", target_bir_lowering=False, num_devices=1)
    data = {name: _np.ascontiguousarray(inputs[name]) for name in _INS}
    data.update(host_tables())
    arrays, a, o = {}, {}, {}
    for name, v in data.items():
        arrays[f"in_{name}_dram"] = v
        a[name] = nc.dram_tensor(f"in_{name}_dram", v.shape, _mybir.dt.from_np(v.dtype), kind="ExternalInput").ap()
    for name, shape in _OUTS:
        o[name] = nc.dram_tensor(f"out_{name}_dram", shape, _mybir.dt.float32, kind="ExternalOutput").ap()
    build(nc, a, o)
    r = _run(nc, [arrays], core_ids=[0])
    return tuple(r.results[0][f"out_{name}_dram"] for name, _ in _OUTS)
```

```python
import math
from contextlib import ExitStack

import numpy as np

import concourse.bass as bass
from concourse import mybir

F32 = mybir.dt.float32
I32 = mybir.dt.int32
ALU = mybir.AluOpType
ACT = mybir.ActivationFunctionType
X = mybir.AxisListType.X

P = 128
D = 1024
N_PROMPT = 256
DEC_B, DEC_T = 8, 8
N_SAMPLE = DEC_B * DEC_T
TOK = N_PROMPT + N_SAMPLE
SZ = [P, P, N_SAMPLE]
OFF = [0, P, 2 * P]
KD = D // P
PAST, PAGE = 256, 128
PAGES = PAST // PAGE
H = 4
DQK, DV_A = 64, 128
ATT_W = H * DV_A
CONV_CH, CONV_W = 512, 31
CC = CONV_CH // P
HIST = CONV_W - 1
DK_C, DV_C = 256, 512
N_EXP, N_GRP, PER_GRP = 16, 4, 4
D_FF = 512
KF = D_FF // P
ALPHA = float((2 * 2) ** 0.25)
EPS = 1e-5
CHUNK = 64
CUTS = TOK // CHUNK
MAX_PAIRS = ((2 * TOK + N_EXP * (CHUNK - 1)) // CHUNK + 1) // 2
MAX_CHUNKS = 2 * MAX_PAIRS
RING = 6
LAM_INIT = 0.8 - 0.6 * math.exp(-0.3 * 0)
NEG = -1e30

S0_RING = 5
SEQ_ORDER = [0, 4, 1, 5, 2, 6, 3, 7]

LOG_G = np.log1p(-np.exp2(-5.0 - np.arange(H, dtype=np.float64)))


def layout(*fields):
    at, out = 0, {}
    for name, width in fields:
        out[name] = (at, width)
        at += width
    return out, at


GEN, GEN_W = layout(("ident", P), ("before", P), ("ones", P), ("eidx", 3 * N_EXP), ("gidx", 3 * N_GRP),
                    ("cuts", CUTS))
PLN, PLN_W = layout(("earlier", N_EXP * N_EXP), ("seq", MAX_CHUNKS), ("pairs", MAX_PAIRS), ("slots", P))
TBA, TBA_W = layout(("cos", 3 * 8), ("sin", 3 * 8), ("mask", P), ("smask", 4 * N_SAMPLE), ("pair", N_SAMPLE),
                    ("sgn", 2))
TBC, TBC_W = layout(("cos", TOK), ("sin", TOK), ("dec", H * P), ("sdec", H * N_SAMPLE), ("qdec", H * (TOK - P)),
                    ("kdec", 3 * H), ("own", 4))


def host_tables():
    f = np.float32
    p = np.arange(P)
    gen = np.zeros((P, GEN_W), f)

    def put(t, lay, name, a):
        at, w = lay[name]
        t[:, at:at + w] = np.asarray(a, f).reshape(P, w)

    put(gen, GEN, "ident", np.eye(P))
    put(gen, GEN, "before", p[:, None] < p[None, :])
    put(gen, GEN, "ones", np.ones((P, P)))
    put(gen, GEN, "eidx", np.tile(np.arange(N_EXP) - 32.0, (P, 3)))
    put(gen, GEN, "gidx", np.tile(np.arange(N_GRP) - 8.0, (P, 3)))
    put(gen, GEN, "cuts", np.tile(np.arange(CUTS) * float(CHUNK), (P, 1)))
    pln = np.zeros((P, PLN_W), f)
    e = np.arange(N_EXP)
    put(pln, PLN, "earlier", np.tile((e[None, :] < e[:, None]).reshape(1, -1), (P, 1)))
    put(pln, PLN, "seq", np.tile(np.arange(MAX_CHUNKS), (P, 1)))
    put(pln, PLN, "pairs", np.tile(np.arange(MAX_PAIRS) * 2, (P, 1)))
    put(pln, PLN, "slots", np.tile(np.arange(P), (P, 1)))

    pos = np.concatenate([np.arange(N_PROMPT), np.tile(PAST + np.arange(DEC_T), DEC_B)]).astype(f)
    tba = np.zeros((P, TBA_W), f)
    inv = f(500000.0) ** (-np.arange(0, 16, 2, dtype=f) / f(16))
    ang = pos[:, None] * inv[None, :].astype(f)
    ca, sa = np.zeros((3 * P, 8), f), np.zeros((3 * P, 8), f)
    ca[:TOK], sa[:TOK] = np.cos(ang), np.sin(ang)
    put(tba, TBA, "cos", ca.reshape(3, P, 8).transpose(1, 0, 2))
    put(tba, TBA, "sin", sa.reshape(3, P, 8).transpose(1, 0, 2))
    put(tba, TBA, "mask", np.where(p[None, :] <= p[:, None], 0.0, NEG))
    b2, m, q = p // 64, (p // 8) % 8, p % 8
    cb, ct = np.arange(64) // 8, np.arange(64) % 8
    sm = np.stack([np.where((cb[None] == 2 * g + b2[:, None]) & (ct[None] <= q[:, None]), 0.0, NEG) for g in range(4)], 1)
    put(tba, TBA, "smask", sm)
    cols = np.arange(64)
    put(tba, TBA, "pair", (b2[:, None] == cols[None] // 32) & (m[:, None] // 2 == (cols[None] // 8) % 4)
        & (q[:, None] == cols[None] % 8))
    put(tba, TBA, "sgn", np.stack([m % 2 == 0, m % 2 == 1], 1))

    tbc = np.zeros((P, TBC_W), f)
    inv = f(10000.0) ** (-np.linspace(0.0, 1.0, DK_C // 2, dtype=f))
    ang = (pos[:, None] * inv[None, :].astype(f)).astype(f)
    put(tbc, TBC, "cos", np.cos(ang).T)
    put(tbc, TBC, "sin", np.sin(ang).T)
    d = p[None, :] - p[:, None]
    dec = np.stack([np.where(d >= 0, np.exp(np.maximum(d, 0) * LOG_G[h]), 0.0) for h in range(H)], 1)
    put(tbc, TBC, "dec", dec)
    i = np.arange(64)
    ds = i[None, :] % 8 - i[:, None] % 8
    same = i[None, :] // 8 == i[:, None] // 8
    sd = np.zeros((P, H, 64))
    sd[:64] = np.stack([np.where(same & (ds >= 0), np.exp(np.maximum(ds, 0) * LOG_G[h]), 0.0) for h in range(H)], 1)
    put(tbc, TBC, "sdec", sd)
    idx = np.concatenate([p, i % 8])
    put(tbc, TBC, "qdec", np.tile(np.stack([np.exp((idx + 1) * LOG_G[h]) for h in range(H)])[None], (P, 1, 1)))
    kd = np.zeros((P, 3, H))
    for h in range(H):
        kd[:, 0, h] = kd[:, 1, h] = np.exp((P - 1 - p) * LOG_G[h])
        kd[:64, 2, h] = np.exp((DEC_T - 1 - i % 8) * LOG_G[h])
    put(tbc, TBC, "kdec", kd)
    own = np.zeros((P, 4))
    own[:64] = i[:, None] % 32 // 8 == np.arange(4)[None]
    put(tbc, TBC, "own", own)

    entry = np.zeros((P, 3, 2, 4), np.int32)
    tok = np.arange(3)[None, :, None] * P + p[:, None, None]
    entry[..., 1] = np.arange(2)[None, None] * TOK + tok
    empty = np.zeros((P * MAX_PAIRS, 4), np.int32)
    empty[:, 1] = 1 << 20
    return {"gen": gen, "tba": tba, "tbc": tbc, "pln": pln, "entry": entry.reshape(P, 24), "empty": empty}


def build(nc, a, o):
    with ExitStack() as ctx:
        def sb(name, shape, dt=F32):
            return ctx.enter_context(nc.sbuf_tensor(name, [P] + shape, dt))

        def sem(name):
            return ctx.enter_context(nc.semaphore(name))

        y_rows = [nc.dram_tensor(f"y_rows{l}", (2 * TOK, D), F32, kind="Internal").ap() for l in range(2)]
        table = [nc.dram_tensor(f"table{l}", (P * MAX_PAIRS, 4), I32, kind="Internal").ap() for l in range(2)]

        ring = sb("ring", [RING, 4096])
        x = sb("x", [3, D])
        xT = sb("xT", [KD, TOK])
        gen = sb("gen_sb", [GEN_W])
        wr = sb("wr", [KD, N_EXP])
        rbias = sb("rbias", [N_EXP])
        entry = sb("entry_sb", [3, 2, 4], I32)
        stat = sb("stat", [3, 2, 6])
        mv = sb("mv", [3, 2])
        rstd = sb("rstd", [3, 1])
        epsc = sb("epsc", [1])
        rt = sb("rt", [12, 3, N_EXP])
        rs = sb("rs", [12, 3, N_GRP])
        r1 = sb("r1", [12, 3])
        slot_i = sb("slot_i", [3, 2], I32)
        pairs_i = sb("pairs_i", [2], I32)
        slot_pages = sb("slot_pages", [DEC_B * PAGES], I32)
        SCR = 21184
        scratch = sb("scratch", [SCR])
        ps = ctx.enter_context(nc.psum_tensor("ps", [P, 8, 512], F32))

        def carve(*fields):
            at, out = 0, {}
            for name, n, *start in fields:
                s = out[start[0]][1] + (start[1] if len(start) > 1 else 0) if start else at
                out[name] = (scratch[:, s:s + n], s)
                if not start:
                    at += n
            assert at <= SCR, at
            return {k: v[0] for k, v in out.items()}

        A = carve(("qkv", 3 * 1536), ("qT", H * TOK), ("kT", H * TOK), ("up", CC * (HIST + N_PROMPT)),
                  ("us", CC * DEC_B * (HIST + DEC_T)), ("acc", CC * TOK), ("sig", 2 * TOK),
                  ("kp", 2 * PAGES * 512), ("vp", 2 * PAGES * 512), ("QB", 2 * H * 64),
                  ("e", 2 * 512), ("w", 256), ("wT", 256), ("es", TOK), ("wTs", 192),
                  ("ao", DEC_B * DV_A), ("tba", TBA_W), ("subln", DV_A), ("cwT", CC * 32), ("small", 128),
                  ("lam", 4 * DQK),
                  ("kp2", 2 * PAGES * 512, "up"), ("vp2", 2 * PAGES * 512, "up", 2 * PAGES * 512),
                  ("mixT", KD * TOK, "up"),  ("ao2", 1024, "kp"), ("lngb", 2048, "vp"),
                  ("stin", 1024, "ao"), ("clg", 1024, "ao"), ("cwin", 512, "es"), ("uo", 1024, "e"))
        C = carve(("q", 2 * TOK), ("k", 2 * TOK), ("qd", 2 * (TOK - P)), ("v", 3 * DV_C), ("g", 16 * TOK),
                  ("kd", 3 * DK_C), ("kdm", 4 * TOK), ("sc", 2 * P + 64), ("S", 2 * DV_C), ("o", 4 * DV_C),
                  ("s0", S0_RING * 2 * DV_C), ("tbc", TBC_W), ("small", 64),
                  ("tmp", 4 * TOK, "kdm"), ("lngb", 2048, "o"))
        M = carve(("pick", 2 * 3 * P), ("slotf", 6), ("xgT", KD * P), ("sg", D_FF), ("hid", D_FF), ("hidT", 2 * KF * CHUNK), ("y", D),
                  ("tab", MAX_PAIRS * 4), ("pln", PLN_W), ("ptmp", N_EXP * N_EXP), ("ch", 3 * N_EXP), ("sidx", 1), ("done", N_EXP),
                  ("experts", MAX_PAIRS), ("yy", 3 * 2 * D),
                  ("lngb", 2048))

        def gcol(name):
            at, w = GEN[name]
            return gen[:, at:at + w]

        ident, before, ones = gcol("ident"), gcol("before"), gcol("ones")

        def acol(name):
            at, w = TBA[name]
            return A["tba"][:, at:at + w]

        def ccol(name):
            at, w = TBC[name]
            return C["tbc"][:, at:at + w]

        bank_full = [sem(f"bank_full{b}") for b in range(8)]
        bank_read = [sem(f"bank_read{b}") for b in range(8)]
        jobs, turns = {}, [0] * 8

        def plan(name, bank):
            jobs[name] = (bank, turns[bank])
            turns[bank] += 1

        def plan_mixer_a():
            rot = [("xT0", t, i) for t in range(3) for i in range(2)]
            rot += [("a", c) for c in range(CC)] + [("g", c) for c in range(CC)]
            rot += [("cw",), ("st", 0), ("st", 1)]
            rot += [("qkv", n, t) for n in range(2) for t in range(2)] + [("qkv", "qk", 2)] + [("qkv", 2, t) for t in range(3)]
            rot += [("qkT", n, t) for n in range(2) for t in range(3)]
            rot += [("uo", i) for i in range(2)]
            for n, name in enumerate(rot):
                plan(name, n % 8)
            for t in range(3):
                plan(("cvt", t), (2, 3, 7)[t])
            for it in range(9):
                if it < 8:
                    plan(("S", it, 0), 0)
                    plan(("S", it, 1), 1)
                    if it % 2 == 0:
                        for i in range(4):
                            plan(("kpT", it // 2, i), (4, 5, 6, 4)[i])
                        plan(("SS", it // 2), 5)
                    else:
                        plan(("wTs", it // 2), 6)
                        if it % 4 == 1:
                            plan(("AO", it // 4), 7)
                if it >= 1:
                    plan(("wT", it - 1), 2)
                    if (it - 1) % 4 == 0:
                        plan(("O", (it - 1) // 4), 3)
            for i in range(2):
                plan(("att", i), i)
                plan(("aoT", i), 4 + i)
            for t in range(3):
                plan(("cT", t), (2, 6, 7)[t])
            for n in range(2):
                for t in range(3):
                    plan(("out0", n, t), (3, 0, 1, 2, 4, 5)[3 * n + t])

        def plan_mixer_c():
            for h in range(H):
                for i in range(2):
                    for c in range(2):
                        plan(("qk", h, i, c), (3, 4, 5, 2)[2 * i + c])
                plan(("v", h, 2), 0)
                plan(("v", h, 0), 1)
                if h:
                    for e in range(4):
                        plan(("oT", h - 1, e), (6, 7, 3, 4)[e])
                for name, b in ((("sc", h), 5), (("kd", h, 0), 0), (("kd", h, 1), 2), (("gg", h, 0), 6),
                                (("o", h, 2), 1), (("o", h, 3), 7), (("o", h, 0), 0), (("v", h, 1), 2), (("gg", h, 1), 6),
                                (("o", h, 1), 2), (("gg", h, 2), 6), (("gg", h, 3), 6)):
                    plan(name, b)

                def new_states(m):
                    return [("sn", h, m, c, j) for c in range(2) for j in range(2)]

                def both(name):
                    return [(name, h, c) for c in range(2)]

                for n, name in enumerate(new_states(0) + both("S1") + new_states(1) + new_states(2) + both("S2") + new_states(3)):
                    plan(name, 3 + n % 3)
            for e in range(4):
                plan(("oT", H - 1, e), (0, 3, 4, 5)[e])
            for n in range(2):
                for t in range(3):
                    plan(("out1", n, t), (1, 2, 6, 7, 0, 3)[3 * n + t])

        def plan_router(l):
            for n, name in enumerate([("xTm", l, t, i) for t in range(3) for i in range(2)] +
                                     [("lgt", l), ("rank", l)]):
                plan(name, n % 8)

        turns_before_experts = []
        plan_mixer_a()
        plan_router(0)
        turns_before_experts.append(list(turns))
        for n, name in enumerate([("xT1", t, i) for t in range(3) for i in range(2)]):
            plan(name, n)
        plan_mixer_c()
        plan_router(1)
        turns_before_experts.append(list(turns))

        def bank(name):
            return ps[:, jobs[name][0], :]

        def claim(eng, name):
            b, k = jobs[name]
            if k:
                eng.wait_ge(bank_read[b], k)

        def full(name):
            return bank_full[jobs[name][0]]

        def read(name):
            return bank_read[jobs[name][0]]

        def await_full(eng, name):
            eng.wait_ge(bank_full[jobs[name][0]], jobs[name][1] + 1)

        def await_read(eng, name):
            eng.wait_ge(bank_read[jobs[name][0]], jobs[name][1] + 1)

        w_landed = [sem(f"w_landed{s}") for s in range(RING)]
        e_landed = [[sem(f"e_landed{l}_{s}") for s in range(RING)] for l in range(2)]
        last_job = {}
        for n in range(2):
            last_job[0, n] = ("ag"[n], CC - 1)
            last_job[0, 5 + n] = ("out0", n, 2)
            for r in range(2):
                last_job[1, 12 + 2 * n + r] = ("out1", n, 2)
        for n in range(3):
            last_job[0, 2 + n] = ("qkv", 2 if n == 2 else "qk", 2)
        for h in range(H):
            last_job[1, 3 * h] = ("qk", h, 1, 1)
            last_job[1, 3 * h + 1] = ("v", h, 1)
            last_job[1, 3 * h + 2] = ("gg", h, 3)
        loads, landed_at, last_in_slot = {}, [0] * RING, [{}, {}]
        for l, (count, first) in enumerate(((7, 5), (16, 2))):
            for n in range(count):
                s = (first + n) % RING
                landed_at[s] += 32 if l == 1 and n < 12 and n % 3 == 0 else 16
                loads[l, n] = (s, landed_at[s])
                last_in_slot[l][s] = last_job[l, n]

        def w_block(l, n):
            return ring[:, loads[l, n][0], :].rearrange("p (k c) -> p k c", c=512)

        def w_arrived(pe, l, n):
            pe.wait_ge(w_landed[loads[l, n][0]], loads[l, n][1])

        names = """x_in tables_in tba_in lam_in pt_in clg_in empty_in pool_met stored kept_out kv_out
                 dve_step pool_step pads_zero conv_step conv_done rot_step lam_sums lam_exp cn_var
                 cn_std cn_pre cn_post S_bias w_done kp_in0 kp_in1 vp_in0 vp_in1 conv_step_s kp_new
                 QB_set SS_bias ps_done ao_zero ao_read_k att_ss att_std att_done ao_done u_out tbc_in
                 qk_rot kdm_set os_zero on_var on_std sn_done S2_done S2_out g_done ln_in ln_var
                 ln_std x_done lgs_ready lg_exp mask_ready entry_set entries rows_in plan_ready v_half
                 plan_in yy_in0 yy_in1 yy_in2 yy_asked cw_in u_set pe_met""".split()
        S = {n: sem(n) for n in names}
        s0_in = [sem(f"s0_in{i}") for i in range(S0_RING)]
        s0_out = [sem(f"s0_out{i}") for i in range(S0_RING)]
        loop_names = """tab_in sidx_set yb_open pick_halves slots_moved pick_set y_out tr_full xa_done xd_done
                        gu_full silu_done ht_full ht_read y_full hid_done0 hid_done1 ya_done0 ya_done1
                        yd_done0 yd_done1""".split()
        L = [{n: sem(f"{n}_{l}") for n in loop_names} for l in range(2)]

        block = ctx.enter_context(nc.Block())

        qkv = A["qkv"].rearrange("p (t c) -> p t c", t=3)
        qT = A["qT"].rearrange("p (h t) -> p h t", h=H)
        kT = A["kT"].rearrange("p (h t) -> p h t", h=H)
        up = A["up"].rearrange("p (c t) -> p c t", c=CC)
        us = A["us"].rearrange("p (c b t) -> p c b t", c=CC, b=DEC_B)
        acc = A["acc"].rearrange("p (c t) -> p c t", c=CC)
        sig = A["sig"].rearrange("p (i t) -> p i t", i=2)
        un = A["sig"][:, 0:CC * N_SAMPLE].rearrange("p (c t) -> p c t", c=CC)
        kps = [A[n].rearrange("p (b g c) -> p b g c", b=2, g=PAGES) for n in ("kp", "kp2")]
        vps = [A[n].rearrange("p (b g c) -> p b g c", b=2, g=PAGES) for n in ("vp", "vp2")]
        QB = A["QB"].rearrange("p (b h c) -> p b h c", b=2, h=H)
        ebuf = A["e"].rearrange("p (i m k) -> p i m k", i=2, m=2)
        wbuf = A["w"]
        wT = A["wT"].rearrange("p (k q) -> p k q", k=2)
        es = A["es"]
        wTs = A["wTs"].rearrange("p (k c) -> p k c", k=3)
        ao = A["ao"].rearrange("p (b e) -> p b e", b=DEC_B)
        ao2 = A["ao2"].rearrange("p (b e) -> p b e", b=DEC_B)
        cwT = A["cwT"].rearrange("p (c j) -> p c j", c=CC)
        mixT = A["mixT"].rearrange("p (k t) -> p k t", k=KD)
        kpT = xT[:, :, :].rearrange("p (b h) t -> p b h t", b=2)
        uo = A["uo"].rearrange("p (i c) -> p i c", i=2)
        stin = A["stin"].rearrange("p (i c) -> p i c", i=2)
        cwin = A["cwin"]
        lam_in = A["lam"].rearrange("p (i d) -> p i d", i=4)
        sm = A["small"]
        mx, nb, sums = sm[:, 0:2], sm[:, 2:4], sm[:, 4:8].rearrange("p (i m) -> p i m", i=2)
        rr, smx, snb, ssum, srl = sm[:, 8:10], sm[:, 10:11], sm[:, 11:12], sm[:, 12:13], sm[:, 13:14]
        neglam, lamrow, lam2 = sm[:, 14:15], sm[:, 15:16], sm[:, 16:18]
        cvar, cstd = sm[:, 18:24].rearrange("p (t c) -> p t c", t=3), sm[:, 24:27]
        ss_att, rs_att = sm[:, 32:40], sm[:, 40:48]
        ss_ao, rs_ao = sm[:, 48:56], sm[:, 56:64]

        qr = C["q"].rearrange("p (c t) -> p c t", c=2)
        kr = C["k"].rearrange("p (c t) -> p c t", c=2)
        qd = C["qd"].rearrange("p (c t) -> p c t", c=2)
        vh = C["v"].rearrange("p (t e) -> p t e", t=3)
        gT = C["g"].rearrange("p (k t) -> p k t", k=16)
        kd = C["kd"].rearrange("p (t d) -> p t d", t=3)
        kdm = C["kdm"][:, 0:4 * DK_C].rearrange("p (m d) -> p m d", m=4)
        sc = C["sc"]
        St = C["S"].rearrange("p (c e) -> p c e", c=2)
        ob = C["o"].rearrange("p (t e) -> p t e", t=4)
        s0b = C["s0"].rearrange("p (i c e) -> p i c e", i=S0_RING, c=2)
        tmp = C["tmp"].rearrange("p (i t) -> p i t", i=4)
        cm = C["small"]
        ovar, ostd, ostat = cm[:, 0:8].rearrange("p (t c) -> p t c", t=4), cm[:, 8:12], cm[:, 16:40].rearrange("p (t c) -> p t c", t=4)

        pick = M["pick"].rearrange("p (c t s) -> p c t s", c=2, t=3)
        slotf = M["slotf"].rearrange("p (c t) -> p c t", c=2)
        xgT = M["xgT"].rearrange("p (k s) -> p k s", k=KD)
        done_i, experts_i = (M[n].bitcast(I32) for n in ("done", "experts"))
        sidx = M["sidx"].bitcast(I32)
        sg, hid, yb = M["sg"], M["hid"], M["y"]
        hidT = M["hidT"].rearrange("p (i j s) -> p i j s", i=2, j=KF)
        tab = M["tab"].bitcast(I32).rearrange("p (i w) -> p i w", i=MAX_PAIRS)
        tabf = M["tab"].rearrange("p (i w) -> p i w", i=MAX_PAIRS)
        yy = M["yy"].rearrange("p (c t d) -> p c t d", c=2, t=3)
        HALF = [slice(0, CHUNK), slice(CHUNK, P)]
        B_TR, B_GU, B_HT, B_Y = 0, 2, 4, 6

        def cols_a(t):
            return slice(OFF[t], OFF[t] + SZ[t])

        def rows(dram, t0, n):
            return dram[t0:t0 + n, :]

        def bcast(ap, shape):
            return ap.broadcast_to([P] + shape)

        def last_pair(eng, l, back=0):
            eng.wait_ge(S["plan_ready"], l + 1)
            return eng.value_load(pairs_i[0:1, back:back + 1], min_val=2 * TOK // P - 1 - back, max_val=MAX_PAIRS - 1 - back)

        @block.sync
        def _(sp):
            wa = a["w_in_a"][0].rearrange("(p k) c -> p k c", k=KD)
            wo = a["w_out_a"][0].rearrange("(k p) c -> p k c", p=P)
            wc = a["w_in_c"][0].rearrange("(p k) c -> p k c", k=KD)
            woc = a["w_out_c"][0].rearrange("(r k p) c -> r p k c", p=P, r=2)

            def load(l, n, parts):
                if n >= RING:
                    await_full(sp, last_job[l, n - RING])
                for c0, src in parts:
                    dst = w_block(l, n)[:, :, c0:c0 + src.shape[-1]]
                    sp.dma_start(dst, src).then_inc(w_landed[loads[l, n][0]], 16)

            def expert_loads(l, e0, first=False):
                gu = [a["w_e_gate"][l], a["w_e_up"][l]]
                for par in range(2):
                    e = e0 + par
                    if not first:
                        chunks = sp.value_load(done_i[0:1, bass.ds(e - 2, 1)], min_val=1, max_val=MAX_CHUNKS + 1)
                    for j in range(3):
                        s = 3 * par + j
                        if first:
                            await_full(sp, last_in_slot[l][s])
                        else:
                            sp.wait_ge(e_landed[l][s], e0 * 8)
                            sp.wait_ge(L[l][("gu_full", "gu_full", "y_full")[j]], chunks)
                        if j < 2:
                            src = gu[j].rearrange("n (p k) f -> n p (k f)", k=KD)[bass.ds(e, 1)].rearrange("n p f -> (n p) f")
                            dst = ring[:, s, :]
                        else:
                            src = a["w_e_down"][l].rearrange("n (j p) d -> n p j d", p=P)[bass.ds(e, 1)].rearrange("n p j d -> (n p) j d")
                            dst = ring[:, s, :].rearrange("p (j d) -> p j d", j=KF)
                        sp.dma_start(dst, src).then_inc(e_landed[l][s], 16)

            def experts(l):
                expert_loads(l, 0, first=True)
                sp.wait_ge(S["plan_ready"], l + 1)
                with sp.Fori(1, N_EXP // 2) as i:
                    expert_loads(l, i * 2)

            sp.dma_start(x[:, 0:2, :], a["x_prompt"][0].rearrange("(t p) d -> p t d", p=P)).then_inc(S["x_in"], 16)
            sp.dma_start(x[0:64, 2, :], a["x_sample"].rearrange("b t d -> (b t) d")).then_inc(S["x_in"], 16)
            sp.dma_start(gen[:, :], a["gen"]).then_inc(S["x_in"], 16)
            for n, c0 in enumerate((1536, 2048, 0, 512, 1024)):
                load(0, n, [(0, wa[:, :, c0:c0 + 512])])
            for n in range(2):
                load(0, 5 + n, [(0, wo[:, :, n * 512:n * 512 + 512])])
            def load_pages(g):
                for b in range(2):
                    for pg in range(PAGES):
                        page = sp.value_load(slot_pages[0:1, (2 * g + b) * PAGES + pg:(2 * g + b) * PAGES + pg + 1],
                                             min_val=0, max_val=a["cache_k"].shape[1] - 1)
                        for dst, cache, landed in ((kps[g % 2], "cache_k", "kp_in"), (vps[g % 2], "cache_v", "vp_in")):
                            src = a[cache][0].rearrange("n s m d -> n s (m d)")[bass.ds(page, 1)].rearrange("n s c -> (n s) c")
                            sp.dma_start(dst[:, b, pg, :], src).then_inc(S[f"{landed}{g % 2}"], 16)

            sp.wait_ge(S["pt_in"], 16)
            load_pages(0)
            for i in range(2):
                await_read(sp, ("uo", i))
            sp.dma_start(o["conv_prompt"][0, 0], uo[0:HIST, 0, :]).then_inc(S["u_out"], 16)
            for b in range(DEC_B):
                sp.dma_start(o["conv_sample"][0, b, HIST - DEC_T:HIST, :], uo[8 * b:8 * b + 8, 1, :]).then_inc(S["u_out"], 16)
            await_full(sp, ("cvt", 2))
            load_pages(1)
            for g in range(2):
                await_full(sp, ("SS", g))
                await_full(sp, ("wT", 2 * g))
                load_pages(g + 2)
            experts(0)

            def load_c(n):
                h, j = n // 3, n % 3
                if j == 0:
                    load(1, n, [(0, wc[:, :, h * DK_C:(h + 1) * DK_C]), (DK_C, wc[:, :, D + h * DK_C:D + (h + 1) * DK_C])])
                else:
                    c0 = 2 * D + (j - 1) * 2 * D + h * DV_C
                    load(1, n, [(0, wc[:, :, c0:c0 + DV_C])])

            chunks = sp.value_load(done_i[0:1, N_EXP - 2:N_EXP - 1], min_val=1, max_val=MAX_CHUNKS + 1)
            for n in (4, 5, 0):
                s = loads[1, n][0]
                sp.wait_ge(e_landed[0][s], 16 * N_EXP // 2)
                sp.wait_ge(L[0]["gu_full" if s < 2 else "y_full"], chunks)
                load_c(n)
            sp.wait_ge(S["yy_asked"], 1)
            for n in (1, 2, 3):
                sp.wait_ge(e_landed[0][loads[1, n][0]], 16 * N_EXP // 2)
                load_c(n)
            for n in range(RING, 3 * H):
                load_c(n)
            for n in range(2):
                for r in range(2):
                    load(1, 12 + 2 * n + r, [(0, woc[r][:, :, n * 512:n * 512 + 512])])
            experts(1)
            for s in range(RING):
                sp.wait_ge(e_landed[1][s], 16 * N_EXP // 2)
            sp.wait_ge(S["stored"], 16 * 3)
            sp.wait_ge(S["kept_out"], 16)

        def counted(pool, semaphore, value):
            pool.wait_ge(semaphore, value)
            pool.sem_inc(S["pool_met"], 1)

        def experts_pool(pool, l):
            Q = L[l]
            pool.wait_ge(S["entries"], l + 1)
            pool.wait_ge(S["empty_in"], 32)
            for t in range(3):
                for c in range(2):
                    pool.indirect_dma_start(
                        out=table[l], out_offset=bass.IndirectOffsetOnAxis(ap=slot_i[0:SZ[t], t, c:c + 1], axis=0),
                        in_=entry[0:SZ[t], t, c, :], in_offset=None).then_inc(S["rows_in"], 16)
            pool.wait_ge(S["rows_in"], 96 * (l + 1))

            pool.dma_start(tab.rearrange("p i w -> p (i w)"), table[l].rearrange("(p i) w -> p (i w)", i=MAX_PAIRS)).then_inc(Q["tab_in"], 16)
            pool.wait_ge(Q["tab_in"], 16)

            def scatter(i):
                pool.tensor_copy(sidx, tab[:, bass.ds(i, 1), 1]).then_inc(Q["sidx_set"], 1)
                counted(pool, Q["sidx_set"], i + 1)
                for hf in range(2):
                    counted(pool, Q[f"ya_done{hf}"], i + 2)
                    counted(pool, Q[f"yd_done{hf}"], i + 2)
                pool.indirect_dma_start(
                    out=y_rows[l], out_offset=bass.IndirectOffsetOnAxis(ap=sidx, axis=0),
                    in_=yb, in_offset=None, bounds_check=2 * TOK - 1, oob_is_err=False).then_inc(Q["y_out"], 16)
                counted(pool, Q["y_out"], i * 16 + 16)
                pool.sem_inc(Q["yb_open"], 1)

            pool.sem_inc(Q["yb_open"], 1)
            last = last_pair(pool, l)
            with pool.Fori(0, last) as i:
                scatter(i)
            scatter(last)

        @block.gpsimd
        def _(pool):
            steps = [0]

            def link(ins):
                steps[0] += 1
                ins.then_inc(S["pool_step"], 1)
                pool.wait_ge(S["pool_step"], steps[0])

            pool.memset(up[:, :, 0:HIST], 0.0).then_inc(S["pads_zero"], 1)
            pool.memset(QB[:, :, :, :], 0.0).then_inc(S["pads_zero"], 1)
            pool.memset(epsc[:, :], EPS).then_inc(S["pads_zero"], 1)
            pool.memset(mv[:, :, :], 1.0).then_inc(S["pads_zero"], 1)
            pool.memset(rt[:, :, :, :], 0.0).then_inc(S["pads_zero"], 1)
            pool.memset(sm[:, :], 1.0).then_inc(S["pads_zero"], 1)
            await_full(pool, ("a", 0))
            for l in range(2):
                pool.dma_start(table[l], a["empty"]).then_inc(S["empty_in"], 16)
            pool.dma_start(slot_pages[0:1, :], a["page_table"].rearrange("b g -> (b g)").rearrange("(o n) -> o n", o=1)).then_inc(S["pt_in"], 16)
            pool.dma_start(o["conv_sample"][0][:, 0:HIST - DEC_T, :], a["state_conv"][0][:, DEC_T:HIST, :]).then_inc(S["kept_out"], 16)
            await_full(pool, ("cw",))
            await_read(pool, ("cw",))
            pool.wait_ge(S["u_set"], 2 * CC + 1)
            for i in range(2):
                await_read(pool, ("st", i))
            taps = A["w"].rearrange("p (c b t) -> p c b t", c=CC, b=DEC_B), A["wT"].rearrange("p (c b t) -> p c b t", c=CC, b=DEC_B)
            sums_s = acc[:, :, N_PROMPT:].rearrange("p c (b t) -> p c b t", b=DEC_B)
            weight = cwT.unsqueeze(2).unsqueeze(2)
            for j in range(CONV_W):
                pool.tensor_tensor(taps[j % 2], us[:, :, :, j:j + DEC_T], weight[:, :, :, :, j].broadcast_to([P, CC, DEC_B, DEC_T]), ALU.mult).then_inc(S["conv_step_s"], 1)
                pool.wait_ge(S["conv_step_s"], 2 * j + 1)
                other = weight[:, :, :, :, CONV_W].broadcast_to([P, CC, DEC_B, DEC_T]) if j == 0 else sums_s
                pool.tensor_tensor(sums_s, taps[j % 2], other, ALU.add).then_inc(S["conv_step_s"], 1)
                if j:
                    pool.wait_ge(S["conv_step_s"], 2 * j + 2)

            cosA = acol("cos").rearrange("p (t j) -> p t j", t=3)
            sinA = acol("sin").rearrange("p (t j) -> p t j", t=3)
            tr = A["w"].rearrange("p (m j) -> p m j", j=8), A["wT"].rearrange("p (m j) -> p m j", j=8)
            pool.wait_ge(S["tba_in"], 16)
            for t in range(3):
                for n in range(2):
                    await_read(pool, ("qkv", "qk" if t == 2 else n, t))
                z = SZ[t]
                v = qkv[0:z, t, 0:1024].rearrange("p (m d) -> p m d", d=DQK)
                t1, t2 = v[:, :, 0:8], v[:, :, 8:16]
                c8 = cosA[0:z, t, :].unsqueeze(1).broadcast_to([z, 16, 8])
                s8 = sinA[0:z, t, :].unsqueeze(1).broadcast_to([z, 16, 8])
                a1, a2 = tr[0][0:z, 0:16], tr[0][0:z, 16:32]
                b1, b2 = tr[1][0:z, 0:16], tr[1][0:z, 16:32]
                pool.tensor_tensor(a1, t1, c8, ALU.mult)
                pool.tensor_tensor(a2, t2, s8, ALU.mult)
                pool.tensor_tensor(b1, t2, c8, ALU.mult)
                link(pool.tensor_tensor(b2, t1, s8, ALU.mult))
                pool.tensor_tensor(t1, a1, a2, ALU.subtract)
                ins = pool.tensor_tensor(t2, b1, b2, ALU.add)
                ins.then_inc(S["rot_step"], 1)
                pool.wait_ge(S["rot_step"], t + 1)
            kdst = [o["k_prompt"][0, 0].rearrange("(t p) m d -> p t (m d)", p=P), o["k_sample"][0].rearrange("b t m d -> (b t) (m d)")]
            vdst = [o["v_prompt"][0, 0].rearrange("(t p) m d -> p t (m d)", p=P), o["v_sample"][0].rearrange("b t m d -> (b t) (m d)")]
            for t in range(3):
                await_read(pool, ("qkv", 2, t))
            for dst, c0 in ((kdst, 512), (vdst, 1024)):
                pool.dma_start(dst[0], qkv[:, 0:2, c0:c0 + 512]).then_inc(S["kv_out"], 16)
                pool.dma_start(dst[1], qkv[0:64, 2, c0:c0 + 512]).then_inc(S["kv_out"], 16)

            for t in range(3):
                await_read(pool, ("qkT", 0, t))
            for g in range(4):
                if g:
                    await_full(pool, ("SS", g - 1))
                for h in range(H):
                    for half in range(2):
                        hp = slice(64 * half, 64 * half + 64)
                        c0 = 16 * h + 8 * half
                        src = qT[hp, h, 2 * P + 16 * g:2 * P + 16 * g + 16].rearrange("p (b q) -> p b q", b=2)
                        pool.tensor_copy(QB[hp, :, h, c0:c0 + 8], src).then_inc(S["QB_set"], 1)
            def state(dram, b, h):
                return dram[0, b, h].rearrange("(c p) e -> p c e", p=P)

            def load_state(j):
                pool.dma_start(s0b[:, j % S0_RING], state(a["state_ret"], SEQ_ORDER[j % DEC_B], j // DEC_B)).then_inc(s0_in[j % S0_RING], 16)

            pool.wait_ge(S["x_done"], 3)
            for j in range(S0_RING):
                load_state(j)
            experts_pool(pool, 0)
            pool.wait_ge(S["tbc_in"], 16)
            own = ccol("own")
            for h in range(H):
                await_read(pool, ("kd", h, 1))
                kd_src = kd[0:64, 2, :]
                for m in range(4):
                    pool.tensor_scalar(kdm[0:64, m, :], kd_src, own[0:64, m:m + 1], None, ALU.mult).then_inc(S["kdm_set"], 1)
                for b in range(DEC_B):
                    j = h * DEC_B + b
                    pool.wait_ge(S["sn_done"], 2 * DEC_B * h + 4 * (b // 2) + 3 + b % 2)
                    pool.dma_start(state(o["ret_sample"], SEQ_ORDER[b], h), s0b[:, j % S0_RING]).then_inc(s0_out[j % S0_RING], 16)
                    if j >= 1 and j + S0_RING - 1 < H * DEC_B:
                        pool.wait_ge(s0_out[(j - 1) % S0_RING], 16 * ((j - 1) // S0_RING + 1))
                        load_state(j + S0_RING - 1)
                    if b == 6:
                        pool.wait_ge(S["S2_done"], 2 * (h + 1))
                        pool.dma_start(o["ret_prompt"][0, 0, h].rearrange("(c p) e -> p c e", p=P), St).then_inc(S["S2_out"], 16)
            for i in range(S0_RING):
                pool.wait_ge(s0_out[i], 16 * len(range(i, H * DEC_B, S0_RING)))
            pool.wait_ge(S["S2_out"], 16 * H)
            experts_pool(pool, 1)

        def load_norm(act, k, lngb):
            for i, name in enumerate(("ln_g", "ln_b")):
                act.dma_start(lngb[:, i * D:(i + 1) * D], a[name][k // 2, k % 2].partition_broadcast(P)).then_inc(S["ln_in"], 16)

        def root(act, k, t):
            act.wait_ge(S["ln_var"], 3 * k + t + 1)
            act.activation(rstd[0:SZ[t], t, :], mv[0:SZ[t], t, 1:2], ACT.Sqrt, bias=epsc[0:SZ[t], 0:1]).then_inc(S["ln_std"], 1)

        def turned_x(act, name, t):
            for i in range(2):
                await_full(act, name + (t, i))
                act.activation(xT[:, 4 * i:4 * i + 4, cols_a(t)], bank(name + (t, i))[:, 0:4 * SZ[t]].rearrange("p (k t) -> p k t", k=4),
                               ACT.Copy).then_inc(read(name + (t, i)), 1)

        def experts_act(act, l):
            Q = L[l]
            root(act, 2 * l, 0)
            for t in range(3):
                if t < 2:
                    root(act, 2 * l, t + 1)
                turned_x(act, ("xTm", l), t)
            if l == 1:
                act.wait_ge(S["S2_out"], 16 * H)
            act.wait_ge(S["x_done"], 6 * l + 3)
            load_norm(act, 2 * l + 1, M["lngb"])
            act.dma_start(M["pln"], a["pln"]).then_inc(S["plan_in"], 16)
            if l == 0:
                act.dma_start(C["tbc"], a["tbc"]).then_inc(S["tbc_in"], 16)
            act.wait_ge(S["lgs_ready"], l + 1)
            act.activation(rt[:, 1, :, :], rt[:, 0, :, :], ACT.Exp).then_inc(S["lg_exp"], 1)

            def turned(i):
                act.wait_ge(Q["tr_full"], i + 1)
                act.activation(xgT[:, 0:4, :], ps[:, B_TR, :].rearrange("p (k s) -> p k s", k=4), ACT.Copy).then_inc(Q["xa_done"], 1)

            def swish(i, hf):
                act.wait_ge(Q["gu_full"], i * 2 + (hf + 2))
                act.activation(sg[HALF[hf], :], ps[HALF[1 - hf], B_GU + hf, :], ACT.Silu).then_inc(Q["silu_done"], 1)

            def hidden(i, hf):
                act.wait_ge(Q["ht_full"], i * 2 + (hf + 1))
                act.activation(hidT[:, hf, :, :], ps[:, B_HT + hf, 0:KF * CHUNK].rearrange("p (j s) -> p j s", j=KF), ACT.Copy).then_inc(Q["ht_read"], 1)

            def result(i, hf):
                act.wait_ge(Q["y_full"], i * 2 + (hf + 2))
                act.wait_ge(Q["yb_open"], i + 1)
                act.activation(yb[HALF[hf], 0:512], ps[HALF[hf], B_Y + hf, :], ACT.Copy).then_inc(Q[f"ya_done{hf}"], 1)

            for hf in range(2):
                act.sem_inc(Q[f"ya_done{hf}"], 1)
            last = last_pair(act, l)
            turned(0)
            swish(0, 0)
            hidden(0, 0)
            with act.Fori(0, last) as i:
                swish(i, 1)
                result(i, 0)
                turned(i + 1)
                hidden(i, 1)
                swish(i + 1, 0)
                result(i, 1)
                hidden(i + 1, 0)
            swish(last, 1)
            result(last, 0)
            hidden(last, 1)
            result(last, 1)
            act.wait_ge(Q["y_out"], last * 16 + 16)
            for t in range(3):
                for c in range(2):
                    act.dma_start(yy[0:SZ[t], c, t, :], y_rows[l][c * TOK + OFF[t]:c * TOK + OFF[t] + SZ[t], :]).then_inc(S[f"yy_in{t}"], 16)
            act.sem_inc(S["yy_asked"], 1)
            if l == 1:
                root(act, 3, 0)
                for t in range(3):
                    if t < 2:
                        root(act, 3, t + 1)
                    act.wait_ge(S["x_done"], 9 + t + 1)
                    dst = o["y_sample"].rearrange("b t d -> (b t) d") if t == 2 else o["y_prompt"][0][t * P:(t + 1) * P, :]
                    act.dma_start(dst, x[0:SZ[t], t, :]).then_inc(S["stored"], 16)
                act.wait_ge(S["kv_out"], 64)

        @block.scalar
        def _(act):
            act.dma_start(cwin[0:CONV_W, :], a["conv_w"][0]).then_inc(S["cw_in"], 16)
            act.dma_start(cwin[CONV_W:CONV_W + 1, :], a["conv_b"]).then_inc(S["cw_in"], 16)
            for i in range(2):
                act.dma_start(stin[0:120, i, :], a["state_conv"][0, 4 * i:4 * i + 4].rearrange("b w c -> (b w) c")).then_inc(S["cw_in"], 16)
            act.dma_start(A["tba"], a["tba"]).then_inc(S["tba_in"], 16)
            act.dma_start(lam_in, a["lambda_a"][0].partition_broadcast(P)).then_inc(S["lam_in"], 16)
            act.dma_start(A["subln"], a["subln_a"][0].partition_broadcast(P)).then_inc(S["lam_in"], 16)
            act.dma_start(wr[:, :, :], a["w_router"].rearrange("(p k) e -> p k e", k=KD)).then_inc(S["tables_in"], 16)
            act.dma_start(rbias[:, :], a["b_router"].partition_broadcast(P)).then_inc(S["tables_in"], 16)
            act.dma_start(entry[:, :, :, :].rearrange("p t c w -> p (t c w)"), a["entry"]).then_inc(S["tables_in"], 16)

            for t in range(3):
                await_full(act, ("xT0", t, 0))
                act.activation(xT[:, 0:4, cols_a(t)], bank(("xT0", t, 0))[:, 0:4 * SZ[t]].rearrange("p (k t) -> p k t", k=4),
                               ACT.Copy).then_inc(read(("xT0", t, 0)), 1)
            act.wait_ge(S["lam_sums"], 1)
            act.activation(lam2, rr, ACT.Exp).then_inc(S["lam_exp"], 1)
            for c in range(CC):
                await_full(act, ("g", c))
                if c >= 2:
                    act.wait_ge(S["u_set"], 2 * (c - 1))
                act.activation(sig[:, c % 2, :], bank(("g", c))[:, 0:TOK], ACT.Sigmoid).then_inc(read(("g", c)), 1)
            for i in range(2):
                await_full(act, ("st", i))
                act.activation(us[:, :, 4 * i:4 * i + 4, 0:HIST],
                               bank(("st", i))[:, 0:480].rearrange("p (c b w) -> p c b w", c=CC, b=4), ACT.Copy).then_inc(read(("st", i)), 1)
            act.dma_start(A["clg"][:, 0:512], a["conv_ln_g"][0].partition_broadcast(P)).then_inc(S["clg_in"], 16)
            act.dma_start(A["clg"][:, 512:1024], a["conv_ln_b"][0].partition_broadcast(P)).then_inc(S["clg_in"], 16)
            for n in range(3):
                for t in range(3 if n == 2 else 2):
                    await_full(act, ("qkv", n, t))
                    act.activation(qkv[0:SZ[t], t, n * 512:n * 512 + 512], bank(("qkv", n, t))[0:SZ[t], :], ACT.Copy).then_inc(read(("qkv", n, t)), 1)
                if n == 1:
                    j = ("qkv", "qk", 2)
                    await_full(act, j)
                    act.activation(qkv[0:64, 2, 0:512], bank(j)[0:64, :], ACT.Copy)
                    act.activation(qkv[0:64, 2, 512:1024], bank(j)[64:128, :], ACT.Copy).then_inc(read(j), 1)
            for n, dst in enumerate((qT, kT)):
                for t in range(3):
                    await_full(act, ("qkT", n, t))
                    act.activation(dst[:, :, cols_a(t)], bank(("qkT", n, t))[:, 0:4 * SZ[t]].rearrange("p (k t) -> p k t", k=4),
                                   ACT.Copy).then_inc(read(("qkT", n, t)), 1)
            for i, r in enumerate((HIST, 64)):
                await_full(act, ("uo", i))
                act.activation(uo[0:r, i, :], bank(("uo", i))[0:r, :], ACT.Copy).then_inc(read(("uo", i)), 1)
                await_read(act, ("uo", i))
            for t in range(3):
                await_full(act, ("cvt", t))
                await_full(act, ("qkT", 0, t))
                act.activation(qkv[0:SZ[t], t, 0:512], bank(("cvt", t))[0:SZ[t], :], ACT.Copy).then_inc(read(("cvt", t)), 1)
            act.wait_ge(S["cn_var"], 3)
            act.activation(cstd, cvar[:, :, 1], ACT.Sqrt, bias=epsc[:, 0:1]).then_inc(S["cn_std"], 1)
            for it in range(9):
                g = it // 2
                if it < 8:
                    if it == 0:
                        act.wait_ge(S["u_out"], 16 * 9)
                    n = (it // 4 + 1) * P
                    if it % 2 == 0:
                        for i in (0, 2):
                            await_full(act, ("kpT", g, i))
                            act.activation(kpT[:, i // 2, :, (i % 2) * P:(i % 2) * P + P],
                                           bank(("kpT", g, i)).rearrange("p (h t) -> p h t", h=H), ACT.Copy).then_inc(read(("kpT", g, i)), 1)
                    act.wait_ge(S["S_bias"], it + 1)
                    if it >= 2:
                        act.wait_ge(S["w_done"], it - 1)
                    for m in range(2):
                        act.activation(ebuf[:, it % 2, m, 0:n], bank(("S", it, m))[:, 0:n], ACT.Exp, bias=nb[:, m:m + 1],
                                       scale=DQK ** -0.5, accum_out=sums[:, it % 2, m:m + 1]).then_inc(read(("S", it, m)), 1)
                    if it % 2 == 0:
                        act.wait_ge(S["SS_bias"], g + 1)
                        act.activation(es, bank(("SS", g))[:, 0:TOK], ACT.Exp, bias=snb, scale=DQK ** -0.5,
                                       accum_out=ssum).then_inc(read(("SS", g)), 1)
                    else:
                        await_full(act, ("wTs", g))
                        act.activation(wTs[:, 0:2, :], bank(("wTs", g))[:, 0:128].rearrange("p (k c) -> p k c", k=2), ACT.Copy)
                        act.activation(wTs[0:64, 2, :], bank(("wTs", g))[0:64, 128:192], ACT.Copy).then_inc(read(("wTs", g)), 1)
                if it == 5:
                    for t in range(3):
                        act.wait_ge(S["cn_pre"], t + 1)
                        act.activation(qkv[0:SZ[t], t, 0:512], qkv[0:SZ[t], t, 0:512], ACT.Silu).then_inc(S["cn_post"], 1)
                if it >= 1:
                    n = ((it - 1) // 4 + 1)
                    await_full(act, ("wT", it - 1))
                    act.activation(wT[:, 0:n, :], bank(("wT", it - 1))[:, 0:n * P].rearrange("p (k q) -> p k q", k=n), ACT.Copy).then_inc(read(("wT", it - 1)), 1)
            load_norm(act, 0, A["lngb"])
            for i in range(2):
                await_read(act, ("O", i))
                for h in range(H):
                    act.activation(wbuf[:, 0:P], qkv[:, i, 512 + h * P:512 + h * P + P], ACT.Square,
                                   accum_out=ss_att[:, 4 * i + h:4 * i + h + 1]).then_inc(S["att_ss"], 1)
                    act.wait_ge(S["att_ss"], 4 * i + h + 1)
            act.wait_ge(S["ao_read_k"], 1)
            act.activation(rs_att, ss_att, ACT.Sqrt, bias=epsc[:, 0:1], scale=1.0 / DV_A).then_inc(S["att_std"], 1)
            act.activation(rs_ao, ss_ao, ACT.Sqrt, bias=epsc[:, 0:1], scale=1.0 / DV_A).then_inc(S["att_std"], 1)
            for i in range(2):
                await_full(act, ("att", i))
                act.activation(mixT[:, 0:4, cols_a(i)], bank(("att", i)).rearrange("p (h t) -> p h t", h=H), ACT.Copy).then_inc(read(("att", i)), 1)
                await_full(act, ("aoT", i))
                for h in range(H):
                    src = bank(("aoT", i)).rearrange("p (b h r) -> p b h r", b=4, h=H)[:, :, h, 0:8]
                    ins = act.activation(mixT[:, h, 2 * P + 32 * i:2 * P + 32 * i + 32].rearrange("p (b q) -> p b q", b=4), src, ACT.Copy)
                ins.then_inc(read(("aoT", i)), 1)
            for t in range(3):
                await_full(act, ("cT", t))
                act.activation(mixT[:, 4:8, cols_a(t)], bank(("cT", t))[:, 0:4 * SZ[t]].rearrange("p (k t) -> p k t", k=4), ACT.Copy).then_inc(read(("cT", t)), 1)
            experts_act(act, 0)

            root(act, 1, 0)
            for t in range(3):
                if t < 2:
                    root(act, 1, t + 1)
                turned_x(act, ("xT1",), t)
            act.wait_ge(S["tbc_in"], 16)
            kdec = ccol("kdec").rearrange("p (t h) -> p t h", t=3)

            def swish_gate(h, c):
                await_full(act, ("gg", h, c))
                act.activation(gT[:, 4 * h + c, :], bank(("gg", h, c))[:, 0:TOK], ACT.Silu).then_inc(read(("gg", h, c)), 1)

            for h in range(H):
                def values(t):
                    await_full(act, ("v", h, t))
                    act.activation(vh[0:SZ[t], t, :], bank(("v", h, t))[0:SZ[t], :], ACT.Copy).then_inc(read(("v", h, t)), 1)

                await_full(act, ("v", h, 2))
                if h:
                    act.wait_ge(S["sn_done"], 16 * h)
                act.activation(vh[0:64, 2, :], bank(("v", h, 2))[0:64, :], ACT.Copy).then_inc(S["v_half"], 1)
                values(0)
                await_full(act, ("kd", h, 0))
                for t in range(2):
                    ins = act.activation(kd[:, t, :], bank(("kd", h, 0))[:, t * 256:t * 256 + 256], ACT.Copy, scale=kdec[:, t, h:h + 1])
                ins.then_inc(read(("kd", h, 0)), 1)
                await_full(act, ("kd", h, 1))
                act.activation(kd[0:64, 2, :], bank(("kd", h, 1))[0:64, 0:256], ACT.Copy, scale=kdec[0:64, 2, h:h + 1]).then_inc(read(("kd", h, 1)), 1)
                swish_gate(h, 0)
                values(1)
                swish_gate(h, 1)
                act.wait_ge(S["on_var"], 2 * h + 1)
                act.activation(ostd[:, 0:2], ovar[:, 0:2, 1], ACT.Sqrt, bias=epsc[:, 0:1]).then_inc(S["on_std"], 1)
                swish_gate(h, 2)
                swish_gate(h, 3)
                act.wait_ge(S["on_var"], 2 * h + 2)
                act.activation(ostd[:, 2:4], ovar[:, 2:4, 1], ACT.Sqrt, bias=epsc[:, 0:1]).then_inc(S["on_std"], 1)
            await_full(act, ("oT", H - 1, 3))
            load_norm(act, 2, C["lngb"])
            experts_act(act, 1)

        def tile_norm(dve, link, k, lngb, t):
            z = SZ[t]
            dve.bn_aggr(mv[0:z, t, :], stat[0:z, t, :, :].rearrange("p i s -> p (i s)")).then_inc(S["ln_var"], 1)
            dve.wait_ge(S["ln_var"], 3 * k + t + 1)
            dve.wait_ge(S["ln_in"], 32 * (k + 1))
            xs = x[0:z, t, :]
            link(dve.scalar_tensor_tensor(xs, xs, mv[0:z, t, 0:1], lngb[0:z, 0:D], ALU.subtract, ALU.mult))
            dve.wait_ge(S["ln_std"], 3 * k + t + 1)
            link(dve.reciprocal(rstd[0:z, t, :], rstd[0:z, t, :]))
            dve.scalar_tensor_tensor(xs, xs, rstd[0:z, t, :], lngb[0:z, D:2 * D], ALU.mult, ALU.add).then_inc(S["x_done"], 1)

        def residual(dve, link, name, k, lngb):
            for n in range(2):
                for t in range(3):
                    z = SZ[t]
                    j = name + (n, t)
                    await_full(dve, j)
                    xs = x[0:z, t, n * 512:n * 512 + 512]
                    if t < 2:
                        dve.scalar_tensor_tensor(xs, xs, ALPHA, bank(j), ALU.mult, ALU.add).then_inc(read(j), 1)
                    else:
                        link(dve.scalar_tensor_tensor(xs, xs, ALPHA, bank(j)[HALF[0], :], ALU.mult, ALU.add))
                        dve.tensor_tensor(xs, xs, bank(j)[HALF[1], :], ALU.add).then_inc(read(j), 1)
                    await_read(dve, j)
                    link(dve.bn_stats(stat[0:z, t, n, :], xs))
                    if n == 1:
                        tile_norm(dve, link, k, lngb, t)

        def experts_dve(dve, link, l):
            Q = L[l]
            T3, T4 = [3, N_EXP], [3, N_GRP]
            lg, ex, probs, sel, sel2, oh1, sel3, oh2, both, w1, rank, t9 = (rt[:, i, :, :] for i in range(12))

            def col(i):
                return r1[:, i, :]

            def wide(ap, n=N_EXP):
                return ap.unsqueeze(2).broadcast_to([P, 3, n])

            await_full(dve, ("lgt", l))
            lb = bank(("lgt", l))
            dve.tensor_copy(lg[:, 0:2, :], lb[:, 0:32].rearrange("p (t e) -> p t e", t=2))
            dve.tensor_copy(lg[0:64, 2, :], lb[0:64, 32:48]).then_inc(read(("lgt", l)), 1)
            await_read(dve, ("lgt", l))
            link(dve.tensor_reduce(col(0), lg, X, ALU.max))
            dve.tensor_tensor(lg, lg, wide(col(0)), ALU.subtract).then_inc(S["lgs_ready"], 1)
            dve.wait_ge(S["lg_exp"], l + 1)
            link(dve.tensor_reduce(col(1), ex, X, ALU.add))
            link(dve.reciprocal(col(1), col(1)))
            link(dve.tensor_tensor(probs, ex, wide(col(1)), ALU.mult))
            dve.wait_ge(S["tables_in"], 48)
            link(dve.tensor_tensor(sel, probs, rbias[:, :].unsqueeze(1).broadcast_to([P] + T3), ALU.add))
            g4 = sel.rearrange("p t (g j) -> p t g j", j=PER_GRP)
            m1, n1, m2, n2, top, mm, nn, sec, gs, eq, oh, pen = (rs[:, i, :, :] for i in range(12))
            dve.tensor_tensor(m1, g4[:, :, :, 0], g4[:, :, :, 1], ALU.max)
            dve.tensor_tensor(n1, g4[:, :, :, 0], g4[:, :, :, 1], ALU.min)
            dve.tensor_tensor(m2, g4[:, :, :, 2], g4[:, :, :, 3], ALU.max)
            link(dve.tensor_tensor(n2, g4[:, :, :, 2], g4[:, :, :, 3], ALU.min))
            dve.tensor_tensor(top, m1, m2, ALU.max)
            dve.tensor_tensor(mm, m1, m2, ALU.min)
            link(dve.tensor_tensor(nn, n1, n2, ALU.max))
            link(dve.tensor_tensor(sec, mm, nn, ALU.max))
            link(dve.tensor_tensor(gs, top, sec, ALU.add))
            gidx = gcol("gidx").rearrange("p (t g) -> p t g", t=3)
            eidx = gcol("eidx").rearrange("p (t e) -> p t e", t=3)
            link(dve.tensor_reduce(col(2), gs, X, ALU.max))
            link(dve.tensor_tensor(eq, gs, wide(col(2), N_GRP), ALU.is_equal))
            link(dve.tensor_tensor(eq, eq, gidx, ALU.mult))
            link(dve.tensor_reduce(col(3), eq, X, ALU.min))
            link(dve.tensor_tensor(oh, gidx, wide(col(3), N_GRP), ALU.is_equal))
            link(dve.tensor_scalar(pen, oh, 1.0, -NEG, ALU.subtract, ALU.mult))
            s2 = sel2.rearrange("p t (g j) -> p t g j", j=PER_GRP)
            link(dve.tensor_tensor(s2, g4, pen.unsqueeze(3).broadcast_to([P, 3, N_GRP, PER_GRP]), ALU.add))

            def best(src, dst, c):
                link(dve.tensor_reduce(col(c), src, X, ALU.max))
                link(dve.tensor_tensor(t9, src, wide(col(c)), ALU.is_equal))
                link(dve.tensor_tensor(t9, t9, eidx, ALU.mult))
                link(dve.tensor_reduce(col(c), t9, X, ALU.min))
                link(dve.tensor_tensor(dst, eidx, wide(col(c)), ALU.is_equal))

            best(sel2, oh1, 4)
            link(dve.scalar_tensor_tensor(sel3, oh1, 3 * NEG, sel2, ALU.mult, ALU.add))
            best(sel3, oh2, 5)
            dve.tensor_tensor(both, oh1, oh2, ALU.add).then_inc(S["mask_ready"], 1)
            for c, hot in ((6, oh1), (7, oh2)):
                link(dve.tensor_tensor(w1, hot, probs, ALU.mult))
                link(dve.tensor_reduce(col(c), w1, X, ALU.add))
            link(dve.tensor_tensor(col(8), col(6), col(7), ALU.add))
            link(dve.reciprocal(col(8), col(8)))
            if l:
                dve.wait_ge(S["rows_in"], 96)
            ef = entry[:, :, :, :].bitcast(F32)
            for c in range(2):
                dve.tensor_tensor(ef[:, :, c, 2], col(6 + c), col(8), ALU.mult).then_inc(S["entry_set"], 1)
            await_full(dve, ("rank", l))
            rb = bank(("rank", l))
            dve.wait_ge(S["plan_in"], 16 * (l + 1))
            pt, ch, first_ch, end_ch = M["ptmp"], M["ch"][:, 0:N_EXP], M["ch"][:, N_EXP:2 * N_EXP], M["ch"][:, 2 * N_EXP:]

            def pcol(name):
                at, w = PLN[name]
                return M["pln"][:, at:at + w]

            many = pt[:, 0:N_EXP * CUTS].rearrange("p (e k) -> p e k", e=N_EXP)
            link(dve.tensor_tensor(many, rb[:, 48:64].unsqueeze(2).broadcast_to([P, N_EXP, CUTS]),
                                   gcol("cuts").unsqueeze(1).broadcast_to([P, N_EXP, CUTS]), ALU.is_gt))
            link(dve.tensor_reduce(ch, many, X, ALU.add))
            before_e = pt.rearrange("p (e f) -> p e f", e=N_EXP)
            link(dve.tensor_tensor(before_e, ch.unsqueeze(1).broadcast_to([P, N_EXP, N_EXP]),
                                   pcol("earlier").rearrange("p (e f) -> p e f", e=N_EXP), ALU.mult))
            link(dve.tensor_reduce(first_ch, before_e, X, ALU.add))
            dve.tensor_tensor(end_ch, first_ch, ch, ALU.add)
            dve.scalar_tensor_tensor(rank[:, 0:2, :], rb[:, 0:32].rearrange("p (t e) -> p t e", t=2), 1.0 / CHUNK,
                                     first_ch.unsqueeze(1).broadcast_to([P, 2, N_EXP]), ALU.mult, ALU.add)
            link(dve.scalar_tensor_tensor(rank[0:64, 2, :], rb[0:64, 32:48], 1.0 / CHUNK, first_ch[0:64, :], ALU.mult, ALU.add))
            dve.sem_inc(read(("rank", l)), 1)
            for c, hot in ((9, oh1), (10, oh2)):
                link(dve.tensor_tensor(w1, hot, rank, ALU.mult))
                link(dve.tensor_reduce(col(c), w1, X, ALU.add))
            flat = r1[:, 9:11, :]
            link(dve.tensor_scalar(slotf, flat, float(CHUNK), None, ALU.mult))

            def pick_rows(n, first=False):
                if not first:
                    dve.wait_ge(Q["slots_moved"], n)
                    dve.wait_ge(Q["pick_set"], n)
                dve.tensor_tensor(pick, slotf.unsqueeze(3).broadcast_to([P, 2, 3, P]),
                                  pcol("slots").unsqueeze(1).unsqueeze(1).broadcast_to([P, 2, 3, P]), ALU.is_equal).then_inc(Q["pick_halves"], 1)
                dve.wait_ge(Q["pick_halves"], n + 1)
                dve.tensor_scalar(slotf, slotf, float(P), None, ALU.subtract).then_inc(Q["slots_moved"], 1)
                dve.tensor_tensor(pick[:, 0], pick[:, 0], pick[:, 1], ALU.add).then_inc(Q["pick_set"], 1)

            pick_rows(0, first=True)
            passed = pt[:, 0:6 * MAX_PAIRS].rearrange("p (c t i) -> p c t i", c=2, t=3)
            pair = r1[:, 6:8, :]
            link(dve.tensor_tensor(passed, flat.unsqueeze(3).broadcast_to([P, 2, 3, MAX_PAIRS]),
                                   pcol("pairs").unsqueeze(1).unsqueeze(1).broadcast_to([P, 2, 3, MAX_PAIRS]), ALU.is_ge))
            link(dve.tensor_reduce(pair, passed, X, ALU.add))
            link(dve.tensor_scalar(pair, pair, 1.0, 1.0 - P * MAX_PAIRS, ALU.subtract, ALU.mult))
            link(dve.scalar_tensor_tensor(flat, flat, float(CHUNK * MAX_PAIRS), pair, ALU.mult, ALU.add))
            for c in range(2):
                dve.tensor_copy(slot_i[:, :, c], col(9 + c)).then_inc(S["entry_set"], 1)
            dve.wait_ge(S["entry_set"], 4 * (l + 1))
            dve.sem_inc(S["entries"], 1)
            dve.tensor_scalar(done_i, end_ch, 1.0, None, ALU.add)
            past = pt[:, 0:MAX_CHUNKS * 8].rearrange("p (c j) -> p c j", j=8)
            wide_w = w1.rearrange("p t e -> p (t e)")[:, 0:MAX_CHUNKS]
            halves = []
            for q in range(2):
                half = (wide_w, t9.rearrange("p t e -> p (t e)")[:, 0:MAX_CHUNKS])[q]
                link(dve.tensor_tensor(past, end_ch[:, 8 * q:8 * q + 8].unsqueeze(1).broadcast_to([P, MAX_CHUNKS, 8]),
                                       pcol("seq").unsqueeze(2).broadcast_to([P, MAX_CHUNKS, 8]), ALU.is_le))
                link(dve.tensor_reduce(half, past, X, ALU.add))
                halves.append(half)
            link(dve.tensor_tensor(halves[0], halves[0], halves[1], ALU.add))
            own = halves[1]
            link(dve.tensor_scalar(own, halves[0], N_EXP - 1.0, None, ALU.min))
            ev, od = (own.rearrange("p (i q) -> p q i", q=2)[:, q, :] for q in range(2))
            code = wide_w[:, 0:MAX_PAIRS]
            link(dve.scalar_tensor_tensor(code, od, float(N_EXP), ev, ALU.mult, ALU.add))
            link(dve.scalar_tensor_tensor(code[:, 0:MAX_PAIRS - 1], ev[:, 1:MAX_PAIRS], float(N_EXP ** 2), code[:, 0:MAX_PAIRS - 1], ALU.mult, ALU.add))
            dve.tensor_copy(experts_i, code)
            some = pt[:, 0:MAX_PAIRS]
            link(dve.tensor_scalar(some, pcol("pairs"), end_ch[:, N_EXP - 1:N_EXP], None, ALU.is_lt))
            link(dve.tensor_reduce(r1[:, 11, 1:2], some, X, ALU.add))
            link(dve.tensor_scalar(pairs_i[:, 1:2], r1[:, 11, 1:2], -2.0, None, ALU.add))
            dve.tensor_scalar(pairs_i[:, 0:1], r1[:, 11, 1:2], -1.0, None, ALU.add).then_inc(S["plan_ready"], 1)

            def turned(i):
                dve.wait_ge(Q["tr_full"], i + 1)
                dve.tensor_copy(xgT[:, 4:8, :], ps[:, B_TR + 1, :].rearrange("p (k s) -> p k s", k=4)).then_inc(Q["xd_done"], 1)

            def hidden(i, hf):
                dve.wait_ge(Q["silu_done"], i * 2 + (hf + 1))
                dve.wait_ge(Q["tab_in"], 16)
                dve.scalar_tensor_tensor(hid[HALF[hf], :], sg[HALF[hf], :], tabf[HALF[hf], bass.ds(i, 1), 2],
                                         ps[HALF[hf], B_GU + hf, :], ALU.mult, ALU.mult).then_inc(Q[f"hid_done{hf}"], 1)

            def result(i, hf):
                dve.wait_ge(Q["y_full"], i * 2 + (hf + 2))
                dve.wait_ge(Q["yb_open"], i + 1)
                dve.tensor_copy(yb[HALF[hf], 512:1024], ps[HALF[1 - hf], B_Y + hf, :]).then_inc(Q[f"yd_done{hf}"], 1)

            for hf in range(2):
                dve.sem_inc(Q[f"yd_done{hf}"], 1)
                dve.sem_inc(Q[f"hid_done{hf}"], 1)
            last = last_pair(dve, l)
            turned(0)
            pick_rows(1)
            hidden(0, 0)
            with dve.Fori(0, last) as i:
                hidden(i, 1)
                result(i, 0)
                turned(i + 1)
                pick_rows(i + 2)
                hidden(i + 1, 0)
                result(i, 1)
            hidden(last, 1)
            result(last, 0)
            result(last, 1)
            for t in range(3):
                z = SZ[t]
                dve.wait_ge(S[f"yy_in{t}"], 32 * (l + 1))
                link(dve.scalar_tensor_tensor(x[0:z, t, :], x[0:z, t, :], ALPHA, yy[0:z, 0, t, :], ALU.mult, ALU.add))
                link(dve.tensor_tensor(x[0:z, t, :], x[0:z, t, :], yy[0:z, 1, t, :], ALU.add))
                dve.bn_stats(stat[0:z, t, 0, :], x[0:z, t, 0:512])
                link(dve.bn_stats(stat[0:z, t, 1, :], x[0:z, t, 512:1024]))
                tile_norm(dve, link, 2 * l + 1, M["lngb"], t)

        @block.vector
        def _(dve):
            steps = [0]

            def link(ins):
                steps[0] += 1
                ins.then_inc(S["dve_step"], 1)
                dve.wait_ge(S["dve_step"], steps[0])

            def half_of_xT(name, dst):
                for t in range(3):
                    await_full(dve, name + (t, 1))
                    dve.tensor_copy(dst[:, 4:8, cols_a(t)], bank(name + (t, 1))[:, 0:4 * SZ[t]].rearrange("p (k t) -> p k t", k=4)).then_inc(read(name + (t, 1)), 1)

            half_of_xT(("xT0",), xT)
            dve.wait_ge(S["lam_in"], 32)
            dve.wait_ge(S["pads_zero"], 6)
            dve.tensor_scalar(A["subln"], A["subln"], 1.0 - LAM_INIT, None, ALU.mult)
            lp = lam_in.rearrange("p (i j) d -> p i j d", i=2)
            link(dve.tensor_tensor(lp[:, :, 0, :], lp[:, :, 0, :], lp[:, :, 1, :], ALU.mult))
            dve.tensor_reduce(rr, lp[:, :, 0, :], X, ALU.add).then_inc(S["lam_sums"], 1)
            dve.wait_ge(S["lam_exp"], 1)
            link(dve.tensor_tensor(neglam, lam2[:, 1:2], lam2[:, 0:1], ALU.subtract))
            link(dve.tensor_scalar(neglam, neglam, -LAM_INIT, None, ALU.add))
            dve.wait_ge(S["tba_in"], 16)
            sgn = acol("sgn")
            link(dve.scalar_tensor_tensor(lamrow, sgn[:, 1:2], neglam, sgn[:, 0:1], ALU.mult, ALU.add))

            for c in range(CC):
                await_full(dve, ("a", c))
                await_read(dve, ("g", c))
                ab = bank(("a", c))
                dve.tensor_tensor(up[:, c, HIST:], ab[:, 0:N_PROMPT], sig[:, c % 2, 0:N_PROMPT], ALU.mult).then_inc(S["u_set"], 1)
                dve.tensor_tensor(us[:, c, :, HIST:], ab[:, N_PROMPT:TOK].rearrange("p (b t) -> p b t", b=DEC_B),
                                  sig[:, c % 2, N_PROMPT:].rearrange("p (b t) -> p b t", b=DEC_B), ALU.mult).then_inc(S["u_set"], 1)
                dve.wait_ge(S["u_set"], 2 * c + 2)
                dve.sem_inc(read(("a", c)), 1)
            dve.tensor_copy(un.rearrange("p c (b t) -> p c b t", b=DEC_B), us[:, :, :, HIST:]).then_inc(S["u_set"], 1)
            await_full(dve, ("cw",))
            dve.tensor_copy(cwT, bank(("cw",))[:, 0:128].rearrange("p (c j) -> p c j", c=CC)).then_inc(read(("cw",)), 1)
            await_read(dve, ("cw",))
            for i in range(2):
                await_read(dve, ("st", i))
            n = 0
            for j in range(CONV_W):
                for c in range(CC):
                    ext, out = up[:, c, j:j + N_PROMPT], acc[:, c, 0:N_PROMPT]
                    if j == 0:
                        ins = dve.tensor_scalar(out, ext, cwT[:, c, 0:1], cwT[:, c, CONV_W:CONV_W + 1], ALU.mult, ALU.add)
                    else:
                        dve.wait_ge(S["conv_step"], n - CC + 1)
                        ins = dve.scalar_tensor_tensor(out, ext, cwT[:, c, j:j + 1], out, ALU.mult, ALU.add)
                    ins.then_inc(S["conv_step"], 1)
                    n += 1
            dve.wait_ge(S["conv_step"], n)
            dve.sem_inc(S["conv_done"], 1)
            for t in range(3):
                await_full(dve, ("qkv", 2, t))
            await_read(dve, ("qkT", 1, 2))
            for b in range(2):
                dve.tensor_copy(kpT[:, b, :, PAST:], kT[:, :, N_PROMPT:]).then_inc(S["kp_new"], 1)
            for t in range(3):
                await_read(dve, ("cvt", t))
                z = SZ[t]
                link(dve.bn_stats(stat[0:z, t, 0, :], qkv[0:z, t, 0:512]))
                dve.bn_aggr(cvar[0:z, t, :], stat[0:z, t, 0, :]).then_inc(S["cn_var"], 1)

            def conv_norm(t):
                if t == 0:
                    dve.wait_ge(S["cn_std"], 1)
                    link(dve.reciprocal(cstd, cstd))
                    dve.wait_ge(S["clg_in"], 32)
                z = SZ[t]
                c = qkv[0:z, t, 0:512]
                link(dve.scalar_tensor_tensor(c, c, cvar[0:z, t, 0:1], A["clg"][0:z, 0:512], ALU.subtract, ALU.mult))
                dve.scalar_tensor_tensor(c, c, cstd[0:z, t:t + 1], A["clg"][0:z, 512:1024], ALU.mult, ALU.add).then_inc(S["cn_pre"], 1)

            causal = acol("mask")
            smask = acol("smask").rearrange("p (g c) -> p g c", g=4)
            for it in range(9):
                g = it // 2
                if it >= 1:
                    s = it - 1
                    n = (s // 4 + 1) * P
                    await_read(dve, ("S", s, 0))
                    await_read(dve, ("S", s, 1))
                    link(dve.reciprocal(rr, sums[:, s % 2, :]))
                    link(dve.tensor_scalar(rr[:, 1:2], rr[:, 1:2], neglam, None, ALU.mult))
                    if s:
                        await_full(dve, ("wT", s - 1))
                    link(dve.tensor_scalar(wbuf[:, 0:n], ebuf[:, s % 2, 0, 0:n], rr[:, 0:1], None, ALU.mult))
                    dve.scalar_tensor_tensor(wbuf[:, 0:n], ebuf[:, s % 2, 1, 0:n], rr[:, 1:2], wbuf[:, 0:n], ALU.mult, ALU.add).then_inc(S["w_done"], 1)
                if it < 8:
                    i = it // 4
                    n = (i + 1) * P
                    if it % 2 == 0:
                        for k in (1, 3):
                            await_full(dve, ("kpT", g, k))
                            dve.tensor_copy(kpT[:, k // 2, :, P:2 * P], bank(("kpT", g, k)).rearrange("p (h t) -> p h t", h=H)).then_inc(read(("kpT", g, k)), 1)
                    await_full(dve, ("S", it, 0))
                    await_full(dve, ("S", it, 1))
                    diag = ps[:, 0:2, i * P:i * P + P]
                    link(dve.tensor_tensor(diag, diag, causal.unsqueeze(1).broadcast_to([P, 2, P]), ALU.add))
                    link(dve.tensor_reduce(mx, ps[:, 0:2, 0:n], X, ALU.max))
                    dve.tensor_scalar(nb, mx, -DQK ** -0.5, None, ALU.mult).then_inc(S["S_bias"], 1)
                    if it % 2 == 0:
                        if it % 4 == 0:
                            claim(dve, ("AO", it // 4))
                            dve.memset(ps[:, 7, :], 0.0).then_inc(S["ao_zero"], 1)
                        await_full(dve, ("SS", g))
                        sb_ = bank(("SS", g))
                        link(dve.tensor_tensor(sb_[:, PAST:TOK], sb_[:, PAST:TOK], smask[:, g, :], ALU.add))
                        link(dve.tensor_reduce(smx, sb_[:, 0:TOK], X, ALU.max))
                        dve.tensor_scalar(snb, smx, -DQK ** -0.5, None, ALU.mult).then_inc(S["SS_bias"], 1)
                    else:
                        await_read(dve, ("SS", g))
                        link(dve.reciprocal(srl, ssum))
                        link(dve.tensor_tensor(srl, srl, lamrow, ALU.mult))
                        dve.tensor_scalar(es, es, srl, None, ALU.mult).then_inc(S["ps_done"], 1)
                        if it % 4 == 3:
                            k = it // 4
                            await_full(dve, ("AO", k))
                            dve.tensor_copy(ao[:, 4 * k:4 * k + 4, :], bank(("AO", k)).rearrange("p (b e) -> p b e", b=4)).then_inc(read(("AO", k)), 1)
                    if it < 3:
                        conv_norm(it)
                if it in (4, 8):
                    i = it // 4 - 1
                    await_full(dve, ("O", i))
                    if i == 0:
                        dve.wait_ge(S["kv_out"], 64)
                    dve.tensor_copy(qkv[:, i, 512:1024], bank(("O", i))).then_inc(read(("O", i)), 1)
            await_read(dve, ("AO", 1))
            link(dve.tensor_tensor(ao2, ao, ao, ALU.mult))
            dve.tensor_reduce(ss_ao, ao2, X, ALU.add).then_inc(S["ao_read_k"], 1)
            g08 = A["subln"]
            dve.wait_ge(S["att_std"], 2)
            link(dve.reciprocal(rs_att, rs_att))
            link(dve.reciprocal(rs_ao, rs_ao))
            for i in range(2):
                v = qkv[:, i, 512:1024].rearrange("p (h e) -> p h e", h=H)
                link(dve.tensor_tensor(v, v, rs_att[:, 4 * i:4 * i + 4].unsqueeze(2).broadcast_to([P, H, P]), ALU.mult))
                dve.tensor_tensor(v, v, g08.unsqueeze(1).broadcast_to([P, H, P]), ALU.mult).then_inc(S["att_done"], 1)
            link(dve.tensor_tensor(ao, ao, rs_ao.unsqueeze(2).broadcast_to([P, DEC_B, P]), ALU.mult))
            dve.tensor_tensor(ao, ao, g08.unsqueeze(1).broadcast_to([P, DEC_B, P]), ALU.mult).then_inc(S["ao_done"], 1)
            residual(dve, link, ("out0",), 0, A["lngb"])
            experts_dve(dve, link, 0)

            dve.wait_ge(S["tbc_in"], 16)
            cosC, sinC = ccol("cos"), ccol("sin")
            dec = ccol("dec").rearrange("p (h i) -> p h i", h=H)
            sdec = ccol("sdec").rearrange("p (h i) -> p h i", h=H)
            qdec = ccol("qdec").rearrange("p (h i) -> p h i", h=H)

            def gate_out(h):
                for e in range(4):
                    await_full(dve, ("oT", h, e))
                    await_read(dve, ("gg", h, e))
                    b = bank(("oT", h, e))
                    g = gT[:, 4 * h + e, :]
                    dve.tensor_tensor(g[:, 0:N_PROMPT], g[:, 0:N_PROMPT], b[:, 0:N_PROMPT], ALU.mult)
                    gs = g[:, N_PROMPT:].rearrange("p (u i v t) -> p i v u t", u=2, i=2, v=2)
                    bs = b[:, 2 * P:].rearrange("p (i v u r) -> p i v u r", i=2, v=2, u=2)
                    for i in range(2):
                        ins = dve.tensor_tensor(gs[:, i], gs[:, i], bs[:, i, :, :, 0:8], ALU.mult)
                    ins.then_inc(read(("oT", h, e)), 1)

            for h in range(H):
                for i, (dst, s) in enumerate(((qr, 1.0), (kr, 1.0 / 16))):
                    if h or i:
                        dve.wait_ge(S["qk_rot"], 2 * (2 * h + i))
                    for c in range(2):
                        await_full(dve, ("qk", h, i, c))
                        b = bank(("qk", h, i, c))[:, 0:TOK]
                        dve.scalar_tensor_tensor(tmp[:, 2 * c, :], b, s, cosC, ALU.mult, ALU.mult)
                        link(dve.scalar_tensor_tensor(tmp[:, 2 * c + 1, :], b, s, sinC, ALU.mult, ALU.mult))
                        dve.sem_inc(read(("qk", h, i, c)), 1)
                    dve.tensor_tensor(dst[:, 0, :], tmp[:, 0, :], tmp[:, 3, :], ALU.subtract).then_inc(S["qk_rot"], 1)
                    dve.tensor_tensor(dst[:, 1, :], tmp[:, 2, :], tmp[:, 1, :], ALU.add).then_inc(S["qk_rot"], 1)
                dve.wait_ge(S["qk_rot"], 4 * h + 4)
                dve.tensor_tensor(qd, qr[:, :, P:], qdec[:, h, :].unsqueeze(1).broadcast_to([P, 2, TOK - P]), ALU.mult).then_inc(S["g_done"], 1)
                dve.wait_ge(S["v_half"], h + 1)
                dve.tensor_tensor(vh[0:64, 2, :], vh[0:64, 2, :], bank(("v", h, 2))[64:128, :], ALU.add).then_inc(read(("v", h, 2)), 1)
                if h:
                    gate_out(h - 1)
                await_full(dve, ("sc", h))
                b = bank(("sc", h))
                dve.tensor_tensor(sc[:, 0:256].rearrange("p (c i) -> p c i", c=2), b[:, 0:256].rearrange("p (c i) -> p c i", c=2),
                                  dec[:, h, :].unsqueeze(1).broadcast_to([P, 2, P]), ALU.mult)
                dve.tensor_tensor(sc[0:64, 256:320], b[0:64, 256:320], sdec[0:64, h, :], ALU.mult).then_inc(read(("sc", h)), 1)
                for t in (2, 3):
                    claim(dve, ("o", h, t))
                    dve.memset(bank(("o", h, t)), 0.0).then_inc(S["os_zero"], 1)

                def new_states(m):
                    for c in range(2):
                        for j in range(2):
                            job = ("sn", h, m, c, j)
                            await_full(dve, job)
                            st = s0b[:, (h * DEC_B + 2 * m + j) % S0_RING, c, :]
                            dve.scalar_tensor_tensor(st, st, float(np.exp(DEC_T * LOG_G[h])), bank(job), ALU.mult, ALU.add).then_inc(read(job), 1)
                            await_read(dve, job)
                            dve.sem_inc(S["sn_done"], 1)

                new_states(0)
                if h:
                    dve.wait_ge(S["S2_out"], 16 * h)
                for c in range(2):
                    await_full(dve, ("S1", h, c))
                    dve.tensor_copy(St[:, c, :], bank(("S1", h, c))).then_inc(read(("S1", h, c)), 1)
                new_states(1)
                new_states(2)

                def norm_o(lo, hi):
                    for t in range(lo, hi):
                        await_full(dve, ("o", h, t))
                        link(dve.bn_stats(ostat[:, t, :], bank(("o", h, t))))
                        link(dve.bn_aggr(ovar[:, t, :], ostat[:, t, :]))
                    dve.sem_inc(S["on_var"], 1)
                    dve.wait_ge(S["on_std"], 2 * h + 1 + lo // 2)
                    link(dve.reciprocal(ostd[:, lo:hi], ostd[:, lo:hi]))
                    for t in range(lo, hi):
                        dve.tensor_scalar(ob[:, t, :], bank(("o", h, t)), ovar[:, t, 0:1], ostd[:, t:t + 1], ALU.subtract, ALU.mult).then_inc(read(("o", h, t)), 1)

                norm_o(0, 2)
                for c in range(2):
                    await_full(dve, ("S2", h, c))
                    dve.scalar_tensor_tensor(St[:, c, :], St[:, c, :], float(np.exp(P * LOG_G[h])), bank(("S2", h, c)), ALU.mult, ALU.add).then_inc(read(("S2", h, c)), 1)
                    await_read(dve, ("S2", h, c))
                    dve.sem_inc(S["S2_done"], 1)
                new_states(3)
                norm_o(2, 4)
            gate_out(H - 1)
            residual(dve, link, ("out1",), 2, C["lngb"])
            experts_dve(dve, link, 1)

        def experts_pe(pe, l, turn_x):
            Q = L[l]
            claimed = []

            def logits(t):
                for i in range(2):
                    await_read(pe, ("xTm", l, t, i))
                if not claimed:
                    pe.wait_ge(S["tables_in"], 48)
                    claim(pe, ("lgt", l))
                    claimed.append(True)
                for k in range(KD):
                    ins = pe.matmul(bank(("lgt", l))[0:SZ[t], t * 16:t * 16 + 16], xT[:, k, cols_a(t)], wr[:, k, :], start=k == 0, stop=k == KD - 1)
                return ins

            turn_x(("xTm", l), 6 * l, after=lambda t: logits(t - 1) if t else None)
            logits(2).then_inc(full(("lgt", l)), 1)
            pe.wait_ge(S["mask_ready"], l + 1)
            both = rt[:, 8, :, :]
            claim(pe, ("rank", l))
            rb = bank(("rank", l))
            for t in range(3):
                for s in range(t + 1):
                    z = SZ[s]
                    pe.matmul(rb[0:SZ[t], t * 16:t * 16 + 16], (ones if s < t else before)[0:z, 0:SZ[t]], both[0:z, s, :], start=s == 0, stop=s == t)
            for s in range(3):
                ins = pe.matmul(rb[:, 48:64], ones[0:SZ[s], :], both[0:SZ[s], s, :], start=s == 0, stop=s == 2)
            ins.then_inc(full(("rank", l)), 1)
            for b in range(8):
                pe.wait_ge(bank_read[b], turns_before_experts[l][b])

            def experts_of(i):
                code = pe.value_load(experts_i[0:1, bass.ds(i, 1)], min_val=0, max_val=N_EXP ** 3 - 1)
                return [(e & 1, (e >> 1) * 16 + 16) for e in (code & 15, (code >> 4) & 15, (code >> 8) & 15)]

            def by_side(side, products):
                with pe.If(side == 0):
                    products(0)
                with pe.If(side == 1):
                    products(3)

            def turn_rows(i):
                pe.wait_ge(Q["pick_set"], i + 1)
                for k in range(KD):
                    for t in range(3):
                        z = SZ[t]
                        ins = pe.matmul(ps[:, B_TR + k // 4, k % 4 * P:k % 4 * P + P], x[0:z, t, :].rearrange("p (q k) -> p k q", k=KD)[:, k, :],
                                        pick[0:z, 0, t, :], start=t == 0, stop=t == 2)
                ins.then_inc(Q["tr_full"], 1)

            def gate_up(i, hf, expert):
                side, landed = expert
                pe.wait_ge(Q["xa_done"], i + 1)
                pe.wait_ge(Q["xd_done"], i + 1)
                pe.wait_ge(Q[f"hid_done{hf}"], i + 1)

                def products(slot):
                    pe.wait_ge(e_landed[l][slot], landed)
                    pe.wait_ge(e_landed[l][slot + 1], landed)
                    for k in range(KD):
                        for j in range(2):
                            ins = pe.matmul(ps[HALF[hf if j else 1 - hf], B_GU + hf, :], xgT[:, k, HALF[hf]],
                                            ring[:, slot + j, k * D_FF:(k + 1) * D_FF], start=k == 0, stop=k == KD - 1)
                    ins.then_inc(Q["gu_full"], 1)

                by_side(side, products)

            def turn_hidden(i, hf):
                pe.wait_ge(Q[f"hid_done{hf}"], i + 2)
                pe.sem_inc(S["pe_met"], 1)
                for j in range(KF):
                    ins = pe.transpose(ps[:, B_HT + hf, j * CHUNK:(j + 1) * CHUNK], hid[HALF[hf], j * P:j * P + P], ident[HALF[hf], HALF[hf]])
                ins.then_inc(Q["ht_full"], 1)

            def down(i, hf, expert):
                side, landed = expert
                pe.wait_ge(Q["ht_read"], i * 2 + (hf + 1))
                pe.wait_ge(Q[f"ya_done{hf}"], i + 1)
                pe.wait_ge(Q[f"yd_done{hf}"], i + 1)

                def products(slot):
                    pe.wait_ge(e_landed[l][slot + 2], landed)
                    for j in range(KF):
                        for n in range(2):
                            ins = pe.matmul(ps[HALF[1 - hf if n else hf], B_Y + hf, :], hidT[:, hf, j, :],
                                            ring[:, slot + 2, j * D + n * 512:j * D + n * 512 + 512], start=j == 0, stop=j == KF - 1)
                    ins.then_inc(Q["y_full"], 1)

                by_side(side, products)

            pe.sem_inc(Q["gu_full"], 1)
            pe.sem_inc(Q["y_full"], 1)
            turn_rows(0)
            last = last_pair(pe, l)
            gate_up(0, 0, experts_of(0)[0])
            turn_hidden(0, 0)
            with pe.Fori(0, last) as i:
                first, second, third = experts_of(i)
                gate_up(i, 1, second)
                down(i, 0, first)
                turn_rows(i + 1)
                turn_hidden(i, 1)
                gate_up(i + 1, 0, third)
                down(i, 1, second)
                turn_hidden(i + 1, 0)
            first, second, _ = experts_of(last)
            gate_up(last, 1, second)
            down(last, 0, first)
            turn_hidden(last, 1)
            down(last, 1, second)
            if l == 0:
                for hf in range(2):
                    pe.wait_ge(Q[f"ya_done{hf}"], last + 2)
                    pe.wait_ge(Q[f"yd_done{hf}"], last + 2)

        @block.tensor
        def _(pe):
            def turn_x(name, done=None, after=None):
                for t in range(3):
                    if done is not None:
                        pe.wait_ge(S["x_done"], done + t + 1)
                    xv = x[0:SZ[t], t, :].rearrange("p (q k) -> p k q", k=KD)
                    for i in range(2):
                        j = name + (t, i)
                        claim(pe, j)
                        for c in range(4):
                            ins = pe.transpose(bank(j)[:, c * SZ[t]:(c + 1) * SZ[t]], xv[:, 4 * i + c, :], ident[0:SZ[t], 0:SZ[t]])
                        ins.then_inc(full(j), 1)
                    if after:
                        after(t)

            def feature_major(j, w, k0):
                claim(pe, j)
                for k in range(KD):
                    ins = pe.matmul(bank(j)[:, 0:TOK], w[:, k, k0:k0 + P], xT[:, k, :], start=k == 0, stop=k == KD - 1)
                ins.then_inc(full(j), 1)
                return ins

            pe.wait_ge(S["x_in"], 16 * 3)
            turn_x(("xT0",))
            for t in range(3):
                for i in range(2):
                    await_read(pe, ("xT0", t, i))
            for n, name in enumerate(("a", "g")):
                w_arrived(pe, 0, n)
                for c in range(CC):
                    ins = feature_major((name, c), w_block(0, n), c * P)
            pe.wait_ge(S["cw_in"], 16 * 4)
            claim(pe, ("cw",))
            for c in range(CC):
                ins = pe.transpose(bank(("cw",))[:, c * 32:c * 32 + 32], cwin[0:32, c * P:c * P + P], ident[0:32, 0:32])
            ins.then_inc(full(("cw",)), 1)
            for i in range(2):
                claim(pe, ("st", i))
                for c in range(CC):
                    ins = pe.transpose(bank(("st", i))[:, c * 120:c * 120 + 120], stin[0:120, i, c * P:c * P + P], ident[0:120, 0:120])
                ins.then_inc(full(("st", i)), 1)
            def side_by_side(j, lhsT, weights, chunks):
                claim(pe, j)
                for k in range(chunks):
                    for n in range(2):
                        ins = pe.matmul(bank(j)[HALF[n], :], lhsT[:, k, cols_a(2)], weights(n, k), start=k == 0, stop=k == chunks - 1)
                ins.then_inc(full(j), 1)

            def split_sum(j, lhsT, weights, chunks):
                claim(pe, j)
                for k in range(chunks):
                    ins = pe.matmul(bank(j)[HALF[k % 2], :], lhsT[:, k, cols_a(2)], weights(k), start=k < 2, stop=k >= chunks - 2)
                ins.then_inc(full(j), 1)

            for n in range(3):
                w_arrived(pe, 0, 2 + n)
                w = w_block(0, 2 + n)
                for t in range(3 if n == 2 else 2):
                    j = ("qkv", n, t)
                    claim(pe, j)
                    for k in range(KD):
                        ins = pe.matmul(bank(j)[0:SZ[t], :], xT[:, k, cols_a(t)], w[:, k, :], start=k == 0, stop=k == KD - 1)
                    ins.then_inc(full(j), 1)
                if n == 1:
                    side_by_side(("qkv", "qk", 2), xT, lambda n, k: w_block(0, 2 + n)[:, k, :], KD)
            for n in range(2):
                for t in range(3):
                    z = SZ[t]
                    pe.wait_ge(S["rot_step"], t + 1)
                    j = ("qkT", n, t)
                    claim(pe, j)
                    for h in range(H):
                        ins = pe.transpose(bank(j)[:, h * z:h * z + z], qkv[0:z, t, n * 512 + h * P:n * 512 + h * P + P], ident[0:z, 0:z])
                    ins.then_inc(full(j), 1)
            pe.wait_ge(S["u_set"], 2 * CC + 1)
            for i in range(2):
                j = ("uo", i)
                claim(pe, j)
                for c in range(CC):
                    if i == 0:
                        ins = pe.transpose(bank(j)[0:HIST, c * P:c * P + P], up[:, c, N_PROMPT:N_PROMPT + HIST], ident)
                    else:
                        ins = pe.transpose(bank(j)[0:64, c * P:c * P + P], un[:, c, :], ident)
                ins.then_inc(full(j), 1)
            pe.wait_ge(S["conv_done"], 1)
            pe.wait_ge(S["conv_step_s"], 2 * CONV_W)
            for t in range(3):
                j = ("cvt", t)
                claim(pe, j)
                for c in range(CC):
                    ins = pe.transpose(bank(j)[0:SZ[t], c * P:c * P + P], acc[:, c, cols_a(t)], ident)
                ins.then_inc(full(j), 1)
            for t in range(3):
                for n in range(2):
                    await_read(pe, ("qkT", n, t))
            pair = acol("pair")
            for it in range(9):
                g = it // 2
                if it < 8:
                    i, h = it // 4, it % 4
                    n = (i + 1) * P
                    for m in range(2):
                        hp = slice(64 * m, 64 * m + 64)
                        claim(pe, ("S", it, m))
                        pe.matmul(bank(("S", it, m))[:, 0:n], qT[hp, h, cols_a(i)], kT[hp, h, 0:n], start=True, stop=True).then_inc(full(("S", it, m)), 1)
                    if it % 2 == 0:
                        pe.wait_ge(S[f"kp_in{g % 2}"], 64 * (g // 2 + 1))
                        for j4 in range(4):
                            j = ("kpT", g, j4)
                            claim(pe, j)
                            for hh in range(H):
                                ins = pe.transpose(bank(j)[:, hh * P:hh * P + P], kps[g % 2][:, j4 // 2, j4 % 2, hh * P:hh * P + P], ident)
                            ins.then_inc(full(j), 1)
                        for j4 in range(4):
                            await_read(pe, ("kpT", g, j4))
                        pe.wait_ge(S["kp_new"], 2)
                        pe.wait_ge(S["QB_set"], 8 * (g + 1))
                        j = ("SS", g)
                        claim(pe, j)
                        for hh in range(H):
                            for b in range(2):
                                ins = pe.matmul(bank(j)[64 * b:64 * b + 64, 0:TOK], QB[:, b, hh, :], kpT[:, b, hh, :], start=hh == 0, stop=hh == H - 1)
                        ins.then_inc(full(j), 1)
                    else:
                        j = ("wTs", g)
                        pe.wait_ge(S["ps_done"], g + 1)
                        claim(pe, j)
                        for pg in range(2):
                            pe.matmul(bank(j)[:, pg * 64:pg * 64 + 64], es[:, pg * P:pg * P + P], pair, start=True, stop=True)
                        pe.matmul(bank(j)[0:64, 128:192], es[:, PAST:TOK], pair, start=True, stop=True).then_inc(full(j), 1)
                        await_read(pe, j)
                        pe.wait_ge(S[f"vp_in{g % 2}"], 64 * (g // 2 + 1))
                        j = ("AO", it // 4)
                        pe.wait_ge(S["ao_zero"], it // 4 + 1)
                        for b in range(2):
                            col = (2 * g + b) % 4 * P
                            for pg in range(3):
                                for hh in range(H):
                                    c0 = b * 32 + hh * 8
                                    if pg < 2:
                                        w, v = wTs[:, pg, c0:c0 + 8], vps[g % 2][:, b, pg, hh * P:hh * P + P]
                                    else:
                                        w, v = wTs[0:64, 2, c0:c0 + 8], qkv[0:64, 2, 1024 + hh * P:1024 + hh * P + P]
                                    ins = pe.matmul(bank(j)[32 * hh:32 * hh + 8, col:col + P], w, v, start=pg == 0, stop=pg == 2)
                        if it % 4 == 3:
                            ins.then_inc(full(j), 1)
                if it >= 1:
                    s = it - 1
                    i, h = s // 4, s % 4
                    j = ("wT", s)
                    pe.wait_ge(S["w_done"], s + 1)
                    claim(pe, j)
                    for k in range(i + 1):
                        ins = pe.transpose(bank(j)[:, k * P:k * P + P], wbuf[:, k * P:k * P + P], ident)
                    ins.then_inc(full(j), 1)
                    await_read(pe, j)
                    j = ("O", i)
                    if h == 0:
                        claim(pe, j)
                    for k in range(i + 1):
                        ins = pe.matmul(bank(j)[:, h * P:h * P + P], wT[:, k, :], qkv[:, k, 1024 + h * P:1024 + h * P + P], start=k == 0, stop=k == i)
                    if h == 3:
                        ins.then_inc(full(j), 1)
            for i in range(2):
                pe.wait_ge(S["att_done"], i + 1)
                claim(pe, ("att", i))
                for h in range(H):
                    ins = pe.transpose(bank(("att", i))[:, h * P:h * P + P], qkv[:, i, 512 + h * P:512 + h * P + P], ident)
                ins.then_inc(full(("att", i)), 1)
                if i == 0:
                    pe.wait_ge(S["ao_done"], 1)
                claim(pe, ("aoT", i))
                for b in range(4):
                    ins = pe.transpose(bank(("aoT", i))[:, b * P:b * P + P], ao[:, 4 * i + b, :], ident)
                ins.then_inc(full(("aoT", i)), 1)
            pe.wait_ge(S["cn_post"], 3)
            for t in range(3):
                z = SZ[t]
                claim(pe, ("cT", t))
                for c in range(CC):
                    ins = pe.transpose(bank(("cT", t))[:, c * z:c * z + z], qkv[0:z, t, c * P:c * P + P], ident[0:z, 0:z])
                ins.then_inc(full(("cT", t)), 1)
            for i in range(2):
                await_read(pe, ("att", i))
                await_read(pe, ("aoT", i))
            for t in range(3):
                await_read(pe, ("cT", t))
            for n in range(2):
                w_arrived(pe, 0, 5 + n)
                w = w_block(0, 5 + n)
                for t in range(2):
                    j = ("out0", n, t)
                    claim(pe, j)
                    for k in range(KD):
                        ins = pe.matmul(bank(j), mixT[:, k, cols_a(t)], w[:, k, :], start=k == 0, stop=k == KD - 1)
                    ins.then_inc(full(j), 1)
                split_sum(("out0", n, 2), mixT, lambda k: w[:, k, :], KD)
            experts_pe(pe, 0, turn_x)

            turn_x(("xT1",), 3)
            for t in range(3):
                for i in range(2):
                    await_read(pe, ("xT1", t, i))

            def turn_out(h):
                for t in range(4):
                    await_read(pe, ("o", h, t))
                for e in range(4):
                    j = ("oT", h, e)
                    claim(pe, j)
                    for t in range(4):
                        ins = pe.transpose(bank(j)[:, t * P:t * P + P], ob[:, t, e * P:e * P + P], ident)
                    ins.then_inc(full(j), 1)

            for h in range(H):
                w_arrived(pe, 1, 3 * h)
                w = w_block(1, 3 * h)
                for i in range(2):
                    for c in range(2):
                        ins = feature_major(("qk", h, i, c), w, i * DK_C + c * P)
                w_arrived(pe, 1, 3 * h + 1)
                w = w_block(1, 3 * h + 1)

                def values(t):
                    j = ("v", h, t)
                    claim(pe, j)
                    for k in range(KD):
                        ins = pe.matmul(bank(j), xT[:, k, cols_a(t)], w_block(1, 3 * h + 1)[:, k, :], start=k == 0, stop=k == KD - 1)
                    ins.then_inc(full(j), 1)

                def sample_pair(m):
                    for c in range(2):
                        for j in range(2):
                            p = 2 * m + j
                            n = h * DEC_B + p
                            b = SEQ_ORDER[p]
                            if c == 0:
                                pe.wait_ge(s0_in[n % S0_RING], 16 * (n // S0_RING + 1))
                            pe.matmul(bank(("o", h, 2 + p // 4))[32 * (p % 4):32 * (p % 4) + 8, :],
                                      qd[:, c, P + b * 8:P + b * 8 + 8], s0b[:, n % S0_RING, c, :], start=c == 0, stop=False)
                    for j in range(2):
                        p = 2 * m + j
                        b = SEQ_ORDER[p]
                        ins = pe.matmul(bank(("o", h, 2 + p // 4))[32 * (p % 4):32 * (p % 4) + 8, :],
                                        sc[0:64, 256 + b * 8:256 + b * 8 + 8], vh[0:64, 2, :], start=False, stop=True)
                    if m % 2:
                        ins.then_inc(full(("o", h, 2 + m // 2)), 1)
                    for c in range(2):
                        for j in range(2):
                            job = ("sn", h, m, c, j)
                            rows32 = slice(32 * j, 32 * j + 32)
                            claim(pe, job)
                            pe.matmul(bank(job), kdm[rows32, m, c * P:c * P + P], vh[rows32, 2, :], start=True, stop=True).then_inc(full(job), 1)

                split_sum(("v", h, 2), xT, lambda k: w_block(1, 3 * h + 1)[:, k, :], KD)
                values(0)
                if h:
                    turn_out(h - 1)
                pe.wait_ge(S["qk_rot"], 4 * h + 4)
                j = ("sc", h)
                claim(pe, j)
                for t in range(3):
                    for c in range(2):
                        ins = pe.matmul(bank(j)[0:SZ[t], cols_a(t)], kr[:, c, cols_a(t)], qr[:, c, cols_a(t)], start=c == 0, stop=c == 1)
                ins.then_inc(full(j), 1)
                for i in range(2):
                    j = ("kd", h, i)
                    claim(pe, j)
                    for t in ((0, 1), (2,))[i]:
                        for c in range(2):
                            at = (t % 2) * 256 + c * P
                            ins = pe.transpose(bank(j)[0:SZ[t], at:at + P], kr[:, c, cols_a(t)], ident)
                    ins.then_inc(full(j), 1)
                w_arrived(pe, 1, 3 * h + 2)
                w = w_block(1, 3 * h + 2)
                feature_major(("gg", h, 0), w, 0)
                for t in (0, 2):
                    await_read(pe, ("v", h, t))
                await_read(pe, ("sc", h))
                pe.wait_ge(S["g_done"], h + 1)
                pe.wait_ge(S["os_zero"], 2 * (h + 1))
                pe.wait_ge(S["kdm_set"], 4 * (h + 1))
                sample_pair(0)
                await_read(pe, ("kd", h, 0))
                for c in range(2):
                    j = ("S1", h, c)
                    claim(pe, j)
                    pe.matmul(bank(j), kd[:, 0, c * P:c * P + P], vh[:, 0, :], start=True, stop=True).then_inc(full(j), 1)
                j = ("o", h, 0)
                claim(pe, j)
                pe.matmul(bank(j), sc[:, 0:P], vh[:, 0, :], start=True, stop=True).then_inc(full(j), 1)
                values(1)
                sample_pair(1)
                feature_major(("gg", h, 1), w, P)
                sample_pair(2)
                await_read(pe, ("v", h, 1))
                j = ("o", h, 1)
                claim(pe, j)
                pe.matmul(bank(j), sc[:, P:2 * P], vh[:, 1, :], start=True, stop=False)
                for c in range(2):
                    await_read(pe, ("S1", h, c))
                for c in range(2):
                    ins = pe.matmul(bank(j), qd[:, c, 0:P], St[:, c, :], start=False, stop=c == 1)
                ins.then_inc(full(j), 1)
                for c in range(2):
                    j = ("S2", h, c)
                    claim(pe, j)
                    pe.matmul(bank(j), kd[:, 1, c * P:c * P + P], vh[:, 1, :], start=True, stop=True).then_inc(full(j), 1)
                feature_major(("gg", h, 2), w, 2 * P)
                sample_pair(3)
                feature_major(("gg", h, 3), w, 3 * P)
            turn_out(H - 1)
            for e in range(4):
                await_read(pe, ("oT", H - 1, e))
            for n in range(2):
                for r in range(2):
                    w_arrived(pe, 1, 12 + 2 * n + r)
                for t in range(2):
                    j = ("out1", n, t)
                    claim(pe, j)
                    for r in range(2):
                        w = w_block(1, 12 + 2 * n + r)
                        for k in range(KD):
                            ins = pe.matmul(bank(j)[0:SZ[t], :], gT[:, r * KD + k, cols_a(t)], w[:, k, :], start=r + k == 0, stop=r + k == KD)
                    ins.then_inc(full(j), 1)
                split_sum(("out1", n, 2), gT, lambda k: w_block(1, 12 + 2 * n + k // KD)[:, k % KD, :], 2 * KD)
            experts_pe(pe, 1, turn_x)

_INS = ["x_prompt", "x_sample", "cache_k", "cache_v", "page_table", "state_conv", "state_ret", "w_in_a", "lambda_a",
        "subln_a", "conv_w", "conv_b", "conv_ln_g", "conv_ln_b", "w_out_a", "w_in_c", "w_out_c", "ln_g", "ln_b",
        "w_router", "b_router", "w_e_gate", "w_e_up", "w_e_down"]
_OUTS = [("y_prompt", (1, 256, 1024)), ("y_sample", (8, 8, 1024)), ("k_prompt", (1, 1, 256, 8, 64)),
         ("v_prompt", (1, 1, 256, 4, 128)), ("conv_prompt", (1, 1, 30, 512)), ("ret_prompt", (1, 1, 4, 256, 512)),
         ("k_sample", (1, 8, 8, 8, 64)), ("v_sample", (1, 8, 8, 4, 128)), ("conv_sample", (1, 8, 30, 512)),
         ("ret_sample", (1, 8, 4, 256, 512))]


def kernel(**inputs):
    import numpy as _np
    import concourse.bacc as _bacc
    from concourse import mybir as _mybir
    from concourse.bass_utils import run_bass_kernel_spmd as _run

    nc = _bacc.Bacc("TRN2", target_bir_lowering=False, num_devices=1)
    data = {name: _np.ascontiguousarray(inputs[name]) for name in _INS}
    data.update(host_tables())
    arrays, a, o = {}, {}, {}
    for name, v in data.items():
        arrays[f"in_{name}_dram"] = v
        a[name] = nc.dram_tensor(f"in_{name}_dram", v.shape, _mybir.dt.from_np(v.dtype), kind="ExternalInput").ap()
    for name, shape in _OUTS:
        o[name] = nc.dram_tensor(f"out_{name}_dram", shape, _mybir.dt.float32, kind="ExternalOutput").ap()
    build(nc, a, o)
    r = _run(nc, [arrays], core_ids=[0])
    return tuple(r.results[0][f"out_{name}_dram"] for name, _ in _OUTS)
```
